# Optimizing a Trainium2 kernel written in Bass

```python
import jax, jax.numpy as jnp
from jax import lax
import numpy as np

D_MODEL = 1024
BATCH = 1
SEQ = 1024
DEPTH = 1

CONV_WIDTH = D_MODEL
CONV_K = 3
N_Q_HEADS = 16
N_KV_HEADS = 4
HEAD_DIM = 64
ATTN_WIDTH = N_Q_HEADS * HEAD_DIM
KV_WIDTH = N_KV_HEADS * HEAD_DIM
WINDOW = 128
BLOCK = 128
N_BRANCHES = 2
EPS = 1e-6
NEG_INF = -1e30

IN_SIZES = (CONV_WIDTH, CONV_WIDTH, CONV_WIDTH, CONV_WIDTH,
            ATTN_WIDTH, KV_WIDTH, KV_WIDTH, ATTN_WIDTH,
            N_BRANCHES * D_MODEL)
IN_COLS = sum(IN_SIZES)
SPLIT_POINTS = tuple(int(c) for c in np.cumsum(IN_SIZES)[:-1])


def rms_norm(x, g):
    xf = x.astype(jnp.float32)
    y = xf * lax.rsqrt(jnp.mean(xf * xf, axis=-1, keepdims=True) + EPS)
    return (y * g.astype(jnp.float32)).astype(x.dtype)

def causal_depthwise_conv(u, w):
    s = u.shape[1]
    up = jnp.pad(u, ((0, 0), (CONV_K - 1, 0), (0, 0)))
    y = up[:, 0:s] * w[0]
    for k in range(1, CONV_K):
        y = y + up[:, k:k + s] * w[k]
    return y

def sliding_window_attention(q, k, v, sinks):
    b, s = q.shape[0], q.shape[1]
    nb = s // BLOCK
    g = N_Q_HEADS // N_KV_HEADS
    qb = q.reshape(b, nb, BLOCK, N_KV_HEADS, g, HEAD_DIM)

    def band(t):
        tb = t.reshape(b, nb, BLOCK, N_KV_HEADS, HEAD_DIM)
        prev = jnp.pad(tb[:, :-1], ((0, 0), (1, 0), (0, 0), (0, 0), (0, 0)))
        return jnp.concatenate([prev, tb], axis=2)

    kb, vb = band(k), band(v)
    scale = HEAD_DIM ** -0.5
    scores = jnp.einsum('bnqhgd,bnkhd->bnhgqk', qb.astype(jnp.float32),
                        kb.astype(jnp.float32)) * scale
    blk = jnp.arange(nb)[:, None, None]
    q_pos = blk * BLOCK + jnp.arange(BLOCK)[None, :, None]
    k_pos = (blk - 1) * BLOCK + jnp.arange(2 * BLOCK)[None, None, :]
    diff = q_pos - k_pos
    valid = (diff >= 0) & (diff < WINDOW) & (k_pos >= 0)
    scores = jnp.where(valid[None, :, None, None], scores, NEG_INF)
    sink = sinks.astype(jnp.float32).reshape(N_KV_HEADS, g)[None, None, :, :, None, None]
    m = jnp.maximum(jnp.max(scores, axis=-1, keepdims=True), sink)
    p = jnp.exp(scores - m)
    p = p / (jnp.sum(p, axis=-1, keepdims=True) + jnp.exp(sink - m))
    out = jnp.einsum('bnhgqk,bnkhd->bnqhgd', p.astype(v.dtype), vb)
    return out.reshape(b, s, ATTN_WIDTH)

def hybrid_layer(x, norm_g, w_in, conv_w, q_norm_g, k_norm_g, sinks,
                 w_conv_out, w_attn_out, gate_b, w_out):
    b, s, _ = x.shape
    h = rms_norm(x, norm_g)
    u = jnp.einsum('bsd,dc->bsc', h, w_in)
    v_c, b_c, c_c, z_c, q, k, v, z_a, gate_logits = jnp.split(u, SPLIT_POINTS, axis=-1)

    y_c = b_c * causal_depthwise_conv(c_c * v_c, conv_w)
    y_c = y_c * jax.nn.silu(z_c)
    y_a = jnp.einsum('bsc,cd->bsd', y_c, w_conv_out)

    q = rms_norm(q.reshape(b, s, N_Q_HEADS, HEAD_DIM), q_norm_g)
    k = rms_norm(k.reshape(b, s, N_KV_HEADS, HEAD_DIM), k_norm_g)
    v = v.reshape(b, s, N_KV_HEADS, HEAD_DIM)
    o = sliding_window_attention(q, k, v, sinks) * jax.nn.silu(z_a)
    y_b = jnp.einsum('bsc,cd->bsd', o, w_attn_out)

    gates = jax.nn.sigmoid(gate_logits + gate_b)
    g_a, g_b = jnp.split(gates, N_BRANCHES, axis=-1)
    merged = g_a * y_a + g_b * y_b
    return x + jnp.einsum('bsd,de->bse', merged, w_out)

def first_inputs(seed: int = 0) -> dict:
    key = jax.random.key(seed)
    ks = jax.random.split(key, 12)
    f32 = jnp.float32
    x = jax.random.normal(ks[0], (BATCH, SEQ, D_MODEL), f32)
    norm_g = 1.0 + 0.05 * jax.random.normal(ks[1], (DEPTH, D_MODEL), f32)
    w_in = jax.random.normal(ks[2], (DEPTH, D_MODEL, IN_COLS), f32) * D_MODEL ** -0.5
    conv_w = jax.random.normal(ks[3], (DEPTH, CONV_K, CONV_WIDTH), f32) * CONV_K ** -0.5
    q_norm_g = 1.0 + 0.05 * jax.random.normal(ks[4], (DEPTH, HEAD_DIM), f32)
    k_norm_g = 1.0 + 0.05 * jax.random.normal(ks[5], (DEPTH, HEAD_DIM), f32)
    sinks = 0.5 * jax.random.normal(ks[6], (DEPTH, N_Q_HEADS), f32)
    w_conv_out = jax.random.normal(ks[7], (DEPTH, CONV_WIDTH, D_MODEL), f32) * CONV_WIDTH ** -0.5
    w_attn_out = jax.random.normal(ks[8], (DEPTH, ATTN_WIDTH, D_MODEL), f32) * ATTN_WIDTH ** -0.5
    gate_b = 0.02 * jax.random.normal(ks[9], (DEPTH, N_BRANCHES * D_MODEL), f32)
    w_out = jax.random.normal(ks[10], (DEPTH, D_MODEL, D_MODEL), f32) * D_MODEL ** -0.5
    return {"x": x, "norm_g": norm_g, "w_in": w_in, "conv_w": conv_w,
            "q_norm_g": q_norm_g, "k_norm_g": k_norm_g, "sinks": sinks,
            "w_conv_out": w_conv_out, "w_attn_out": w_attn_out,
            "gate_b": gate_b, "w_out": w_out}

def first_block(x, norm_g, w_in, conv_w, q_norm_g, k_norm_g, sinks,
              w_conv_out, w_attn_out, gate_b, w_out):
    for l in range(DEPTH):
        x = hybrid_layer(x, norm_g[l], w_in[l], conv_w[l], q_norm_g[l], k_norm_g[l],
                         sinks[l], w_conv_out[l], w_attn_out[l], gate_b[l], w_out[l])
    return x


N_MEM = 256
MIX_WIDTH = D_MODEL
POOL_WIDTH = MIX_WIDTH // 2
POOL_GROUPS = 4
POOL_GROUP_DIM = POOL_WIDTH // POOL_GROUPS
POOL_WINDOWS = (2, 4, 8, 16)
GLA_VALUE_WIDTH = MIX_WIDTH - POOL_WIDTH
GLA_KEY_WIDTH = GLA_VALUE_WIDTH // 2
GLA_HEADS = 4
GLA_DK = GLA_KEY_WIDTH // GLA_HEADS
GLA_DV = GLA_VALUE_WIDTH // GLA_HEADS
GLA_GATE_RANK = 16
GLA_GATE_NORMALIZER = 16.0
GLA_CHUNK = 64
OFF_Q = POOL_WIDTH
OFF_K = OFF_Q + GLA_KEY_WIDTH
OFF_V = OFF_K + GLA_KEY_WIDTH
OFF_G = OFF_V + GLA_VALUE_WIDTH
OFF_R = OFF_G + GLA_GATE_RANK
IN_PROJ_WIDTH = OFF_R + GLA_VALUE_WIDTH
XATTN_HEADS = 4
XATTN_HEAD_DIM = D_MODEL // XATTN_HEADS
D_FF = 2816
CONV_WIDTH_2 = 3


def rms_norm_2(x, w):
    x32 = x.astype(jnp.float32)
    y = x32 * lax.rsqrt(jnp.mean(x32 * x32, axis=-1, keepdims=True) + EPS)
    return (y * w.astype(jnp.float32)).astype(x.dtype)

def multiscale_pool(p, pool_w, pool_scale):
    b, s, _ = p.shape
    pg = p.reshape(b, s, POOL_GROUPS, POOL_GROUP_DIM)
    cs = jnp.cumsum(pg.astype(jnp.float32), axis=1)
    t = jnp.arange(s)
    pooled = []
    for g, w in enumerate(POOL_WINDOWS):
        c = cs[:, :, g]
        c_prev = jnp.pad(c, ((0, 0), (w, 0), (0, 0)))[:, :s]
        cnt = jnp.minimum(t + 1, w).astype(jnp.float32)[None, :, None]
        pooled.append((c - c_prev) / cnt)
    pooled = jnp.stack(pooled, axis=2).astype(p.dtype) - pg
    mixed = jnp.einsum('bsgc,gcd->bsgd', pooled, pool_w)
    return mixed.reshape(b, s, POOL_WIDTH) * pool_scale

def gla_chunked(q, k, v, log_g):
    b, h, s, dk = q.shape
    dv = v.shape[-1]
    nc = s // GLA_CHUNK
    f32 = jnp.float32
    q = q.astype(f32).reshape(b, h, nc, GLA_CHUNK, dk) * (dk ** -0.5)
    k = k.astype(f32).reshape(b, h, nc, GLA_CHUNK, dk)
    v = v.astype(f32).reshape(b, h, nc, GLA_CHUNK, dv)
    G = jnp.cumsum(log_g.astype(f32).reshape(b, h, nc, GLA_CHUNK, dk), axis=3)
    G_last = G[:, :, :, -1]
    q_dec = q * jnp.exp(G)
    k_dec = k * jnp.exp(-G)
    causal = jnp.tril(jnp.ones((GLA_CHUNK, GLA_CHUNK), dtype=bool))
    scores = jnp.where(causal, jnp.einsum('bhnid,bhnjd->bhnij', q_dec, k_dec), 0.0)
    o_intra = jnp.einsum('bhnij,bhnje->bhnie', scores, v)
    k_to_end = k * jnp.exp(G_last[:, :, :, None] - G)
    chunk_kv = jnp.einsum('bhnjd,bhnje->bhnde', k_to_end, v)
    decay = jnp.exp(G_last)

    def step(state, inp):
        dec, kv = inp
        return state * dec[..., None] + kv, state

    init = jnp.zeros((b, h, dk, dv), f32)
    _, prev_states = lax.scan(step, init, (jnp.moveaxis(decay, 2, 0), jnp.moveaxis(chunk_kv, 2, 0)))
    prev_states = jnp.moveaxis(prev_states, 0, 2)
    o_inter = jnp.einsum('bhnid,bhnde->bhnie', q_dec, prev_states)
    return (o_intra + o_inter).reshape(b, h, s, dv)

def hybrid_mixer(h, w_in, pool_w, pool_scale, gk_w2, gk_b, gla_norm_w, w_out):
    b, s, _ = h.shape
    proj = h @ w_in
    p = proj[..., :OFF_Q]
    q = proj[..., OFF_Q:OFF_K]
    k = proj[..., OFF_K:OFF_V]
    v = proj[..., OFF_V:OFF_G]
    g_low = proj[..., OFF_G:OFF_R]
    r = proj[..., OFF_R:]
    pool_out = multiscale_pool(p, pool_w, pool_scale)
    log_g = jax.nn.log_sigmoid((g_low @ gk_w2 + gk_b).astype(jnp.float32)) / GLA_GATE_NORMALIZER

    def heads(t, d):
        return t.reshape(b, s, GLA_HEADS, d).transpose(0, 2, 1, 3)

    o = gla_chunked(heads(q, GLA_DK), heads(k, GLA_DK), heads(v, GLA_DV), heads(log_g, GLA_DK))
    o = rms_norm_2(o, gla_norm_w).transpose(0, 2, 1, 3).reshape(b, s, GLA_VALUE_WIDTH).astype(h.dtype)
    gla_out = o * jax.nn.silu(r)
    return jnp.concatenate([pool_out, gla_out], axis=-1) @ w_out

def memory_cross_attention(h, mem_n, wq, wkv, wo):
    b, s, _ = h.shape
    m = mem_n.shape[1]
    q = (h @ wq).reshape(b, s, XATTN_HEADS, XATTN_HEAD_DIM)
    kv = mem_n @ wkv
    k = kv[..., :D_MODEL].reshape(b, m, XATTN_HEADS, XATTN_HEAD_DIM)
    v = kv[..., D_MODEL:].reshape(b, m, XATTN_HEADS, XATTN_HEAD_DIM)
    scores = jnp.einsum('bshd,bmhd->bhsm', q, k).astype(jnp.float32) * (XATTN_HEAD_DIM ** -0.5)
    probs = jax.nn.softmax(scores, axis=-1).astype(v.dtype)
    o = jnp.einsum('bhsm,bmhd->bshd', probs, v).reshape(b, s, D_MODEL)
    return o @ wo

def conv_ffn(h, w_up, conv_w, conv_b, w_down):
    s = h.shape[1]
    u = h @ w_up
    u_pad = jnp.pad(u, ((0, 0), (CONV_WIDTH_2 - 1, 0), (0, 0)))
    u = conv_b + conv_w[0] * u_pad[:, 0:s] + conv_w[1] * u_pad[:, 1:1 + s] + conv_w[2] * u_pad[:, 2:2 + s]
    gate = u[..., :D_FF]
    val = u[..., D_FF:]
    return (jax.nn.silu(gate) * val) @ w_down

def second_inputs(seed: int = 0) -> dict:
    key = jax.random.key(seed)
    ks = jax.random.split(key, 24)
    f32 = jnp.float32
    L = DEPTH

    def nrm(k, shape, scale):
        return jax.random.normal(k, shape, f32) * scale

    def gain(k, shape):
        return 1.0 + 0.05 * jax.random.normal(k, shape, f32)

    return {
        'x': jax.random.normal(ks[0], (BATCH, SEQ, D_MODEL), f32),
        'mem': jax.random.normal(ks[1], (BATCH, N_MEM, D_MODEL), f32),
        'norm_mix_w': gain(ks[2], (L, D_MODEL)),
        'w_in': nrm(ks[3], (L, D_MODEL, IN_PROJ_WIDTH), D_MODEL ** -0.5),
        'pool_w': nrm(ks[4], (L, POOL_GROUPS, POOL_GROUP_DIM, POOL_GROUP_DIM), POOL_GROUP_DIM ** -0.5),
        'pool_scale': 0.5 + 0.05 * jax.random.normal(ks[5], (L, POOL_WIDTH), f32),
        'gk_w2': nrm(ks[6], (L, GLA_GATE_RANK, GLA_KEY_WIDTH), GLA_GATE_RANK ** -0.5),
        'gk_b': nrm(ks[7], (L, GLA_KEY_WIDTH), 0.1),
        'gla_norm_w': gain(ks[8], (L, GLA_DV)),
        'w_out': nrm(ks[9], (L, MIX_WIDTH, D_MODEL), MIX_WIDTH ** -0.5),
        'norm_xattn_w': gain(ks[10], (L, D_MODEL)),
        'norm_mem_w': gain(ks[11], (L, D_MODEL)),
        'xattn_wq': nrm(ks[12], (L, D_MODEL, D_MODEL), D_MODEL ** -0.5),
        'xattn_wkv': nrm(ks[13], (L, D_MODEL, 2 * D_MODEL), D_MODEL ** -0.5),
        'xattn_wo': nrm(ks[14], (L, D_MODEL, D_MODEL), D_MODEL ** -0.5),
        'norm_ffn_w': gain(ks[15], (L, D_MODEL)),
        'ffn_w_up': nrm(ks[16], (L, D_MODEL, 2 * D_FF), D_MODEL ** -0.5),
        'ffn_conv_w': nrm(ks[17], (L, CONV_WIDTH_2, 2 * D_FF), CONV_WIDTH_2 ** -0.5),
        'ffn_conv_b': nrm(ks[18], (L, 2 * D_FF), 0.01),
        'ffn_w_down': nrm(ks[19], (L, D_FF, D_MODEL), D_FF ** -0.5),
        'norm_final_w': gain(ks[20], (D_MODEL,)),
    }

def second_block(x, mem, norm_mix_w, w_in, pool_w, pool_scale, gk_w2, gk_b, gla_norm_w, w_out,
              norm_xattn_w, norm_mem_w, xattn_wq, xattn_wkv, xattn_wo,
              norm_ffn_w, ffn_w_up, ffn_conv_w, ffn_conv_b, ffn_w_down, norm_final_w):
    for l in range(DEPTH):
        h = rms_norm_2(x, norm_mix_w[l])
        x = x + hybrid_mixer(h, w_in[l], pool_w[l], pool_scale[l], gk_w2[l], gk_b[l], gla_norm_w[l], w_out[l])
        h = rms_norm_2(x, norm_xattn_w[l])
        m = rms_norm_2(mem, norm_mem_w[l])
        x = x + memory_cross_attention(h, m, xattn_wq[l], xattn_wkv[l], xattn_wo[l])
        h = rms_norm_2(x, norm_ffn_w[l])
        x = x + conv_ffn(h, ffn_w_up[l], ffn_conv_w[l], ffn_conv_b[l], ffn_w_down[l])
    return rms_norm_2(x, norm_final_w)


def setup_inputs(seed=0):
    out = dict(first_inputs(seed))
    for name, value in second_inputs(seed + 1).items():
        if name != "x":
            out[name + "_2"] = value
    return out


def reference(
    x, norm_g, w_in, conv_w, q_norm_g, k_norm_g, sinks, w_conv_out, w_attn_out, gate_b, w_out,
    mem_2, norm_mix_w_2, w_in_2, pool_w_2, pool_scale_2, gk_w2_2, gk_b_2, gla_norm_w_2, w_out_2,
    norm_xattn_w_2, norm_mem_w_2, xattn_wq_2, xattn_wkv_2, xattn_wo_2, norm_ffn_w_2, ffn_w_up_2,
    ffn_conv_w_2, ffn_conv_b_2, ffn_w_down_2, norm_final_w_2,
):
    x = first_block(
        x, norm_g, w_in, conv_w, q_norm_g, k_norm_g, sinks, w_conv_out, w_attn_out, gate_b,
        w_out,
    )
    return second_block(
        x, mem_2, norm_mix_w_2, w_in_2, pool_w_2, pool_scale_2, gk_w2_2, gk_b_2, gla_norm_w_2,
        w_out_2, norm_xattn_w_2, norm_mem_w_2, xattn_wq_2, xattn_wkv_2, xattn_wo_2,
        norm_ffn_w_2, ffn_w_up_2, ffn_conv_w_2, ffn_conv_b_2, ffn_w_down_2, norm_final_w_2,
    )


_drawn_inputs = setup_inputs


def setup_inputs(seed=0):
    import zlib

    import numpy as np

    out = dict(_drawn_inputs(seed))
    spreads = {}
    factors = {'q_norm_g': 8.0,
     'k_norm_g': 8.0,
     'sinks': 25.643,
     'gate_b': 8.0,
     'gk_b_2': 3.309,
     'gla_norm_w_2': 3.01,
     'norm_xattn_w_2': 8.0,
     'norm_mem_w_2': 7.201,
     'ffn_conv_b_2': 46.766,
     'norm_ffn_w_2': 8.0}
    for name, (base, spread) in spreads.items():
        noise = np.random.default_rng([zlib.crc32(name.encode()), seed]).standard_normal(out[name].shape)
        drawn = base * np.exp(spread * noise) if base else spread * noise
        out[name] = __import__('jax').numpy.asarray(drawn.astype(out[name].dtype))
    for name, factor in factors.items():
        out[name] = (out[name] * factor).astype(out[name].dtype)
    return out
```

```python
from contextlib import ExitStack

import concourse.bass as bass
from concourse import mybir

F32 = mybir.dt.float32
F32R = mybir.dt.float32r
U32 = mybir.dt.uint32
ALU = mybir.AluOpType
ACT = mybir.ActivationFunctionType
AX_X = mybir.AxisListType.X

P = 128
D = 1024
S = 1024
KT = D // P
HALF = 512
NB = S // P
EPS = 1e-6
NEG = -1e30

V_C, B_C, C_C, Z_C, Q_C, K_C, V_A, Z_A, G_A, G_B = 0, 8, 16, 24, 32, 40, 42, 44, 52, 60
HEADS, KV, DH = 16, 4, 64
MEM = 256
POOL_WINDOWS = (2, 4, 8, 16)
CHUNK = 64
XHEADS, XD = 4, 256
FF = 2816
FF_TILES = FF // P
FF_GROUPS = (8, 8, 6)

T_KV = 0
T_Q = T_KV + 4
T_CONV = T_Q + 8
T_Z = T_CONV + 32
T_YB = T_Z + 8
T_YA = T_YB + 16
T_WO = T_YA + 16
T_P = T_WO + 8
T_GL = T_P + 4
T_QK = T_GL + 1
T_V = T_QK + 4
T_R = T_V + 4
T_WO2 = T_R + 4
T_XQ = T_WO2 + 8
T_MK = T_XQ + 8
T_MV = T_MK + 8
T_XO = T_MV + 8
T_FF = T_XO + 8
T_END = T_FF + sum(2 * n + 8 for n in FF_GROUPS)

PARAM_ROWS = [("norm_g", 8), ("conv_w", 24), ("gate_b", 16), ("norm_mix_w_2", 8), ("pool_scale_2", 4),
              ("gk_b_2", 2), ("gla_norm_w_2", 1), ("norm_xattn_w_2", 8), ("norm_mem_w_2", 8),
              ("norm_ffn_w_2", 8)]
PCOL, _at = {}, 0
for _name, _n in PARAM_ROWS:
    PCOL[_name] = _at
    _at += _n
ROWS0 = _at
FFW = ROWS0
FFW2 = FFW + 2 * 2 * FF_TILES
PCOLS = FFW2 + 2 * 2 * FF_TILES


class Tally:

    def __init__(self, eng, sem):
        self.eng, self.sem, self.base, self.n, self.i, self.per = eng, sem, 0, 0, None, 0

    def value(self):
        v = self.base + self.n
        return v if self.i is None else self.i * self.per + v

    def add(self, ins):
        self.n += 1
        ins.then_inc(self.sem, 1)

    def link(self, ins):
        self.add(ins)
        self.eng.wait_ge(self.sem, self.value())

    def enter(self, i, per, start=0):
        self.base += self.n - start * per
        self.n, self.i, self.per = 0, i, per

    def leave(self, end):
        assert self.n == self.per, (self.n, self.per)
        self.base += self.per * end
        self.n, self.i = 0, None


def hybrid_then_mixer_kernel(nc, x, norm_g, w_in, conv_w, q_norm_g, k_norm_g, sinks, w_conv_out, w_attn_out,
                             gate_b, w_out, mem_2, norm_mix_w_2, w_in_2, pool_w_2, pool_scale_2, gk_w2_2,
                             gk_b_2, gla_norm_w_2, w_out_2, norm_xattn_w_2, norm_mem_w_2, xattn_wq_2,
                             xattn_wkv_2, xattn_wo_2, norm_ffn_w_2, ffn_w_up_2, ffn_conv_w_2, ffn_conv_b_2,
                             ffn_w_down_2, norm_final_w_2, out):
    ctx = ExitStack()
    with ctx:
        def sem(name):
            return ctx.enter_context(nc.semaphore(name))

        BIG = KT * S * 4
        arena_bytes = nc.sbuf_bytes_remaining // 64 * 64
        arena = ctx.enter_context(nc.sbuf_tensor("arena", [P, arena_bytes // 4], F32))
        base0 = (nc.sbuf_usable_end - nc.sbuf_bytes_remaining - arena_bytes) // 32 * 32 + 32
        end0 = nc.sbuf_usable_end - nc.sbuf_bytes_remaining
        A, B, C, DD, E = (base0 + n * BIG for n in range(5))
        WRING = base0 + 5 * BIG

        def at(name, shape, dtype, offset):
            size = 4
            for n in shape[1:]:
                size *= n
            assert offset + size <= end0, (name, offset + size - end0)
            return nc.alloc_sbuf_tensor_at(name, shape, dtype, offset=offset)

        wbytes = KT * P * 4
        wraw = [at(f"wraw{n}", [P, KT, P], F32, WRING + n * wbytes) for n in range(2)]
        whi = [at(f"whi{n}", [P, KT, P], F32R, WRING + (2 + n) * wbytes) for n in range(2)]
        wlo = [at(f"wlo{n}", [P, KT, P], F32R, WRING + (4 + n) * wbytes) for n in range(2)]
        top = [WRING + 6 * wbytes]

        def keep(name, shape, dtype):
            t = at(name, shape, dtype, top[0])
            size = 4
            for n in shape[1:]:
                size *= n
            top[0] += (size + 31) // 32 * 32
            return t

        R = keep("R", [P, S], F32)
        ident = keep("ident", [P, P], F32)
        ones = keep("ones", [P, P], F32)
        head_ones = keep("head_ones", [P, P], F32)
        mask_rest = keep("mask_rest", [P, 2 * P], F32)
        late = top[0]
        mask_first = keep("mask_first", [P, 2 * P], F32)
        half_sel = keep("half_sel", [P, 2], F32)
        pcol = keep("pcol", [P, PCOLS], F32)
        hgb = keep("hgb", [P, 16], F32)
        sink = keep("sink", [P, HEADS], F32)
        gcols = keep("gcols", [P, 2], F32)
        gkq = keep("gkq", [P, 1], F32)
        eps = keep("eps", [P, 1], F32)
        idle_act = keep("idle_act", [P, 8], F32)
        idle_dve = keep("idle_dve", [P, 8], F32)
        holds = [0]
        rq = keep("rq", [P, NB, 2, 4, 2], F32)
        small = keep("small", [P, 7, 2, 4], F32)
        mx, nm, sd, es, sums, den, rqb = ([small[:, m, n, :] for n in range(2)] for m in range(7))
        cmask = at("chunk_mask", [P, P], F32, late)
        dec = at("dec", [P, 2, S // CHUNK], F32, late + 512)
        stats = at("stats", [P, 8], F32, late + 640)
        rcnt = at("rcnt", [P, 16], F32, late + 672)
        TMP = top[0]

        sq = [at(f"sq{n}", [P, S], F32, TMP + n * 4 * S) for n in range(2)]
        ssum = at("ssum", [P, S], F32, TMP + 8 * S)
        rows = at("rows", [P, 3, P], F32, TMP + 12 * S)
        vraw = at("vraw", [P, 2, S], F32, TMP)
        zraw = at("zraw", [P, S], F32, TMP)
        zth = at("zth", [P, S], F32, TMP + 4 * S)
        zo = at("zo", [P, S], F32, TMP + 8 * S)
        tv = at("tv", [P, S], F32, TMP)
        cv = at("cv", [P, S + 2], F32, TMP + 4 * S)
        zt = at("zt", [P, S], F32, E + 24576)
        th = at("th", [P, S], F32, E + 28672)
        h1, h2, h3 = (at(f"h{n}", [P, HALF], F32, TMP + 8 * S + 32 + 2048 * n) for n in range(3))

        xhi = at("xhi", [P, KT, S], F32R, A)
        xlo = at("xlo", [P, KT, S], F32R, B)
        xraw = at("xraw", [P, NB, D], F32, C)
        xt32 = at("xt32", [P, KT, S], F32, DD)
        q32 = at("q32", [P, 2, 4, S], F32, C)
        sqq = at("sqq", [P, 2, 4, S], F32, E)
        kT32 = at("kT32", [P, 2, P + S], F32, DD)
        v32 = at("v32", [P, NB + 1, 2 * P], F32, DD + 9216)
        rk = at("rk", [P, 2, S], F32, DD + 9216)
        kraw = at("kraw", [P, 2, S], F32, DD + 18432)
        khi = at("khi", [P, 2, 2 * P], F32R, DD + 18432)
        klo = at("klo", [P, 2, 2 * P], F32R, DD + 20480)
        vhi = at("vhi", [P, 2, 2, P], F32R, DD + 22528)
        vlo = at("vlo", [P, 2, 2, P], F32R, DD + 24576)
        qhi = at("qhi", [P, 2, 4 * P], F32R, E)
        qlo = at("qlo", [P, 2, 4 * P], F32R, E + 4096)
        Sx = [at(f"Sx{n}", [P, 4, 2 * P], F32, E + 8192 + 4096 * n) for n in range(2)]
        pthi = at("pthi", [P, 2, 4 * P], F32R, E + 16384)
        ptlo = at("ptlo", [P, 2, 4 * P], F32R, E + 20480)
        ohi = at("ohi", [P, KT, S], F32R, DD)
        olo = at("olo", [P, KT, S], F32R, E)
        yc32 = at("yc32", [P, KT, S], F32, E)
        merged = at("merged", [P, KT, S], F32, C)
        mhi = at("mhi", [P, KT, S], F32R, A)
        mlo = at("mlo", [P, KT, S], F32R, B)
        resid = at("resid", [P, KT, S], F32, DD)
        x2hi = at("x2hi", [P, KT, S], F32R, E)
        x2lo = at("x2lo", [P, KT, S], F32R, C)
        qk32 = at("qk32", [P, 4, S], F32, A)
        gv32 = at("gv32", [P, 4, S], F32, A + BIG // 2)
        r32 = at("r32", [P, 4, S], F32, B)
        pool32 = at("pool32", [P, 4, S], F32, B + BIG // 2)
        pa = at("pool_a", [P, S], F32, TMP)
        pb = at("pool_b", [P, S], F32, TMP + 4 * S)
        pw = at("pool_w", [P, 4, P], F32, TMP + 8 * S)
        gk = at("gk", [P, 2, S], F32, TMP)
        gsum = at("gate_sum", [P, S], F32, TMP + 8 * S)
        ghalf = at("gate_half", [P, HALF], F32, TMP + 12 * S)
        glow = at("gate_low", [16, S], F32, B)
        gkw = at("gk_w2", [16, 2 * P], F32, B + 4 * S)
        c2hi = at("c2hi", [P, KT, S], F32R, C)
        c2lo = at("c2lo", [P, KT, S], F32R, E)
        gvt = [at(f"gvt{n}", [P, 4 * P], F32, E + 2048 * n) for n in range(2)]
        gst = [at(f"gst{n}", [P, 2, 2, P], F32, E + 4096 + 2048 * n) for n in range(2)]
        gss = [at(f"gss{n}", [P, 2, 2, P], F32, E + 8192 + 2048 * n) for n in range(2)]
        gket = [at(f"gket{n}", [P, 2 * P], F32, E + 12288 + 1024 * n) for n in range(2)]
        gosq = at("gosq", [P, 2, 2 * P], F32, TMP + 8 * S)
        go = [at(f"go{n}", [P, 2, 2 * P], F32, TMP + 8 * S + 2048 + 2048 * n) for n in range(2)]
        x3hi = at("x3hi", [P, KT, S], F32R, A)
        x3lo = at("x3lo", [P, KT, S], F32R, B)
        xq32 = at("xq32", [P, KT, S], F32, E)
        mthi = at("mem_hi", [P, KT, MEM], F32R, C)
        mtlo = at("mem_lo", [P, KT, MEM], F32R, C + 8192)
        mraw = at("mem_raw", [P, 2, D], F32, C + 16384)
        mkhi = at("mem_k_hi", [P, KT, MEM], F32R, C + 16384)
        mklo = at("mem_k_lo", [P, KT, MEM], F32R, C + 24576)
        mv32 = at("mem_v", [P, 2, D], F32, TMP)
        mjunk = at("mem_squares", [P, D], F32, TMP + 8192)
        xsx = [at(f"xsx{n}", [P, 2, MEM], F32, TMP + 8192 + 2048 * n) for n in range(2)]
        hqhi = [at(f"hqhi{n}", [P, 2, S], F32R, A + 16384 * n) for n in range(2)]
        hqlo = [at(f"hqlo{n}", [P, 2, S], F32R, A + 16384 * n + 8192) for n in range(2)]
        hvhi = [at(f"hvhi{n}", [P, 2, XD], F32R, C + 4096 * n) for n in range(2)]
        hvlo = [at(f"hvlo{n}", [P, 2, XD], F32R, C + 4096 * n + 2048) for n in range(2)]
        xpthi = [at(f"xpthi{n}", [P, 2, MEM], F32R, C + 8192 + 4096 * n) for n in range(2)]
        xptlo = [at(f"xptlo{n}", [P, 2, MEM], F32R, C + 8192 + 4096 * n + 2048) for n in range(2)]
        xohi = at("xohi", [P, KT, S], F32R, E)
        xolo = at("xolo", [P, KT, S], F32R, B)
        x4hi = at("x4hi", [P, KT, S], F32R, A)
        x4lo = at("x4lo", [P, KT, S], F32R, C)
        ubuf = at("ffn_u", [P, S + 2], F32, TMP)
        yg = at("ffn_gate", [P, S], F32, TMP + 4 * S + 32)
        yv = at("ffn_value", [P, S], F32, TMP + 8 * S + 32)
        fhi = at("fhi", [P, KT, S], F32R, E)
        flo = at("flo", [P, KT, S], F32R, B)
        ot = [at(f"ot{n}", [P, D], F32, A + n * 4 * D) for n in range(2)]
        gfin = at("gfin", [P, D], F32, A + 8 * D)
        ojunk = at("out_squares", [P, D], F32, A + 12 * D)


        def qm(h):
            return h % 2 * 2 + h // 2

        def by_half(a):
            return a.rearrange("p (m q) n -> p q m n", q=2)

        bank = [ctx.enter_context(nc.psum_tensor(f"bank{n}", [P, 2, HALF], F32)) for n in range(4)]

        def ps(n):
            return bank[n // 2][:, n % 2, :]

        s_par = sem("params_loaded")
        s_x = [sem(f"x_loaded{n}") for n in range(2)]
        s_const = sem("consts_built")
        s_w = [sem(f"weights_loaded{n}") for n in range(2)]
        s_whi = sem("weights_hi")
        s_wlo = sem("weights_lo")
        s_acc = sem("acc_ready")
        s_free = sem("acc_free")
        s_pt = sem("params_transposed")
        s_pcol = sem("pcol_ready")
        s_xt = sem("x_transposed")
        s_xc = sem("x_copied")
        s_spill = sem("x_spilled")
        s_back = sem("x_back")
        s_xhi = sem("x_hi")
        s_xlo = sem("x_lo")
        s_sq = sem("squares_ready")
        s_sum = sem("squares_summed")
        s_ms = sem("mean_square")
        s_rs = sem("root")
        s_r = sem("r_ready")
        s_act = sem("act_order")
        s_dve = sem("dve_order")
        s_pool = sem("pool_order")
        s_ksq = sem("k_squares")
        s_kms = sem("k_mean_square")
        s_krs = sem("k_root")
        s_kn = sem("k_normed")
        s_pad = sem("kv_padded")
        s_qsq = sem("q_squares")
        s_qms = sem("q_mean_square")
        s_qrs = sem("q_root")
        s_vt = sem("v_transposed")
        s_v = sem("v_ready")
        s_phi = sem("unit_hi")
        s_plo = sem("unit_lo")
        s_vhi = sem("unit_v_hi")
        s_vlo = sem("unit_v_lo")
        s_s = sem("scores_ready")
        s_sf = sem("scores_read")
        s_neg = sem("neg_max")
        s_exp = sem("exp_done")
        s_p = sem("probs_ready")
        s_t = sem("probs_transposed")
        s_pthi = sem("pt_hi")
        s_ptlo = sem("pt_lo")
        s_o = sem("o_ready")
        s_od = sem("o_copied")
        s_zt = sem("z_tanh")
        s_zof = sem("z_gated")
        s_zhi = sem("z_hi")
        s_zlo = sem("z_lo")
        s_gt = sem("gate_tanh")
        s_ct = sem("conv_tanh")
        s_cof = sem("conv_gated")
        s_conv_stored = sem("conv_stored")
        s_conv_back = [sem(f"conv_back{n}") for n in range(4)]
        s_chi = sem("conv_hi")
        s_clo = sem("conv_lo")
        s_mg = sem("merged_ready")
        s_mhi = sem("merged_hi")
        s_mlo = sem("merged_lo")
        s_ft = sem("out_transposed")
        s_fc = sem("out_copied")
        s_store = [sem(f"out_stored{n}") for n in range(2)]
        s_p_windows = sem("p_windows")
        s_pool_mixed = sem("pool_mixed")
        s_pool_done = sem("pool_done")
        s_late = sem("late_consts_built")
        s_pw_loaded = sem("pool_w_loaded")
        s_gate_z = sem("gate_z")
        s_gl_min = sem("gate_min")
        s_gl_sum = sem("gate_sums")
        s_gk_used = sem("gk_exp_used")
        s_ffn_gate = sem("ffn_gate_conv")
        s_gate_exp = sem("gate_exp")
        s_gate_ln = sem("gate_ln")
        s_gk_exp = sem("gk_exp")
        s_r_tanh = sem("r_tanh")
        s_r_silu = sem("r_silu")
        s_gk_loaded = sem("gk_loaded")
        s_gla_turned = sem("gla_turned")
        s_gla_copied = sem("gla_copied")
        s_gla_scores = sem("gla_scores")
        s_gla_masked = sem("gla_masked")
        s_gla_kv = sem("gla_kv")
        s_gla_state = sem("gla_state")
        s_gla_o = sem("gla_o")
        s_gla_o_copied = sem("gla_o_copied")
        s_gla_o_sum = sem("gla_o_sum")
        s_gla_o_root = sem("gla_o_root")
        s_gla_gated = sem("gla_gated")
        s_gla_hi = sem("gla_hi")
        s_gla_lo = sem("gla_lo")
        s_concat_hi = sem("concat_hi")
        s_concat_lo = sem("concat_lo")
        s_mem_loaded = sem("mem_loaded")
        s_mem_squared = sem("mem_squared")
        s_mem_inverse = sem("mem_inverse")
        s_mem_scaled = sem("mem_scaled")
        s_mem_turned = sem("mem_turned")
        s_mem_hi_ready = sem("mem_hi_ready")
        s_mem_lo_ready = sem("mem_lo_ready")
        s_mem_k_hi_ready = sem("mem_k_hi_ready")
        s_head_hi = sem("head_hi")
        s_head_lo = sem("head_lo")
        s_x_scores = sem("x_scores")
        s_x_max = sem("x_max")
        s_x_exp = sem("x_exp")
        s_x_probs = sem("x_probs")
        s_x_turned = sem("x_turned")
        s_x_pt_hi = sem("x_pt_hi")
        s_x_pt_lo = sem("x_pt_lo")
        s_x_o = sem("x_o")
        s_x_o_hi = sem("x_o_hi")
        s_x_o_lo = sem("x_o_lo")
        s_ffn_tanh = sem("ffn_tanh")
        s_ffn_prod = sem("ffn_prod")
        s_ffn_hi = sem("ffn_hi")
        s_ffn_lo = sem("ffn_lo")
        s_gfin_loaded = sem("gfin_loaded")
        s_out_squared = sem("out_squared")
        s_out_normed = sem("out_normed")

        CONV_BANKS = ((1, 2), (3, 2))
        CONSTS, LATE_CONSTS = 15, 19

        def tiles(w):
            return w.rearrange("(k p) (t n) -> p k t n", p=P, n=P)

        w1 = tiles(w_in[0])
        spill = nc.dram_tensor("x_spill", [P, KT * S], F32).ap()
        spill_v = spill.rearrange("p (k s) -> p k s", k=KT)
        conv_spill = nc.dram_tensor("conv_spill", [P, KT * S], F32).ap().rearrange("p (k s) -> p k s", k=KT)

        block = ctx.enter_context(nc.Block())

        def hold(eng, sem, value):
            eng.wait_ge(sem, value)
            holds[0] = (holds[0] + 1) % 8
            if eng.engine == nc.scalar.engine:
                eng.activation(idle_act[:, holds[0]:holds[0] + 1], eps[:, :], ACT.Copy)
            else:
                eng.tensor_copy(idle_dve[:, holds[0]:holds[0] + 1], eps[:, :])

        @block.sync
        def _(sp):
            def load(t, slot, src):
                if not isinstance(t, int) or t >= 2:
                    sp.wait_ge(s_wlo, t - 1)
                k = src.shape[1]
                sp.dma_start(wraw[slot][:, 0:k, :], src).then_inc(s_w[slot], 16)

            def loads(t0, n, *srcs):
                m = len(srcs)
                with sp.Fori(0, n // m) as i:
                    for j, (w, c, step) in enumerate(srcs):
                        load(m * i + (t0 + j), (t0 + j) % 2, w[:, :, bass.ds(i * step + c, 1), :]
                             .rearrange("p k t n -> p k (t n)"))

            n_par = [0]

            def par(dst, src):
                sp.dma_start(dst, src).then_inc(s_par, 16)
                n_par[0] += 1

            named = dict(norm_g=norm_g, conv_w=conv_w, gate_b=gate_b, norm_mix_w_2=norm_mix_w_2,
                         pool_scale_2=pool_scale_2, gk_b_2=gk_b_2, gla_norm_w_2=gla_norm_w_2,
                         norm_xattn_w_2=norm_xattn_w_2, norm_mem_w_2=norm_mem_w_2, norm_ffn_w_2=norm_ffn_w_2)
            x_v = x[0].rearrange("(b p) d -> p b d", p=P)
            for n in range(2):
                sp.dma_start(xraw[:, 4 * n:4 * n + 4, :], x_v[:, 4 * n:4 * n + 4, :]).then_inc(s_x[n], 16)
            for name, n in PARAM_ROWS:
                src = named[name]
                src = src.rearrange("a b (t n) -> (a b t) n", n=P) if name == "conv_w" \
                    else src.rearrange("a (t n) -> (a t) n", n=P)
                par(rows[PCOL[name]:PCOL[name] + n, 0, :], src)
            fw = ffn_conv_w_2.rearrange("a b (t n) -> (a b t) n", n=P)
            par(rows[0:4 * FF_TILES, 1, :], fw[0:4 * FF_TILES, :])
            par(rows[0:2 * FF_TILES, 2, :], fw[4 * FF_TILES:6 * FF_TILES, :])
            par(rows[2 * FF_TILES:4 * FF_TILES, 2, :], ffn_conv_b_2.rearrange("a (t n) -> (a t) n", n=P))
            for h in range(2):
                par(gcols[64 * h:64 * h + 64, 0:1], q_norm_g.rearrange("a d -> d a"))
                par(gcols[64 * h:64 * h + 64, 1:2], k_norm_g.rearrange("a d -> d a"))
            par(sink[:, :], sinks.broadcast_to([P, HEADS]))
            assert n_par[0] == N_PAR

            for t, c in ((0, K_C), (1, K_C + 1), (2, V_A), (3, V_A + 1)):
                load(t, t % 2, w1[:, :, c, :])
                if t == 1:
                    for f in range(KT):
                        sp.wait_ge(s_xc, 2 * f + 2)
                        sp.dma_start(spill_v[:, f, :], xt32[:, f, :]).then_inc(s_spill, 16)
            loads(T_Q, 8, (w1, Q_C, 2), (w1, Q_C + 1, 2))
            loads(T_CONV, 32, (w1, V_C, 1), (w1, C_C, 1), (w1, B_C, 1), (w1, Z_C, 1))
            loads(T_Z, 8, (w1, Z_A, 2), (w1, Z_A + 1, 2))
            loads(T_YB, 16, (w1, G_B, 1), (tiles(w_attn_out[0]), 0, 1))
            loads(T_YA, 16, (w1, G_A, 1), (tiles(w_conv_out[0]), 0, 1))
            wo = tiles(w_out[0])
            loads(T_WO, 8, (wo, 0, 2), (wo, 1, 2))
            win2 = w_in_2[0]
            w2p = tiles(win2[:, 0:4 * P])
            w2q = tiles(win2[:, 4 * P:8 * P])
            w2v = tiles(win2[:, 8 * P:12 * P])
            w2g = tiles(win2[:, 12 * P:13 * P])
            w2r = tiles(win2[:, 12 * P + 16:16 * P + 16])
            loads(T_P, 4, (w2p, 0, 2), (w2p, 1, 2))
            load(T_GL, T_GL % 2, w2g[:, :, 0, :])
            loads(T_QK, 4, (w2q, 0, 2), (w2q, 1, 2))
            loads(T_V, 4, (w2v, 0, 2), (w2v, 1, 2))
            loads(T_R, 4, (w2r, 0, 2), (w2r, 1, 2))
            for t0, w in ((T_WO2, w_out_2[0]), (T_XQ, xattn_wq_2[0])):
                w = tiles(w)
                loads(t0, 8, (w, 0, 2), (w, 1, 2))
            wkv = tiles(xattn_wkv_2[0])
            loads(T_MK, 16, (wkv, 0, 2), (wkv, 1, 2))
            w = tiles(xattn_wo_2[0])
            loads(T_XO, 8, (w, 0, 2), (w, 1, 2))
            wup = tiles(ffn_w_up_2[0])
            t, c = T_FF, 0
            for n in FF_GROUPS:
                loads(t, 2 * n, (wup, c, 1), (wup, FF_TILES + c, 1))
                t += 2 * n
                w = tiles(ffn_w_down_2[0, c * P:(c + n) * P, :])
                loads(t, 8, (w, 0, 2), (w, 1, 2))
                t, c = t + 8, c + n
            out_v = out[0].rearrange("(b p) d -> p b d", p=P)
            for b in range(NB):
                sp.wait_ge(s_out_normed, b + 1)
                sp.dma_start(out_v[:, b, :], ot[b % 2][:, :]).then_inc(s_store[b % 2], 16)
            for n in range(2):
                sp.wait_ge(s_store[n], 16 * NB // 2)

        @block.gpsimd
        def _(pool):
            built = Tally(pool, s_const)
            built.link(pool.memset(ident[:, :], 0.0))
            built.link(pool.affine_select(out=ident[:, :], in_=ident[:, :], compare_op=ALU.not_equal, fill=1.0,
                                          base=0, pattern=[[-1, P]], channel_multiplier=1))
            built.link(pool.memset(eps[:, :], EPS))
            built.link(pool.memset(ones[:, :], 1.0))
            built.link(pool.memset(head_ones[:, :], 0.0))
            built.link(pool.memset(half_sel[:, :], 0.0))
            for h in range(2):
                built.link(pool.memset(head_ones[64 * h:64 * h + 64, 64 * h:64 * h + 64], 1.0))
                built.link(pool.memset(half_sel[64 * h:64 * h + 64, h:h + 1], 1.0))
            built.link(pool.memset(mask_rest[:, :], 0.0))
            built.link(pool.affine_select(out=mask_rest[:, :], in_=mask_rest[:, :], compare_op=ALU.is_gt, fill=NEG,
                                          base=0, pattern=[[1, 2 * P]], channel_multiplier=-1))
            built.link(pool.affine_select(out=mask_rest[:, :], in_=mask_rest[:, :], compare_op=ALU.is_ge, fill=NEG,
                                          base=P, pattern=[[-1, 2 * P]], channel_multiplier=1))
            built.link(pool.memset(mask_first[:, 0:P], NEG))
            built.link(pool.tensor_copy(mask_first[:, P:2 * P], mask_rest[:, P:2 * P]))
            assert built.n == CONSTS

            def sum_squares(n, f, buf):
                pool.wait_ge(s_sq, f + (8 * n + 1))
                if isinstance(f, int) and f == 0:
                    if n:
                        pool.wait_ge(s_ms, 2 * n)
                    pool.tensor_copy(ssum[:, :], sq[buf][:, :]).then_inc(s_sum, 1)
                else:
                    pool.wait_ge(s_sum, f + 8 * n)
                    pool.tensor_tensor(ssum[:, :], ssum[:, :], sq[buf][:, :], ALU.add).then_inc(s_sum, 1)

            for f in range(KT):
                sum_squares(0, f, f % 2)
            pool.wait_ge(s_kn, 4)
            pool.memset(kT32[:, :, 0:P], 0.0).then_inc(s_pad, 1)
            pool.memset(v32[:, 0, :], 0.0).then_inc(s_pad, 1)
            pool.wait_ge(s_sf, KV)
            late_built = Tally(pool, s_late)
            late_built.link(pool.memset(cmask[:, :], 1.0))
            late_built.link(pool.affine_select(out=cmask[:, :], in_=cmask[:, :], compare_op=ALU.is_ge, fill=0.0,
                                               base=0, pattern=[[1, P]], channel_multiplier=-1))
            late_built.link(pool.memset(cmask[0:CHUNK, CHUNK:P], 0.0))
            for n in range(16):
                late_built.link(pool.memset(rcnt[:, n:n + 1], 1.0 / (n + 1)))
            assert late_built.n == LATE_CONSTS
            with pool.Fori(0, KT) as i:
                pool.wait_ge(s_cof, i + 1)
                pool.dma_start(conv_spill[:, bass.ds(i, 1), :].rearrange("p a n -> p (a n)"), tv[:, :])\
                    .then_inc(s_conv_stored, 16)
            pool.wait_ge(s_conv_stored, 16 * KT)
            pool.wait_ge(s_acc, 2 * T_YA)
            for n in range(4):
                pool.dma_start(yc32[:, 2 * n:2 * n + 2, :], conv_spill[:, 2 * n:2 * n + 2, :])\
                    .then_inc(s_conv_back[n], 16)
            pool.wait_ge(s_acc, 2 * T_WO)
            for n in range(4):
                if n:
                    pool.wait_ge(s_back, 16 * n)
                pool.dma_start(resid[:, 2 * n:2 * n + 2, :], spill_v[:, 2 * n:2 * n + 2, :]).then_inc(s_back, 16)
            for f in range(KT):
                sum_squares(1, f, f % 2)
            pool.wait_ge(s_ms, 4)
            pool.dma_start(pw[:, :, :], pool_w_2[0].rearrange("g c d -> c g d")).then_inc(s_pw_loaded, 16)
            pool.wait_ge(s_acc, 2 * T_P)
            pool.dma_start(gkw[:, :], gk_w2_2[0]).then_inc(s_gk_loaded, 16)
            for f in range(KT):
                sum_squares(2, f, f % 2)
            pool.wait_ge(s_acc, 2 * T_XQ)
            pool.dma_start(mraw[:, :, :], mem_2[0].rearrange("(b p) d -> p b d", p=P)).then_inc(s_mem_loaded, 16)
            for f in range(KT):
                sum_squares(3, f, f % 2)
            pool.wait_ge(s_acc, 2 * (T_END - KT))
            pool.dma_start(gfin[:, :], norm_final_w_2.rearrange("(a d) -> a d", a=1).broadcast_to([P, D]))\
                .then_inc(s_gfin_loaded, 16)

        @block.tensor
        def _(pe):
            def dense(t, slot, hi, lo, k_tiles=KT, ready=None, banks=None):
                pe.wait_ge(s_wlo, t + 1)
                for h in range(2):
                    if banks is not None and h == 1:
                        pe.wait_ge(s_free, 2 * t)
                    elif not isinstance(t, int) or t >= 2:
                        pe.wait_ge(s_free, 2 * t + (h - 3))
                    acc = ps(2 * slot + h if banks is None else banks[slot][h])
                    for k in range(k_tiles):
                        if callable(ready) and h == 0:
                            pe.wait_ge(*ready(k))
                        elif ready is not None and h == 0:
                            pe.wait_ge(ready[0], ready[1] + ready[2] * (k + 1))
                        xh, xl = hi[:, k, h * HALF:(h + 1) * HALF], lo[:, k, h * HALF:(h + 1) * HALF]
                        pe.matmul(acc, whi[slot][:, k, :], xh, start=(k == 0), stop=False)
                        pe.matmul(acc, whi[slot][:, k, :], xl, start=False, stop=False)
                        last = pe.matmul(acc, wlo[slot][:, k, :], xh, start=False, stop=(k == k_tiles - 1))
                    last.then_inc(s_acc, 1)

            def mean_square(n):
                pe.wait_ge(s_sum, 8 * (n + 1))
                for h in range(2):
                    pe.matmul(ps(4 + h), ones[:, :], ssum[:, h * HALF:(h + 1) * HALF], start=True, stop=True)\
                        .then_inc(s_ms, 1)

            pe.wait_ge(s_const, CONSTS)
            pe.wait_ge(s_par, 16 * N_PAR)
            pe.transpose(ps(7)[:, 0:ROWS0], rows[0:ROWS0, 0, :], ident[0:ROWS0, 0:ROWS0])
            for n in range(2):
                m = 4 * FF_TILES
                last = pe.transpose(ps(7)[:, ROWS0 + n * m:ROWS0 + (n + 1) * m], rows[0:m, 1 + n, :],
                                    ident[0:m, 0:m])
            last.then_inc(s_pt, 1)
            for f in range(KT):
                for h in range(2):
                    n = 2 * f + h
                    pe.wait_ge(s_x[h], 16)
                    if n == 3:
                        pe.wait_ge(s_pcol, 1)
                    if n >= 4:
                        pe.wait_ge(s_xc, n - 3)
                    for j in range(4):
                        last = pe.transpose(ps(4 + n % 4)[:, j * P:(j + 1) * P],
                                            xraw[:, 4 * h + j, f * P:(f + 1) * P], ident[:, :])
                    last.then_inc(s_xt, 1)
            pe.wait_ge(s_xc, 16)
            dense(0, 0, xhi, xlo, ready=(s_xlo, 0, 1))
            mean_square(0)
            for t in range(1, 4):
                dense(t, t % 2, xhi, xlo)
            pe.wait_ge(s_ksq, 2)
            pe.wait_ge(s_r, 2)
            for n in range(4):
                pe.matmul(ps(4 + n), head_ones[:, :], rk[:, n // 2, (n % 2) * HALF:(n % 2 + 1) * HALF],
                          start=True, stop=True).then_inc(s_kms, 1)
            with pe.Fori(0, 4) as i:
                for j in range(2):
                    dense(2 * i + (T_Q + j), (T_Q + j) % 2, xhi, xlo)
            pe.wait_ge(s_krs, 4)
            pe.wait_ge(s_free, 2 * T_Q)
            for c in range(4):
                for n in range(4):
                    b, f = 2 * c + n // 2, n % 2
                    last = pe.transpose(ps(4 + c)[:, n * P:(n + 1) * P], vraw[:, f, b * P:(b + 1) * P], ident[:, :])
                last.then_inc(s_vt, 1)
            pe.wait_ge(s_qsq, 8)
            pe.wait_ge(s_free, 2 * T_CONV)
            for b in range(NB):
                for gg in range(2):
                    for hh in range(4):
                        c = ((b * 2 + gg) * 4 + hh) * 2
                        last = pe.matmul(ps(0)[:, c:c + 2], sqq[:, gg, hh, b * P:(b + 1) * P], half_sel[:, :],
                                         start=True, stop=True)
            last.then_inc(s_qms, 1)
            pe.wait_ge(s_v, 4)

            def scores(b, g):
                gg, q = g // 2, 64 * (g % 2)
                pe.wait_ge(s_plo, 2 * b + (gg + 1))
                if not isinstance(b, int) or 4 * b + g > 0:
                    pe.wait_ge(s_sf, 4 * b + g)
                for hh in range(4):
                    o = ps(4 + hh // 2)[:, (hh % 2) * 2 * P:(hh % 2 + 1) * 2 * P]
                    qh, ql = (w[q:q + 64, gg, hh * P:(hh + 1) * P] for w in (qhi, qlo))
                    kh, kl = (w[q:q + 64, gg, :] for w in (khi, klo))
                    pe.matmul(o, qh, kh, start=True, stop=False)
                    pe.matmul(o, qh, kl, start=False, stop=False)
                    last = pe.matmul(o, ql, kh, start=False, stop=True)
                last.then_inc(s_s, 1)

            def turn(u, par, first=False):
                pe.wait_ge(s_p, u + 1)
                if not first:
                    pe.wait_ge(s_ptlo, u)
                for kb in range(2):
                    for hh in range(4):
                        last = pe.transpose(ps(6 + kb)[:, hh * P:(hh + 1) * P],
                                            Sx[par][:, hh, kb * P:(kb + 1) * P], ident[:, :])
                last.then_inc(s_t, 1)

            def weigh(u, b, g, first=False):
                pe.wait_ge(s_vlo, 2 * b + (g // 2 + 1))
                pe.wait_ge(s_ptlo, u + 1)
                if not first:
                    pe.wait_ge(s_od, u)
                for kb in range(2):
                    vh, vl = vhi[:, g // 2, kb, :], vlo[:, g // 2, kb, :]
                    pe.matmul(ps(0), vh, pthi[:, kb, :], start=(kb == 0), stop=False)
                    pe.matmul(ps(0), vh, ptlo[:, kb, :], start=False, stop=False)
                    last = pe.matmul(ps(0), vl, pthi[:, kb, :], start=False, stop=(kb == 1))
                last.then_inc(s_o, 1)

            def attend(b):
                for g in range(KV):
                    u = 4 * b + g
                    if not isinstance(b, int) or g >= 2:
                        turn(u - 2, g % 2, first=isinstance(u, int) and u == 2)
                    if not isinstance(b, int) or g >= 3:
                        weigh(u - 3, b if g == 3 else b - 1, (g - 3) % 4, first=isinstance(u, int) and u == 3)
                    dense(u + T_CONV, g % 2, xhi, xlo, banks=CONV_BANKS)
                    scores(b, g)

            attend(0)
            with pe.Fori(1, NB) as b:
                attend(b)
            last_u = 4 * NB
            turn(last_u - 2, 0)
            weigh(last_u - 3, NB - 1, 1)
            turn(last_u - 1, 1)
            weigh(last_u - 2, NB - 1, 2)
            weigh(last_u - 1, NB - 1, 3)
            pe.wait_ge(s_od, last_u)
            pe.wait_ge(s_free, 2 * T_Z)

            with pe.Fori(0, 4) as i:
                for j in range(2):
                    dense(2 * i + (T_Z + j), (T_Z + j) % 2, xhi, xlo)
            with pe.Fori(0, 8) as i:
                dense(2 * i + T_YB, T_YB % 2, xhi, xlo)
                pe.wait_ge(s_zlo, 9)
                dense(2 * i + (T_YB + 1), (T_YB + 1) % 2, ohi, olo)
            with pe.Fori(0, 8) as i:
                dense(2 * i + T_YA, T_YA % 2, xhi, xlo)
                dense(2 * i + (T_YA + 1), (T_YA + 1) % 2, ohi, olo, ready=(s_clo, 0, 1))
            with pe.Fori(0, 4) as i:
                for j in range(2):
                    dense(2 * i + (T_WO + j), (T_WO + j) % 2, mhi, mlo, ready=(s_mlo, 0, 1))
            dense(T_P, T_P % 2, x2hi, x2lo, ready=(s_xlo, 8, 1))
            mean_square(1)
            for t in range(T_P + 1, T_QK):
                dense(t, t % 2, x2hi, x2lo)
            pe.wait_ge(s_pw_loaded, 16)
            for g in range(4):
                for h in range(2):
                    n = 2 * g + h
                    pe.wait_ge(s_p_windows, g + 1)
                    if n == 0:
                        pe.wait_ge(s_r, 4)
                    if n >= 4:
                        pe.wait_ge(s_pool_done, n - 3)
                    pe.matmul(ps(4 + n % 4), pw[:, g, :], pool32[:, g, h * HALF:(h + 1) * HALF],
                              start=True, stop=True).then_inc(s_pool_mixed, 1)
            dense(T_QK, T_QK % 2, x2hi, x2lo)
            pe.wait_ge(s_gk_loaded, 16)
            pe.wait_ge(s_free, 2 * (T_GL + 1))
            pe.wait_ge(s_pool_done, 8)
            for m in range(2):
                for h in range(2):
                    last = pe.matmul(ps(4 + 2 * m + h), gkw[:, m * P:(m + 1) * P],
                                     glow[:, h * HALF:(h + 1) * HALF], start=True, stop=True)
            last.then_inc(s_gate_z, 1)
            dense(T_QK + 1, (T_QK + 1) % 2, x2hi, x2lo)
            with pe.Fori(0, (T_WO2 - T_QK - 2) // 2) as i:
                for j in range(2):
                    dense(2 * i + (T_QK + 2 + j), (T_QK + j) % 2, x2hi, x2lo)

            def gla_turn(b):
                blk = slice(b * P, (b + 1) * P)
                pe.wait_ge(s_gla_masked, b + 1 if b == 0 else b)
                if b:
                    pe.wait_ge(s_gla_copied, b)
                for h in range(4):
                    pe.transpose(ps(4)[:, h * P:(h + 1) * P], gv32[:, h, blk], ident[:, :])
                for m in range(2):
                    last = pe.transpose(ps(6)[:, (2 + m) * P:(3 + m) * P], gk[:, m, blk], ident[:, :])
                last.then_inc(s_gla_turned, 1)

            def gla_scores(b):
                blk = slice(b * P, (b + 1) * P)
                if b:
                    pe.wait_ge(s_gla_copied, b + 1)
                for h in range(4):
                    q, m = 64 * (h % 2), h // 2
                    last = pe.matmul(bank[3][:, h % 2, m * P:(m + 1) * P], qk32[q:q + 64, 2 + m, blk], qk32[q:q + 64, m, blk],
                                     start=True, stop=True)
                last.then_inc(s_gla_scores, 1)

            def gla_kv(b):
                pe.wait_ge(s_gla_copied, b + 1)
                if b:
                    pe.wait_ge(s_gla_state, b)
                for c in range(2):
                    for h in range(4):
                        q, m = 64 * (h % 2), h // 2
                        rows_c = slice(c * CHUNK, (c + 1) * CHUNK)
                        last = pe.matmul(bank[1][q:q + 64, c, m * P:(m + 1) * P],
                                         gket[b % 2][rows_c, h * 64:(h + 1) * 64],
                                         gvt[b % 2][rows_c, h * P:(h + 1) * P], start=True, stop=True)
                last.then_inc(s_gla_kv, 1)

            def gla_out(b):
                pe.wait_ge(s_gla_masked, b + 1)
                pe.wait_ge(s_gla_state, b + 1)
                if b:
                    pe.wait_ge(s_gla_o_copied, b)
                for h in range(4):
                    q, m = 64 * (h % 2), h // 2
                    pe.matmul(bank[0][:, h % 2, m * P:(m + 1) * P], gvt[b % 2][:, h * P:(h + 1) * P],
                              gst[b % 2][:, h % 2, m, :], start=True, stop=False, skip_group_check=True)
                    for c in range(2):
                        lo = m * P + c * CHUNK
                        tok = b * P + c * CHUNK
                        last = pe.matmul(bank[0][:, h % 2, lo:lo + CHUNK], gss[b % 2][q:q + 64, c, m, :],
                                         qk32[q:q + 64, m, tok:tok + CHUNK], start=False, stop=(c == 1),
                                         skip_group_check=True)
                last.then_inc(s_gla_o, 1)

            def gla_sum(b):
                pe.wait_ge(s_gla_o_copied, b + 1)
                if b:
                    pe.wait_ge(s_gla_gated, b)
                pe.matmul(ps(5), ones[:, :], gosq[:, :, :].rearrange("p q n -> p (q n)"), start=True, stop=True)\
                    .then_inc(s_gla_o_sum, 1)

            pe.wait_ge(s_free, 2 * T_WO2)
            pe.wait_ge(s_gk_used, 8)
            pe.wait_ge(s_r_silu, 8)
            gla_scores(0)
            gla_turn(0)
            gla_kv(0)
            for b in range(NB):
                if b + 1 < NB:
                    gla_turn(b + 1)
                gla_out(b)
                if b + 1 < NB:
                    gla_scores(b + 1)
                    gla_kv(b + 1)
                gla_sum(b)
            pe.wait_ge(s_gla_o_copied, NB)
            with pe.Fori(0, 4) as i:
                for j in range(2):
                    dense(2 * i + (T_WO2 + j), (T_WO2 + j) % 2, c2hi, c2lo,
                          ready=lambda k: (s_concat_lo, k + 1) if k < 4 else (s_gla_lo, NB))

            dense(T_XQ, T_XQ % 2, x3hi, x3lo, ready=(s_xlo, 16, 1))
            mean_square(2)
            dense(T_XQ + 1, (T_XQ + 1) % 2, x3hi, x3lo)
            pe.wait_ge(s_mem_scaled, 2)
            pe.wait_ge(s_r, 6)
            for c in range(4):
                for n in range(4):
                    f, a = 2 * c + n // 2, n % 2
                    last = pe.transpose(ps(4 + c)[:, n * P:(n + 1) * P], mraw[:, a, f * P:(f + 1) * P], ident[:, :])
                last.then_inc(s_mem_turned, 1)
            with pe.Fori(0, 3) as i:
                for j in range(2):
                    dense(2 * i + (T_XQ + 2 + j), (T_XQ + j) % 2, x3hi, x3lo)
            pe.wait_ge(s_mem_lo_ready, 4)
            with pe.Fori(0, 4) as i:
                for j in range(2):
                    t, slot = 2 * i + (T_MK + j), (T_MK + j) % 2
                    pe.wait_ge(s_wlo, t + 1)
                    pe.wait_ge(s_free, 2 * t - 2)
                    acc = ps(2 * slot)[:, 0:MEM]
                    for k in range(KT):
                        pe.matmul(acc, whi[slot][:, k, :], mthi[:, k, :], start=(k == 0), stop=False)
                        pe.matmul(acc, whi[slot][:, k, :], mtlo[:, k, :], start=False, stop=False)
                        last = pe.matmul(acc, wlo[slot][:, k, :], mthi[:, k, :], start=False, stop=(k == KT - 1))
                    last.then_inc(s_acc, 2)
            with pe.Fori(0, 4) as i:
                for j in range(2):
                    t, slot = 2 * i + (T_MV + j), (T_MV + j) % 2
                    pe.wait_ge(s_wlo, t + 1)
                    pe.wait_ge(s_free, 2 * t - 2)
                    for a in range(2):
                        acc = ps(2 * slot)[:, a * P:(a + 1) * P]
                        blk = slice(a * P, (a + 1) * P)
                        for k in range(KT):
                            pe.matmul(acc, mthi[:, k, blk], whi[slot][:, k, :], start=(k == 0), stop=False)
                            pe.matmul(acc, mtlo[:, k, blk], whi[slot][:, k, :], start=False, stop=False)
                            last = pe.matmul(acc, mthi[:, k, blk], wlo[slot][:, k, :], start=False,
                                             stop=(k == KT - 1))
                    last.then_inc(s_acc, 2)

            def x_scores(h, par, j):
                u = 4 * h + j
                pe.wait_ge(s_head_lo, h + 1)
                if not isinstance(u, int) or u >= 2:
                    pe.wait_ge(s_x_exp, u - 1)
                for a in range(2):
                    blk = slice((2 * j + a) * P, (2 * j + a + 1) * P)
                    o = ps(4 + j % 2)[:, a * MEM:(a + 1) * MEM]
                    for k in range(2):
                        if isinstance(h, int):
                            kh, kl = mkhi[:, 2 * h + k, :], mklo[:, 2 * h + k, :]
                        else:
                            kh, kl = (w[:, bass.ds(2 * h + k, 1), :].rearrange("p a n -> p (a n)")
                                      for w in (mkhi, mklo))
                        pe.matmul(o, hqhi[par][:, k, blk], kh, start=(k == 0), stop=False)
                        pe.matmul(o, hqhi[par][:, k, blk], kl, start=False, stop=False)
                        last = pe.matmul(o, hqlo[par][:, k, blk], kh, start=False, stop=(k == 1))
                last.then_inc(s_x_scores, 1)

            def x_turn(u, j):
                pe.wait_ge(s_x_probs, u + 1)
                if not isinstance(u, int) or u >= 2:
                    pe.wait_ge(s_x_pt_lo, u - 1)
                for kb in range(2):
                    for a in range(2):
                        last = pe.transpose(ps(6 + j % 2)[:, (2 * kb + a) * P:(2 * kb + a + 1) * P],
                                            xsx[j % 2][:, a, kb * P:(kb + 1) * P], ident[:, :])
                last.then_inc(s_x_turned, 1)

            def x_weigh(u, par, j):
                pe.wait_ge(s_x_pt_lo, u + 1)
                if not isinstance(u, int) or u >= 2:
                    pe.wait_ge(s_x_o_lo, u - 1)
                for e in range(2):
                    o = ps(j % 2)[:, e * MEM:(e + 1) * MEM]
                    for kb in range(2):
                        vh, vl = (w[par][:, kb, e * P:(e + 1) * P] for w in (hvhi, hvlo))
                        pe.matmul(o, vh, xpthi[j % 2][:, kb, :], start=(kb == 0), stop=False)
                        pe.matmul(o, vh, xptlo[j % 2][:, kb, :], start=False, stop=False)
                        last = pe.matmul(o, vl, xpthi[j % 2][:, kb, :], start=False, stop=(kb == 1))
                last.then_inc(s_x_o, 1)

            pe.wait_ge(s_free, 2 * T_XO)

            def x_head(h, par):
                for j in range(4):
                    u = 4 * h + j
                    x_scores(h, par, j)
                    if not isinstance(h, int) or u >= 2:
                        x_turn(u - 2, j)
                    if not isinstance(h, int) or u >= 3:
                        x_weigh(u - 3, par if j == 3 else 1 - par, (j - 3) % 4)

            x_head(0, 0)
            x_head(1, 1)
            x_head(2, 0)
            x_head(3, 1)
            last_u = 4 * XHEADS
            x_turn(last_u - 2, 0)
            x_weigh(last_u - 3, 1, 1)
            x_turn(last_u - 1, 1)
            x_weigh(last_u - 2, 1, 2)
            x_weigh(last_u - 1, 1, 3)
            pe.wait_ge(s_x_o_lo, last_u)
            with pe.Fori(0, 4) as i:
                for j in range(2):
                    dense(2 * i + (T_XO + j), (T_XO + j) % 2, xohi, xolo)

            t, done = T_FF, 0
            for n in FF_GROUPS:
                if t == T_FF:
                    dense(t, t % 2, x4hi, x4lo, ready=(s_xlo, 24, 1))
                    mean_square(3)
                    dense(t + 1, (t + 1) % 2, x4hi, x4lo)
                first = 1 if t == T_FF else 0
                with pe.Fori(first, n) as i:
                    for j in range(2):
                        dense(2 * i + (t + j), (t + j) % 2, x4hi, x4lo)
                t += 2 * n
                done += n
                with pe.Fori(0, 4) as i:
                    for j in range(2):
                        dense(2 * i + (t + j), (t + j) % 2, fhi, flo, k_tiles=n,
                              ready=(s_ffn_lo, 2 * (done - n), 2))
                t += 8
            for b in range(NB):
                for c in range(2):
                    n = 2 * b + c
                    pe.wait_ge(s_free, 2 * T_END)
                    if n >= 4:
                        pe.wait_ge(s_fc, n - 3)
                    for j in range(4):
                        last = pe.transpose(ps(4 + n % 4)[:, j * P:(j + 1) * P],
                                            resid[:, 4 * c + j, b * P:(b + 1) * P], ident[:, :])
                    last.then_inc(s_ft, 1)

        @block.scalar
        def _(act):
            order = Tally(act, s_act)

            def split(t, slot):
                if isinstance(t, int):
                    act.wait_ge(s_w[slot], 16 * (t // 2 + 1))
                else:
                    raise AssertionError("use split_at")
                if t >= 2:
                    act.wait_ge(s_acc, 2 * (t - 1))
                act.activation(whi[slot][:, :, :], wraw[slot][:, :, :], ACT.Copy).then_inc(s_whi, 1)

            def split_at(i, m, t0):
                slot = t0 % 2
                act.wait_ge(s_w[slot], i * (8 * m) + 16 * (t0 // 2 + 1))
                act.wait_ge(s_acc, i * (2 * m) + 2 * (t0 - 1))
                act.activation(whi[slot][:, :, :], wraw[slot][:, :, :], ACT.Copy).then_inc(s_whi, 1)

            def prepare(n, f, buf, src, hi, g):
                act.activation(hi[:, f, :], src[:, f, :], ACT.Copy, scale=pcol[:, g:g + 1]
                               if isinstance(g, int) else pcol[:, bass.ds(g, 1)]).then_inc(s_xhi, 1)
                if not (n == 0 and isinstance(f, int) and f < 2):
                    act.wait_ge(s_sum, f + (8 * n - 1))
                act.activation(sq[buf][:, :], src[:, f, :], ACT.Square).then_inc(s_sq, 1)

            def root(n):
                for h in range(2):
                    act.wait_ge(s_ms, 2 * n + h + 1)
                    act.activation(ps(4 + h), ps(4 + h), ACT.Sqrt, bias=eps[:, 0:1], scale=1.0 / D)\
                        .then_inc(s_rs, 1)

            act.wait_ge(s_pt, 1)
            act.activation(pcol[:, :], ps(7)[:, 0:PCOLS], ACT.Copy).then_inc(s_pcol, 1)
            act.wait_ge(s_pcol, 1)
            for f in range(KT):
                for h in range(2):
                    n = 2 * f + h
                    act.wait_ge(s_xt, n + 1)
                    act.activation(xt32[:, f, h * HALF:(h + 1) * HALF], ps(4 + n % 4), ACT.Copy).then_inc(s_xc, 1)
                act.wait_ge(s_xc, 2 * f + 2)
                prepare(0, f, f % 2, xt32, xhi, PCOL["norm_g"] + f)
                if f == 5:
                    split(0, 0)
            split(1, 1)
            root(0)
            for t in range(4):
                if t:
                    split(t + 1, (t + 1) % 2)
                if t < 2:
                    act.wait_ge(s_free, 2 * t + 2)
                    act.activation(rk[:, t, :], kraw[:, t, :], ACT.Square).then_inc(s_ksq, 1)
            for n in range(4):
                act.wait_ge(s_kms, n + 1)
                act.activation(rk[:, n // 2, (n % 2) * HALF:(n % 2 + 1) * HALF], ps(4 + n), ACT.Sqrt,
                               bias=eps[:, 0:1], scale=1.0 / DH).then_inc(s_krs, 1)
            with act.Fori(0, 2) as i:
                for jj in range(4):
                    split_at(i, 4, T_Q + jj + 1)
                    q, j = 64 * (jj // 2), jj % 2
                    hold(act, s_free, i * 8 + 2 * (T_Q + jj + 1))
                    act.activation(sqq[q:q + 64, bass.ds(i, 1), 2 * j:2 * j + 2, :],
                                   q32[q:q + 64, bass.ds(i, 1), 2 * j:2 * j + 2, :], ACT.Square).then_inc(s_qsq, 1)
            act.wait_ge(s_pad, 2)
            for c in range(4):
                act.wait_ge(s_vt, c + 1)
                act.activation(v32[:, 1 + 2 * c:3 + 2 * c, :], ps(4 + c).rearrange("p (b n) -> p b n", b=2), ACT.Copy)\
                    .then_inc(s_v, 1)
            act.wait_ge(s_v, 4)
            act.wait_ge(s_qms, 1)
            act.activation(rq[:, :, :, :, :].rearrange("p b g h s -> p (b g h s)"), ps(0)[:, 0:P], ACT.Sqrt,
                           bias=eps[:, 0:1], scale=1.0 / DH).then_inc(s_qrs, 1)

            def unit_hi(b, gg):
                if not isinstance(b, int):
                    hold(act, s_s, 4 * b + (2 * gg - 2))
                cur = slice(0, P) if isinstance(b, int) else bass.ds(b * P, P)
                keys = slice(0, 2 * P) if isinstance(b, int) else bass.ds(b * P, 2 * P)
                act.activation(qhi[:, gg, :].rearrange("p (h n) -> p h n", h=4), q32[:, gg, :, cur], ACT.Copy)
                act.activation(khi[:, gg, :], kT32[:, gg, keys], ACT.Copy).then_inc(s_phi, 1)

            def values_hi(b, gg):
                blocks = slice(0, 2) if isinstance(b, int) else bass.ds(b, 2)
                if not isinstance(b, int):
                    hold(act, s_o, 4 * b + (2 * gg - 2))
                act.activation(vhi[:, gg, :, :], v32[:, blocks, gg * P:(gg + 1) * P], ACT.Copy).then_inc(s_vhi, 1)

            def exps(u, par):
                act.wait_ge(s_neg, u + 1)
                for hh in range(4):
                    act.activation(Sx[par][:, hh, :], Sx[par][:, hh, :], ACT.Exp, bias=nm[par][:, hh:hh + 1],
                                   accum_out=sums[par][:, hh:hh + 1])
                act.activation(es[par][:, :], sd[par][:, :], ACT.Exp).then_inc(s_exp, 1)

            def turned_hi(u):
                act.wait_ge(s_t, u + 1)
                if not isinstance(u, int) or u > 0:
                    act.wait_ge(s_o, u)
                act.activation(pthi[:, :, :], bank[3][:, :, :], ACT.Copy).then_inc(s_pthi, 1)

            def keep_o(u, b, g):
                q = 64 * (g % 2)
                cur = slice(b * P, (b + 1) * P) if isinstance(b, int) else bass.ds(b * P, P)
                act.activation(q32[q:q + 64, g // 2, :, cur],
                               ps(0)[q:q + 64, :].rearrange("p (h n) -> p h n", h=4), ACT.Copy).then_inc(s_od, 1)

            def attend(b):
                for g in range(KV):
                    u = 4 * b + g
                    if isinstance(b, int):
                        split(T_CONV + g + 1, (T_CONV + g + 1) % 2)
                    else:
                        split_at(b, 4, T_CONV + g + 1)
                    if g % 2 == 0:
                        unit_hi(b, g // 2)
                    else:
                        values_hi(b, g // 2)
                    if not isinstance(b, int) or g >= 2:
                        turned_hi(u - 2)
                    if not isinstance(b, int) or g >= 3:
                        keep_o(u - 3, b if g == 3 else b - 1, (g - 3) % 4)
                    exps(u, g % 2)
                    if g == 3:
                        act.wait_ge(s_free, 8 * b + (2 * T_CONV + 8))
                        act.activation(th[:, :], zt[:, :], ACT.Tanh, scale=0.5).then_inc(s_ct, 1)

            attend(0)
            with act.Fori(1, NB) as b:
                attend(b)
            last_u = 4 * NB
            turned_hi(last_u - 2)
            keep_o(last_u - 3, NB - 1, 1)
            turned_hi(last_u - 1)
            keep_o(last_u - 2, NB - 1, 2)
            act.wait_ge(s_o, last_u)
            keep_o(last_u - 1, NB - 1, 3)
            act.wait_ge(s_od, last_u)

            split(T_Z + 1, (T_Z + 1) % 2)
            act.wait_ge(s_conv_stored, 16 * KT)
            with act.Fori(0, 2) as i:
                for jj in range(4):
                    q, j = 64 * (jj // 2), jj % 2
                    split_at(i, 4, T_Z + jj + 2)
                    hold(act, s_zlo, i * 4 + (jj + 1))
                    for s in range(2):
                        last = act.activation(zo[64 * s:64 * s + 64, :],
                                              q32[q:q + 64, bass.ds(i, 1), 2 * j + s, :]
                                              .rearrange("p a n -> p (a n)"), ACT.Copy)
                    act.wait_ge(s_free, i * 8 + (2 * T_Z + 2 * jj + 2))
                    act.activation(zth[:, :], zraw[:, :], ACT.Tanh, scale=0.5).then_inc(s_zt, 1)
                    hold(act, s_zof, i * 4 + (jj + 1))
                    act.activation(ohi[:, bass.ds(i * 4 + jj, 1), :].rearrange("p a n -> p (a n)"), zo[:, :],
                                   ACT.Copy).then_inc(s_zhi, 1)

            def gates(i, t0, g0, n0):
                for h in range(2):
                    hold(act, s_free, i * 4 + (2 * t0 + h + 1))
                    act.activation(tv[:, h * HALF:(h + 1) * HALF], tv[:, h * HALF:(h + 1) * HALF], ACT.Tanh,
                                   scale=0.5, bias=hgb[:, bass.ds(i + g0, 1)]).then_inc(s_gt, 1)

            with act.Fori(0, 8) as i:
                split_at(i, 2, T_YB + 2)
                gates(i, T_YB, 8, 0)
                split_at(i, 2, T_YB + 3)
            for f in range(KT):
                act.wait_ge(s_conv_back[f // 2], 16)
                act.activation(ohi[:, f, :], yc32[:, f, :], ACT.Copy).then_inc(s_chi, 1)
            split(T_YA + 2, T_YA % 2)
            gates(0, T_YA, 0, 16)
            split(T_YA + 3, (T_YA + 3) % 2)
            with act.Fori(1, 8) as i:
                split_at(i, 2, T_YA + 2)
                gates(i, T_YA, 0, 16)
                split_at(i, 2, T_YA + 3)
            for f in range(KT):
                act.wait_ge(s_mg, 2 * f + 2)
                act.activation(mhi[:, f, :], merged[:, f, :], ACT.Copy).then_inc(s_mhi, 1)

            def residual(n, t0, hi, g):
                with act.Fori(0, 4) as i:
                    for j in range(2):
                        split_at(i, 2, t0 + j + 2)
                        act.wait_ge(s_free, i * 4 + (2 * t0 + 2 * j + 2))
                        f = 2 * i + j
                        act.activation(hi[:, bass.ds(f, 1), :], resid[:, bass.ds(f, 1), :], ACT.Copy,
                                       scale=pcol[:, bass.ds(f + g, 1)]).then_inc(s_xhi, 1)
                        hold(act, s_sum, f + (8 * n - 1))
                        act.activation(sq[j][:, :].rearrange("p (a n) -> p a n", a=1), resid[:, bass.ds(f, 1), :],
                                       ACT.Square).then_inc(s_sq, 1)

            residual(1, T_WO, x2hi, PCOL["norm_mix_w_2"])
            root(1)
            for n in range(T_P, T_QK + 1):
                split(n + 2, n % 2)

            def log_gates(m):
                for h in range(2):
                    n = 2 * m + h
                    act.wait_ge(s_gl_min, n + 1)
                    act.activation(ghalf[:, :], ghalf[:, :], ACT.Exp).then_inc(s_gate_exp, 1)
                    act.wait_ge(s_gate_exp, n + 1)
                    act.activation(ghalf[:, :], ghalf[:, :], ACT.Ln, bias=ones[:, 0:1]).then_inc(s_gate_ln, 1)

            def gate_exps(m):
                act.wait_ge(s_gl_sum, m + 1)
                last = gsum[:, :].rearrange("p (c n) -> p c n", n=CHUNK)[:, :, CHUNK - 1:CHUNK]\
                    .rearrange("p c n -> p (c n)")
                act.activation(dec[:, m, :], last, ACT.Exp, scale=1.0 / 16)
                for h in range(2):
                    half = slice(h * HALF, (h + 1) * HALF)
                    n = 4 * m + 2 * h
                    if n:
                        act.wait_ge(s_gk_used, n)
                    act.activation(ghalf[:, :], gsum[:, half], ACT.Exp, scale=1.0 / 16).then_inc(s_gk_exp, 1)
                    act.wait_ge(s_gk_used, n + 1)
                    act.activation(ghalf[:, :], gsum[:, half], ACT.Exp, scale=-1.0 / 16)
                    act.activation(gk[:, m, half], gk[:, m, half], ACT.Exp, scale=1.0 / 16).then_inc(s_gk_exp, 1)

            for n in range(T_QK + 1, T_WO2):
                split(n + 2, n % 2)
                if n == T_QK + 2:
                    log_gates(0)
                if n == T_V:
                    gate_exps(0)
                if n == T_V + 1:
                    log_gates(1)
                if n == T_V + 3:
                    gate_exps(1)
                if n >= T_R:
                    for h in range(2):
                        act.wait_ge(s_free, 2 * n + h + 1)
                        if n > T_R:
                            act.wait_ge(s_r_silu, 2 * (n - T_R) + h - 1)
                        act.activation(ps(4 + h), r32[:, qm(n - T_R), h * HALF:(h + 1) * HALF], ACT.Tanh, scale=0.5)\
                            .then_inc(s_r_tanh, 1)

            def gla_copy(b):
                act.wait_ge(s_gla_turned, b + 1)
                if b >= 2:
                    act.wait_ge(s_gla_o, b - 1)
                act.activation(gvt[b % 2][:, :], ps(4), ACT.Copy)
                act.activation(gket[b % 2][:, :], ps(6)[:, 2 * P:4 * P], ACT.Copy).then_inc(s_gla_copied, 1)

            def gla_keep(b):
                act.wait_ge(s_gla_o, b + 1)
                if b:
                    act.wait_ge(s_gla_o_sum, b)
                act.activation(gosq[:, :, :], bank[0][:, :, 0:2 * P], ACT.Square)
                if b >= 2:
                    act.wait_ge(s_gla_lo, b - 1)
                act.activation(go[b % 2][:, :, :], bank[0][:, :, 0:2 * P], ACT.Copy).then_inc(s_gla_o_copied, 1)

            def gla_root(b):
                act.wait_ge(s_gla_o_sum, b + 1)
                act.activation(ps(5), ps(5), ACT.Sqrt, bias=eps[:, 0:1],
                               scale=1.0 / P).then_inc(s_gla_o_root, 1)

            def gla_hi(b):
                act.wait_ge(s_gla_gated, b + 1)
                act.activation(by_half(c2hi[:, 4:8, b * P:(b + 1) * P]),
                               go[b % 2][:, :, :].rearrange("p q (m n) -> p q m n", m=2), ACT.Copy).then_inc(s_gla_hi, 1)

            gla_copy(0)
            for b in range(NB):
                if b + 1 < NB:
                    gla_copy(b + 1)
                gla_keep(b)
                gla_root(b)
                if b:
                    gla_hi(b - 1)
                if 1 <= b < 5:
                    act.activation(c2hi[:, b - 1, :], pool32[:, b - 1, :], ACT.Copy).then_inc(s_concat_hi, 1)
            gla_hi(NB - 1)
            residual(2, T_WO2, x3hi, PCOL["norm_xattn_w_2"])

            root(2)
            act.wait_ge(s_mem_loaded, 16)
            act.wait_ge(s_ms, 6)
            for a in range(2):
                act.activation(mjunk[:, :], mraw[:, a, :], ACT.Square, accum_out=stats[:, a:a + 1])\
                    .then_inc(s_mem_squared, 1)
                act.wait_ge(s_mem_squared, a + 1)
            act.activation(stats[:, 2:4], stats[:, 0:2], ACT.Sqrt, bias=eps[:, 0:1], scale=1.0 / D)\
                .then_inc(s_mem_squared, 1)
            act.wait_ge(s_mem_inverse, 1)
            for a in range(2):
                act.activation(mraw[:, a, :], mraw[:, a, :], ACT.Copy, scale=stats[:, 4 + a:5 + a])\
                    .then_inc(s_mem_scaled, 1)
            split(T_XQ + 2, T_XQ % 2)
            split(T_XQ + 3, (T_XQ + 1) % 2)
            for c in range(4):
                act.wait_ge(s_mem_turned, c + 1)
                for f in range(2 * c, 2 * c + 2):
                    last = act.activation(mthi[:, f, :], ps(4 + c)[:, (f % 2) * MEM:(f % 2 + 1) * MEM], ACT.Copy,
                                          scale=pcol[:, PCOL["norm_mem_w_2"] + f:PCOL["norm_mem_w_2"] + f + 1])
                last.then_inc(s_mem_hi_ready, 1)
            with act.Fori(0, 2) as i:
                for j in range(2):
                    split_at(i, 2, T_XQ + 4 + j)
            for t in range(T_XQ + 8, T_XQ + 9):
                split(t, t % 2)
            for t in range(T_MK, T_MV):
                split(t + 1, (t + 1) % 2)
                act.wait_ge(s_acc, 2 * t + 2)
                act.activation(mkhi[:, t - T_MK, :], ps(2 * (t % 2))[:, 0:MEM], ACT.Copy)\
                    .then_inc(s_mem_k_hi_ready, 1)
            for t in range(T_MV, T_XO + 1):
                split(t + 1, (t + 1) % 2)

            def head_hi(h, par):
                if h >= 2:
                    act.wait_ge(s_x_scores, 4 * h - 4)
                act.activation(hqhi[par][:, :, :], xq32[:, 2 * h:2 * h + 2, :], ACT.Copy)
                if h >= 2:
                    act.wait_ge(s_x_o, 4 * h - 4)
                act.activation(hvhi[par][:, :, :], mv32[:, :, h * XD:(h + 1) * XD], ACT.Copy).then_inc(s_head_hi, 1)

            def x_exps(u, j):
                act.wait_ge(s_x_max, u + 1)
                if u >= 2:
                    act.wait_ge(s_x_turned, u - 1)
                for a in range(2):
                    last = act.activation(xsx[j % 2][:, a, :], ps(4 + j % 2)[:, a * MEM:(a + 1) * MEM], ACT.Exp,
                                          bias=nm[j % 2][:, a:a + 1], scale=float(XD) ** -0.5,
                                          accum_out=sums[j % 2][:, a:a + 1])
                last.then_inc(s_x_exp, 1)

            def x_turned_hi(u, j):
                act.wait_ge(s_x_turned, u + 1)
                if u >= 2:
                    act.wait_ge(s_x_o, u - 1)
                act.activation(xpthi[j % 2][:, :, :], ps(6 + j % 2).rearrange("p (a n) -> p a n", a=2), ACT.Copy)\
                    .then_inc(s_x_pt_hi, 1)

            def x_out_hi(u, h, j):
                act.wait_ge(s_x_o, u + 1)
                act.activation(xohi[:, 2 * h:2 * h + 2, 2 * j * P:2 * (j + 1) * P],
                               ps(j % 2).rearrange("p (a n) -> p a n", a=2), ACT.Copy).then_inc(s_x_o_hi, 1)

            act.wait_ge(s_free, 2 * T_XO)
            head_hi(0, 0)
            for u in range(4 * XHEADS):
                h, j = u // 4, u % 4
                if j == 1 and h == 0:
                    head_hi(1, 1)
                x_exps(u, j)
                if u >= 2:
                    x_turned_hi(u - 2, j)
                if u >= 3:
                    x_out_hi(u - 3, (u - 3) // 4, (u - 3) % 4)
                if j == 2 and 1 <= h < 3:
                    head_hi(h + 1, (h + 1) % 2)
            u = 4 * XHEADS
            x_turned_hi(u - 2, 0)
            x_out_hi(u - 3, 3, 1)
            x_turned_hi(u - 1, 1)
            x_out_hi(u - 2, 3, 2)
            x_out_hi(u - 1, 3, 3)
            residual(3, T_XO, x4hi, PCOL["norm_ffn_w_2"])

            root(3)
            t, done = T_FF, 0
            for n in FF_GROUPS:
                with act.Fori(0, n) as i:
                    for j in range(2):
                        split_at(i, 2, t + j + 2)
                        for h in range(2):
                            if j == 0:
                                act.wait_ge(s_ffn_gate, i + (done + 1))
                                act.activation(ps(4 + h), yg[:, h * HALF:(h + 1) * HALF], ACT.Tanh, scale=0.5)\
                                    .then_inc(s_ffn_tanh, 1)
                            else:
                                hold(act, s_ffn_prod, i * 2 + (2 * done + h + 1))
                                act.activation(fhi[:, bass.ds(i, 1), h * HALF:(h + 1) * HALF]
                                               .rearrange("p a n -> p (a n)"), yv[:, h * HALF:(h + 1) * HALF],
                                               ACT.Copy).then_inc(s_ffn_hi, 1)
                t += 2 * n
                done += n
                with act.Fori(0, 4 if done < FF_TILES else 3) as i:
                    for j in range(2):
                        split_at(i, 2, t + j + 2)
                t += 8
            act.wait_ge(s_gfin_loaded, 16)
            for b in range(NB):
                if b >= 2:
                    act.wait_ge(s_store[b % 2], 16 * (b // 2))
                for c in range(2):
                    n = 2 * b + c
                    act.wait_ge(s_ft, n + 1)
                    act.activation(ot[b % 2][:, c * HALF:(c + 1) * HALF], ps(4 + n % 4), ACT.Copy).then_inc(s_fc, 1)
                act.wait_ge(s_fc, 2 * b + 2)
                act.activation(ojunk[:, :], ot[b % 2][:, :], ACT.Square, accum_out=stats[:, b % 2:b % 2 + 1])\
                    .then_inc(s_out_squared, 1)
                act.wait_ge(s_out_squared, 2 * b + 1)
                act.activation(stats[:, 2 + b % 2:3 + b % 2], stats[:, b % 2:b % 2 + 1], ACT.Sqrt, bias=eps[:, 0:1],
                               scale=1.0 / D).then_inc(s_out_squared, 1)

        @block.vector
        def _(dve):
            order = Tally(dve, s_dve)

            def split(t, slot):
                dve.wait_ge(s_whi, t + 1)
                dve.tensor_tensor(wlo[slot][:, :, :], wraw[slot][:, :, :], whi[slot][:, :, :].bitcast(F32),
                                  ALU.subtract).then_inc(s_wlo, 1)

            def evac(t, h, slot, dst, parts=(0, P), bank_at=None):
                dve.wait_ge(s_acc, 2 * t + (h + 1))
                lo, hi = parts
                acc = ps(2 * slot + h if bank_at is None else bank_at)
                ins = dve.tensor_tensor(dst, acc[lo:hi, :], R[lo:hi, h * HALF:(h + 1) * HALF], ALU.mult)
                return ins

            def lower(n, f, src, hi, lo, g):
                dve.wait_ge(s_xhi, f + (8 * n + 1))
                fs = slice(f, f + 1) if isinstance(f, int) else bass.ds(f, 1)
                gs = slice(g, g + 1) if isinstance(g, int) else bass.ds(g, 1)
                dve.scalar_tensor_tensor(out=lo[:, fs, :], in0=src[:, fs, :], scalar=pcol[:, gs],
                                         in1=hi[:, fs, :].bitcast(F32), op0=ALU.mult, op1=ALU.subtract)\
                    .then_inc(s_xlo, 1)

            def inverse(n):
                for h in range(2):
                    dve.wait_ge(s_rs, 2 * n + h + 1)
                    dve.reciprocal(R[:, h * HALF:(h + 1) * HALF], ps(4 + h)).then_inc(s_r, 1)
                dve.wait_ge(s_r, 2 * n + 2)

            dve.wait_ge(s_par, 16 * N_PAR)
            dve.tensor_tensor(gkq[:, :], gcols[:, 0:1], gcols[:, 1:2], ALU.mult)
            dve.wait_ge(s_pcol, 1)
            order.link(dve.tensor_scalar(hgb[:, :], pcol[:, PCOL["gate_b"]:PCOL["gate_b"] + 16], 0.5, None, ALU.mult))
            for f in range(KT):
                lower(0, f, xt32, xhi, xlo, PCOL["norm_g"] + f)
                if f == 5:
                    split(0, 0)
            split(1, 1)
            inverse(0)
            dve.wait_ge(s_spill, 16 * KT)
            dve.wait_ge(s_sq, 8)
            for t in range(4):
                if t:
                    split(t + 1, (t + 1) % 2)
                for h in range(2):
                    dst = (kraw if t < 2 else vraw)[:, t % 2, h * HALF:(h + 1) * HALF]
                    evac(t, h, t % 2, dst).then_inc(s_free, 1)
            dve.wait_ge(s_krs, 4)
            with dve.Fori(0, 2) as i:
                order.enter(i, 2)
                for jj in range(4):
                    t, slot = i * 4 + (T_Q + jj), (T_Q + jj) % 2
                    split(t + 1, 1 - slot)
                    if jj % 2 == 0:
                        h = slice(jj // 2 * HALF, (jj // 2 + 1) * HALF)
                        hp = slice(P + jj // 2 * HALF, P + (jj // 2 + 1) * HALF)
                        order.link(dve.reciprocal(rk[:, bass.ds(i, 1), h], rk[:, bass.ds(i, 1), h]))
                        dve.scalar_tensor_tensor(out=kT32[:, bass.ds(i, 1), hp], in0=kraw[:, bass.ds(i, 1), h],
                                                 scalar=gkq[:, 0:1], in1=rk[:, bass.ds(i, 1), h], op0=ALU.mult,
                                                 op1=ALU.mult).then_inc(s_kn, 1)
                    q, j = 64 * (jj // 2), jj % 2
                    for h in range(2):
                        for s in range(2):
                            dst = q32[q:q + 64, bass.ds(i, 1), 2 * j + s, h * HALF:(h + 1) * HALF]\
                                .rearrange("p a n -> p (a n)")
                            ins = evac(t, h, slot, dst, (64 * s, 64 * s + 64))
                        ins.then_inc(s_free, 1)
                order.leave(2)
            dve.wait_ge(s_qrs, 1)
            rq_flat = rq[:, :, :, :, :].rearrange("p b g h s -> p (b g h s)")
            order.link(dve.reciprocal(rq_flat, rq_flat))
            order.link(dve.tensor_scalar(rq_flat, rq_flat, float(DH) ** -0.5, None, ALU.mult))

            def unit_lo(b, gg):
                cur = slice(0, P) if isinstance(b, int) else bass.ds(b * P, P)
                keys = slice(0, 2 * P) if isinstance(b, int) else bass.ds(b * P, 2 * P)
                dve.wait_ge(s_phi, 2 * b + (gg + 1))
                dve.tensor_tensor(qlo[:, gg, :].rearrange("p (h n) -> p h n", h=4), q32[:, gg, :, cur],
                                  qhi[:, gg, :].bitcast(F32).rearrange("p (h n) -> p h n", h=4), ALU.subtract)
                dve.tensor_tensor(klo[:, gg, :], kT32[:, gg, keys], khi[:, gg, :].bitcast(F32), ALU.subtract)\
                    .then_inc(s_plo, 1)

            def values_lo(b, gg):
                blocks = slice(0, 2) if isinstance(b, int) else bass.ds(b, 2)
                dve.wait_ge(s_vhi, 2 * b + (gg + 1))
                dve.tensor_tensor(vlo[:, gg, :, :], v32[:, blocks, gg * P:(gg + 1) * P],
                                  vhi[:, gg, :, :].bitcast(F32), ALU.subtract).then_inc(s_vlo, 1)

            def maxima(b, g, par):
                u = 4 * b + g
                if not isinstance(b, int) or g >= 2:
                    dve.wait_ge(s_t, u - 1)
                hold(dve, s_s, u + 1)
                mask = mask_first if isinstance(b, int) else mask_rest
                for hh in range(4):
                    h = 4 * g + hh
                    last = dve.tensor_tensor_reduce(
                        Sx[par][:, hh, :], ps(4 + hh // 2)[:, (hh % 2) * 2 * P:(hh % 2 + 1) * 2 * P], mask[:, :],
                        rqb[par][:, hh:hh + 1], sink[:, h:h + 1], ALU.add, ALU.max, mx[par][:, hh:hh + 1])
                last.then_inc(s_sf, 1)
                dve.wait_ge(s_sf, u + 1)
                dve.tensor_scalar(nm[par][:, :], mx[par][:, :], -1.0, None, ALU.mult)
                dve.tensor_tensor(sd[par][:, :], sink[:, 4 * g:4 * g + 4], mx[par][:, :], ALU.subtract)\
                    .then_inc(s_neg, 1)

            def load_rq(b, g, par):
                bs = slice(0, 1) if isinstance(b, int) else bass.ds(b, 1)
                order.add(dve.tensor_copy(rqb[par][:, :], rq[:, bs, g // 2, :, g % 2]
                                          .rearrange("p a h -> p (a h)")))
                dve.wait_ge(order.sem, order.value())

            def normalise(u, par):
                dve.wait_ge(s_exp, u + 1)
                order.link(dve.tensor_tensor(den[par][:, :], sums[par][:, :], es[par][:, :], ALU.add))
                order.link(dve.reciprocal(den[par][:, :], den[par][:, :]))
                for hh in range(4):
                    last = dve.tensor_scalar(Sx[par][:, hh, :], Sx[par][:, hh, :], den[par][:, hh:hh + 1], None,
                                             ALU.mult)
                last.then_inc(s_p, 1)

            def turned_lo(u):
                dve.wait_ge(s_pthi, u + 1)
                dve.tensor_tensor(ptlo[:, :, :], bank[3][:, :, :], pthi[:, :, :].bitcast(F32), ALU.subtract)\
                    .then_inc(s_ptlo, 1)

            CW = PCOL["conv_w"]
            hs = [slice(h * HALF, (h + 1) * HALF) for h in range(2)]

            def conv_part(b, g):
                t = 4 * b + (T_CONV + g)
                if g == 0 and not isinstance(b, int):
                    dve.wait_ge(s_conv_stored, b * 16)
                dst = (tv, zt, zt, zt)[g]
                for h in range(2):
                    evac(t, h, 0, dst[:, hs[h]], bank_at=CONV_BANKS[g % 2][h]).then_inc(s_free, 1)
                dve.wait_ge(s_free, 8 * b + (2 * (T_CONV + g) + 2))
                if g == 1:
                    order.link(dve.tensor_tensor(cv[:, 2:2 + S], zt[:, :], tv[:, :], ALU.mult))
                    tap = [pcol[:, (slice(CW + 8 * n, CW + 8 * n + 1) if isinstance(b, int)
                                    else bass.ds(b + (CW + 8 * n), 1))] for n in range(3)]
                    order.link(dve.tensor_scalar(tv[:, :], cv[:, 0:S], tap[0], None, ALU.mult))
                    for n in (1, 2):
                        order.link(dve.scalar_tensor_tensor(out=tv[:, :], in0=cv[:, n:n + S], scalar=tap[n],
                                                            in1=tv[:, :], op0=ALU.mult, op1=ALU.add))
                if g == 2:
                    order.link(dve.tensor_tensor(tv[:, :], zt[:, :], tv[:, :], ALU.mult))
                if g == 3:
                    dve.wait_ge(s_ct, b + 1)
                    order.link(dve.scalar_tensor_tensor(out=zt[:, :], in0=th[:, :], scalar=1.0, in1=zt[:, :],
                                                        op0=ALU.add, op1=ALU.mult))
                    dve.scalar_tensor_tensor(out=tv[:, :], in0=zt[:, :], scalar=0.5, in1=tv[:, :],
                                             op0=ALU.mult, op1=ALU.mult).then_inc(s_cof, 1)
                    dve.wait_ge(s_cof, b + 1)

            def attend(b):
                for g in range(KV):
                    u = 4 * b + g
                    split(u + (T_CONV + 1), (g + 1) % 2)
                    if g % 2 == 0:
                        unit_lo(b, g // 2)
                    else:
                        values_lo(b, g // 2)
                    if not isinstance(b, int) or g >= 1:
                        normalise(u - 1, (g - 1) % 2)
                    if not isinstance(b, int) or g >= 2:
                        turned_lo(u - 2)
                    load_rq(b, g, g % 2)
                    maxima(b, g, g % 2)
                    conv_part(b, g)

            dve.wait_ge(s_vt, 4)
            dve.memset(cv[:, 0:2], 0.0).then_inc(s_zlo, 1)
            dve.wait_ge(s_zlo, 1)
            attend(0)
            with dve.Fori(1, NB) as b:
                order.enter(b, 18, 1)
                attend(b)
                order.leave(NB)
            last_u = 4 * NB
            normalise(last_u - 1, 1)
            turned_lo(last_u - 2)
            turned_lo(last_u - 1)

            split(T_Z + 1, (T_Z + 1) % 2)
            dve.wait_ge(s_conv_stored, 16 * KT)
            with dve.Fori(0, 2) as i:
                order.enter(i, 4)
                for jj in range(4):
                    t, slot = i * 4 + (T_Z + jj), (T_Z + jj) % 2
                    for h in range(2):
                        evac(t, h, slot, zraw[:, h * HALF:(h + 1) * HALF]).then_inc(s_free, 1)
                    split(t + 2, slot)
                    dve.wait_ge(s_zt, i * 4 + (jj + 1))
                    dve.wait_ge(s_free, i * 8 + (2 * T_Z + 2 * jj + 2))
                    order.link(dve.scalar_tensor_tensor(out=zth[:, :], in0=zth[:, :], scalar=1.0, in1=zraw[:, :],
                                                        op0=ALU.add, op1=ALU.mult))
                    dve.scalar_tensor_tensor(out=zo[:, :], in0=zth[:, :], scalar=0.5, in1=zo[:, :],
                                             op0=ALU.mult, op1=ALU.mult).then_inc(s_zof, 1)
                    dve.wait_ge(s_zhi, i * 4 + (jj + 1))
                    fs = bass.ds(i * 4 + jj, 1)
                    dve.tensor_tensor(olo[:, fs, :].rearrange("p a n -> p (a n)"), zo[:, :],
                                      ohi[:, fs, :].rearrange("p a n -> p (a n)").bitcast(F32),
                                      ALU.subtract).then_inc(s_zlo, 1)
                order.leave(2)

            def branch(t0, n0, last):
                def tile(i):
                    for h in range(2):
                        evac(2 * i + t0, h, t0 % 2, tv[:, h * HALF:(h + 1) * HALF]).then_inc(s_free, 1)
                    if last and isinstance(i, int):
                        for f in range(KT):
                            dve.wait_ge(s_chi, f + 1)
                            dve.tensor_tensor(olo[:, f, :], yc32[:, f, :], ohi[:, f, :].bitcast(F32),
                                              ALU.subtract).then_inc(s_clo, 1)
                    split(2 * i + (t0 + 2), t0 % 2)
                    for h in range(2):
                        dve.wait_ge(s_gt, i * 2 + (n0 + h + 1))
                        dve.wait_ge(s_acc, i * 4 + (2 * t0 + 2 + h + 1))
                        dve.scalar_tensor_tensor(out=h1[:, :], in0=tv[:, h * HALF:(h + 1) * HALF], scalar=1.0,
                                                 in1=ps(2 * ((t0 + 1) % 2) + h), op0=ALU.add, op1=ALU.mult)\
                            .then_inc(s_free, 1)
                        dve.wait_ge(s_free, i * 4 + (2 * t0 + 2 + h + 1))
                        m = merged[:, bass.ds(i, 1), h * HALF:(h + 1) * HALF].rearrange("p a n -> p (a n)")
                        if last:
                            dve.scalar_tensor_tensor(out=m, in0=h1[:, :], scalar=0.5, in1=m, op0=ALU.mult,
                                                     op1=ALU.add).then_inc(s_mg, 1)
                            dve.wait_ge(s_mg, i * 2 + (h + 1))
                        else:
                            order.link(dve.tensor_scalar(m, h1[:, :], 0.5, None, ALU.mult))
                    split(2 * i + (t0 + 3), (t0 + 1) % 2)

                if last:
                    tile(0)
                with dve.Fori(1 if last else 0, 8) as i:
                    order.enter(i, 0 if last else 2)
                    tile(i)
                    order.leave(8)

            branch(T_YB, 0, False)
            branch(T_YA, 16, True)
            for f in range(KT):
                dve.wait_ge(s_mhi, f + 1)
                dve.tensor_tensor(mlo[:, f, :], merged[:, f, :], mhi[:, f, :].bitcast(F32), ALU.subtract)\
                    .then_inc(s_mlo, 1)

            def residual(n, t0, hi, lo, g):
                with dve.Fori(0, 4) as i:
                    for j in range(2):
                        t, slot = 2 * i + (t0 + j), (t0 + j) % 2
                        f = 2 * i + j
                        if n == 1 and j == 0:
                            dve.wait_ge(s_back, 16 * i + 16)
                        for h in range(2):
                            dve.wait_ge(s_acc, 2 * t + (h + 1))
                            r = resid[:, bass.ds(f, 1), h * HALF:(h + 1) * HALF].rearrange("p a n -> p (a n)")
                            dve.tensor_tensor(r, ps(2 * slot + h), r, ALU.add).then_inc(s_free, 1)
                        split(t + 2, slot)
                        lower(n, f, resid, hi, lo, f + g)

            residual(1, T_WO, x2hi, x2lo, PCOL["norm_mix_w_2"])
            dve.wait_ge(s_late, LATE_CONSTS)
            order.link(dve.memset(stats[:, :], 0.0))
            inverse(1)
            for g, w in enumerate(POOL_WINDOWS):
                t, slot = T_P + g, (T_P + g) % 2
                for h in range(2):
                    evac(t, h, slot, pool32[:, g, h * HALF:(h + 1) * HALF]).then_inc(s_free, 1)
                split(t + 2, slot)
                dve.wait_ge(s_free, 2 * t + 2)
                src, step, bufs = pool32[:, g, :], 1, (pa, pb)
                while step < w:
                    dst = bufs[0][:, :]
                    dve.tensor_tensor(dst[:, step:S], src[:, step:S], src[:, 0:S - step], ALU.add)
                    order.link(dve.tensor_copy(dst[:, 0:step], src[:, 0:step]))
                    src, step, bufs = dst, 2 * step, bufs[::-1]
                other = bufs[0]
                order.link(dve.tensor_tensor(other[:, 0:w], src[:, 0:w], rcnt[:, 0:w], ALU.mult))
                dve.scalar_tensor_tensor(out=pool32[:, g, w:S], in0=src[:, w:S], scalar=1.0 / w,
                                         in1=pool32[:, g, w:S], op0=ALU.mult, op1=ALU.subtract)
                dve.tensor_tensor(pool32[:, g, 0:w], other[:, 0:w], pool32[:, g, 0:w], ALU.subtract)\
                    .then_inc(s_p_windows, 1)
                dve.wait_ge(s_p_windows, g + 1)
            for h in range(2):
                evac(T_GL, h, T_GL % 2, glow[:, h * HALF:(h + 1) * HALF], (0, 16)).then_inc(s_free, 1)
            split(T_GL + 2, T_GL % 2)
            for n in range(8):
                g, h = n // 2, n % 2
                c = PCOL["pool_scale_2"] + g
                dve.wait_ge(s_pool_mixed, n + 1)
                dve.tensor_scalar(pool32[:, g, h * HALF:(h + 1) * HALF], ps(4 + n % 4), pcol[:, c:c + 1], None,
                                  ALU.mult).then_inc(s_pool_done, 1)

            def put(n, dst):
                for h in range(2):
                    evac(n, h, n % 2, dst[:, h * HALF:(h + 1) * HALF]).then_inc(s_free, 1)

            put(T_QK, qk32[:, 0, :])
            split(T_QK + 2, T_QK % 2)

            def log_gates(m):
                b = PCOL["gk_b_2"] + m
                for h in range(2):
                    n = 2 * m + h
                    half = slice(h * HALF, (h + 1) * HALF)
                    order.link(dve.tensor_scalar(gk[:, m, half], ps(4 + n), pcol[:, b:b + 1], None, ALU.add))
                    order.link(dve.tensor_scalar(gsum[:, half], gk[:, m, half], 0.0, None, ALU.min))
                    dve.scalar_tensor_tensor(out=ghalf[:, :], in0=gsum[:, half], scalar=2.0, in1=gk[:, m, half],
                                             op0=ALU.mult, op1=ALU.subtract).then_inc(s_gl_min, 1)
                    dve.wait_ge(s_gate_ln, n + 1)
                    order.link(dve.tensor_tensor(gk[:, m, half], gsum[:, half], ghalf[:, :], ALU.subtract))

            def gate_sums(m):
                for c in range(S // CHUNK):
                    chunk = slice(c * CHUNK, (c + 1) * CHUNK)
                    last = dve.tensor_tensor_scan(gsum[:, chunk], ones[:, 0:CHUNK], gk[:, m, chunk], 0.0,
                                                  ALU.mult, ALU.add)
                order.link(last)
                g3 = gsum[:, :].rearrange("p (c n) -> p c n", n=CHUNK)
                dve.tensor_tensor(gk[:, m, :].rearrange("p (c n) -> p c n", n=CHUNK),
                                  g3[:, :, CHUNK - 1:CHUNK].broadcast_to([P, S // CHUNK, CHUNK]), g3, ALU.subtract)\
                    .then_inc(s_gl_sum, 1)

            def gate_products(m):
                for h in range(2):
                    half = slice(h * HALF, (h + 1) * HALF)
                    n = 4 * m + 2 * h
                    dve.wait_ge(s_gk_exp, n + 1)
                    dve.scalar_tensor_tensor(out=qk32[:, m, half], in0=qk32[:, m, half], scalar=0.125,
                                             in1=ghalf[:, :], op0=ALU.mult, op1=ALU.mult).then_inc(s_gk_used, 1)
                    dve.wait_ge(s_gk_exp, n + 2)
                    order.link(dve.tensor_tensor(gk[:, m, half], gk[:, m, half], qk32[:, 2 + m, half], ALU.mult))
                    dve.tensor_tensor(qk32[:, 2 + m, half], qk32[:, 2 + m, half], ghalf[:, :], ALU.mult)\
                        .then_inc(s_gk_used, 1)
                dve.wait_ge(s_gk_used, 4 * m + 4)

            for n in range(T_QK + 1, T_WO2):
                dst = qk32[:, n - T_QK, :] if n < T_V else gv32[:, n - T_V, :] if n < T_R else r32[:, qm(n - T_R), :]
                put(n, dst)
                split(n + 2, n % 2)
                if n == T_QK + 2:
                    dve.wait_ge(s_gate_z, 1)
                    log_gates(0)
                if n == T_QK + 3:
                    gate_sums(0)
                if n == T_V:
                    gate_products(0)
                if n == T_V + 1:
                    log_gates(1)
                if n == T_V + 2:
                    gate_sums(1)
                if n == T_V + 3:
                    gate_products(1)
                if n >= T_R:
                    for h in range(2):
                        k = 2 * (n - T_R) + h
                        dve.wait_ge(s_r_tanh, k + 1)
                        r = r32[:, qm(n - T_R), h * HALF:(h + 1) * HALF]
                        dve.scalar_tensor_tensor(out=r, in0=ps(4 + h), scalar=1.0, in1=r, op0=ALU.add,
                                                 op1=ALU.mult).then_inc(s_r_silu, 1)
            dve.wait_ge(s_r_silu, 8)
            for n in range(2):
                order.link(dve.memset(gst[n][:, :, :, :], 0.0))
            order.link(dve.memset(gss[0][:, :, :, :], 0.0))

            def gla_mask(b):
                dve.wait_ge(s_gla_scores, b + 1)
                if b >= 2:
                    dve.wait_ge(s_gla_o, b - 1)
                dve.copy_predicated(gst[b % 2][:, :, :, :], cmask[:, :].bitcast(U32)
                                    .rearrange("p (a b n) -> p a b n", a=1, b=1).broadcast_to([P, 2, 2, P]),
                                    bank[3][:, :, 0:2 * P].rearrange("p q (m n) -> p q m n", m=2))\
                    .then_inc(s_gla_masked, 1)

            def gla_state(b):
                dve.wait_ge(s_gla_kv, b + 1)
                if b:
                    dve.wait_ge(s_gla_o, b)
                for c in range(2):
                    new = gss[b % 2][:, 1, :, :] if c == 0 else gss[(b + 1) % 2][:, 0, :, :]
                    for m in range(2):
                        last = dve.scalar_tensor_tensor(
                            out=new[:, m, :], in0=gss[b % 2][:, c, m, :], scalar=dec[:, m, 2 * b + c:2 * b + c + 1],
                            in1=bank[1][:, c, m * P:(m + 1) * P], op0=ALU.mult, op1=ALU.add)
                    if c == 0:
                        order.link(last)
                    else:
                        last.then_inc(s_gla_state, 1)
                        dve.wait_ge(s_gla_state, b + 1)

            def gla_gate(b):
                dve.wait_ge(s_gla_o_root, b + 1)
                c = PCOL["gla_norm_w_2"]
                grec = R[:, 0:HALF].rearrange("p (q n) -> p q n", q=2)
                order.link(dve.reciprocal(grec, ps(5).rearrange("p (q n) -> p q n", q=2)))
                order.link(dve.scalar_tensor_tensor(out=go[b % 2][:, :, :], in0=go[b % 2][:, :, :],
                                                    scalar=pcol[:, c:c + 1], in1=grec, op0=ALU.mult,
                                                    op1=ALU.mult))
                o = go[b % 2][:, :, :].rearrange("p q (m n) -> p (q m) n", m=2)
                dve.scalar_tensor_tensor(out=o, in0=o, scalar=0.5, in1=r32[:, :, b * P:(b + 1) * P], op0=ALU.mult,
                                         op1=ALU.mult).then_inc(s_gla_gated, 1)

            def gla_lo(b):
                dve.wait_ge(s_gla_hi, b + 1)
                blk = slice(b * P, (b + 1) * P)
                dve.tensor_tensor(by_half(c2lo[:, 4:8, blk]), go[b % 2][:, :, :].rearrange("p q (m n) -> p q m n", m=2),
                                  by_half(c2hi[:, 4:8, blk]).bitcast(F32), ALU.subtract).then_inc(s_gla_lo, 1)

            gla_mask(0)
            gla_state(0)
            for b in range(NB):
                if b + 1 < NB:
                    gla_mask(b + 1)
                    gla_state(b + 1)
                if b:
                    gla_lo(b - 1)
                if b == NB - 1:
                    dve.wait_ge(s_gla_o, NB)
                    for g in range(4):
                        dve.wait_ge(s_concat_hi, g + 1)
                        dve.tensor_tensor(c2lo[:, g, :], pool32[:, g, :], c2hi[:, g, :].bitcast(F32),
                                          ALU.subtract).then_inc(s_concat_lo, 1)
                gla_gate(b)
            gla_lo(NB - 1)
            residual(2, T_WO2, x3hi, x3lo, PCOL["norm_xattn_w_2"])

            inverse(2)
            put(T_XQ, xq32[:, 0, :])
            dve.wait_ge(s_mem_squared, 3)
            dve.reciprocal(stats[:, 4:6], stats[:, 2:4]).then_inc(s_mem_inverse, 1)
            split(T_XQ + 2, T_XQ % 2)
            put(T_XQ + 1, xq32[:, 1, :])
            split(T_XQ + 3, (T_XQ + 1) % 2)
            for c in range(4):
                dve.wait_ge(s_mem_hi_ready, c + 1)
                for f in range(2 * c, 2 * c + 2):
                    g = PCOL["norm_mem_w_2"] + f
                    last = dve.scalar_tensor_tensor(out=mtlo[:, f, :], in0=ps(4 + c)[:, (f % 2) * MEM:(f % 2 + 1) * MEM],
                                                    scalar=pcol[:, g:g + 1], in1=mthi[:, f, :].bitcast(F32),
                                                    op0=ALU.mult, op1=ALU.subtract)
                last.then_inc(s_mem_lo_ready, 1)
            for f in range(2, KT):
                t = T_XQ + f
                if f > 2:
                    split(t + 1, (t + 1) % 2)
                put(t, xq32[:, f, :])
            for t in range(T_MK, T_MV):
                split(t + 1, (t + 1) % 2)
                dve.wait_ge(s_mem_k_hi_ready, t - T_MK + 1)
                dve.tensor_tensor(mklo[:, t - T_MK, :], ps(2 * (t % 2))[:, 0:MEM],
                                  mkhi[:, t - T_MK, :].bitcast(F32), ALU.subtract).then_inc(s_free, 2)
            for t in range(T_MV, T_XO):
                split(t + 1, (t + 1) % 2)
                dve.wait_ge(s_acc, 2 * t + 2)
                dve.tensor_copy(mv32[:, :, (t - T_MV) * P:(t - T_MV + 1) * P],
                                ps(2 * (t % 2))[:, 0:MEM].rearrange("p (a n) -> p a n", a=2)).then_inc(s_free, 2)
            split(T_XO + 1, (T_XO + 1) % 2)

            def head_lo(h, par):
                dve.wait_ge(s_head_hi, h + 1)
                dve.tensor_tensor(hqlo[par][:, :, :], xq32[:, 2 * h:2 * h + 2, :], hqhi[par][:, :, :].bitcast(F32),
                                  ALU.subtract)
                dve.tensor_tensor(hvlo[par][:, :, :], mv32[:, :, h * XD:(h + 1) * XD],
                                  hvhi[par][:, :, :].bitcast(F32), ALU.subtract).then_inc(s_head_lo, 1)

            def x_maxima(u, j):
                dve.wait_ge(s_x_scores, u + 1)
                if u >= 2:
                    dve.wait_ge(s_x_exp, u - 1)
                order.link(dve.tensor_reduce(mx[j % 2][:, 0:2], ps(4 + j % 2).rearrange("p (a n) -> p a n", a=2),
                                             AX_X, ALU.max))
                dve.tensor_scalar(nm[j % 2][:, 0:2], mx[j % 2][:, 0:2], -float(XD) ** -0.5, None, ALU.mult)\
                    .then_inc(s_x_max, 1)

            def x_normalise(u, j):
                dve.wait_ge(s_x_exp, u + 1)
                order.link(dve.reciprocal(den[j % 2][:, 0:2], sums[j % 2][:, 0:2]))
                for a in range(2):
                    last = dve.tensor_scalar(xsx[j % 2][:, a, :], xsx[j % 2][:, a, :], den[j % 2][:, a:a + 1], None,
                                             ALU.mult)
                last.then_inc(s_x_probs, 1)

            def x_turned_lo(u, j):
                dve.wait_ge(s_x_pt_hi, u + 1)
                dve.tensor_tensor(xptlo[j % 2][:, :, :], ps(6 + j % 2).rearrange("p (a n) -> p a n", a=2),
                                  xpthi[j % 2][:, :, :].bitcast(F32), ALU.subtract).then_inc(s_x_pt_lo, 1)

            def x_out_lo(u, h, j):
                dve.wait_ge(s_x_o_hi, u + 1)
                tok = slice(2 * j * P, 2 * (j + 1) * P)
                dve.tensor_tensor(xolo[:, 2 * h:2 * h + 2, tok], ps(j % 2).rearrange("p (a n) -> p a n", a=2),
                                  xohi[:, 2 * h:2 * h + 2, tok].bitcast(F32), ALU.subtract).then_inc(s_x_o_lo, 1)

            head_lo(0, 0)
            for u in range(4 * XHEADS):
                h, j = u // 4, u % 4
                if j == 1 and h == 0:
                    head_lo(1, 1)
                x_maxima(u, j)
                if u >= 1:
                    x_normalise(u - 1, (u - 1) % 4)
                if u >= 2:
                    x_turned_lo(u - 2, j)
                if u >= 3:
                    x_out_lo(u - 3, (u - 3) // 4, (u - 3) % 4)
                if j == 2 and 1 <= h < 3:
                    head_lo(h + 1, (h + 1) % 2)
            u_end = 4 * XHEADS
            x_normalise(u_end - 1, 3)
            x_turned_lo(u_end - 2, 0)
            x_out_lo(u_end - 3, 3, 1)
            x_turned_lo(u_end - 1, 1)
            x_out_lo(u_end - 2, 3, 2)
            x_out_lo(u_end - 1, 3, 3)
            residual(3, T_XO, x4hi, x4lo, PCOL["norm_ffn_w_2"])

            t, done = T_FF, 0
            inverse(3)
            order.link(dve.memset(ubuf[:, 0:2], 0.0))

            def conv(i, dst, c, halves=None):
                col = [pcol[:, bass.ds(i + (FFW + 2 * FF_TILES * n + c), 1)] for n in range(4)]
                order.link(dve.tensor_scalar(dst[:, :], ubuf[:, 0:S], col[0], col[3], ALU.mult, ALU.add))
                order.link(dve.scalar_tensor_tensor(out=dst[:, :], in0=ubuf[:, 1:1 + S], scalar=col[1], in1=dst[:, :],
                                                    op0=ALU.mult, op1=ALU.add))
                return dve.scalar_tensor_tensor(out=dst[:, :], in0=ubuf[:, 2:2 + S], scalar=col[2], in1=dst[:, :],
                                                op0=ALU.mult, op1=ALU.add)

            for n in FF_GROUPS:
                with dve.Fori(0, n) as i:
                    order.enter(i, 7)
                    tt, sl = 2 * i + t, t % 2
                    for h in range(2):
                        evac(tt, h, sl, ubuf[:, 2 + h * HALF:2 + (h + 1) * HALF]).then_inc(s_free, 1)
                    split(tt + 2, sl)
                    dve.wait_ge(s_free, i * 4 + (2 * t + 2))
                    conv(i, yg, done).then_inc(s_ffn_gate, 1)
                    dve.wait_ge(s_ffn_gate, i + (done + 1))
                    for h in range(2):
                        evac(tt + 1, h, 1 - sl, ubuf[:, 2 + h * HALF:2 + (h + 1) * HALF]).then_inc(s_free, 1)
                    split(tt + 3, 1 - sl)
                    dve.wait_ge(s_free, i * 4 + (2 * t + 4))
                    order.link(conv(i, yv, FF_TILES + done))
                    for h in range(2):
                        half = slice(h * HALF, (h + 1) * HALF)
                        dve.wait_ge(s_ffn_tanh, i * 2 + (2 * done + h + 1))
                        order.link(dve.scalar_tensor_tensor(out=yg[:, half], in0=ps(4 + h), scalar=1.0,
                                                            in1=yg[:, half], op0=ALU.add, op1=ALU.mult))
                        dve.scalar_tensor_tensor(out=yv[:, half], in0=yg[:, half], scalar=0.5, in1=yv[:, half],
                                                 op0=ALU.mult, op1=ALU.mult).then_inc(s_ffn_prod, 1)
                    for h in range(2):
                        half = slice(h * HALF, (h + 1) * HALF)
                        dve.wait_ge(s_ffn_hi, i * 2 + (2 * done + h + 1))
                        dve.tensor_tensor(flo[:, bass.ds(i, 1), half].rearrange("p a n -> p (a n)"), yv[:, half],
                                          fhi[:, bass.ds(i, 1), half].rearrange("p a n -> p (a n)").bitcast(F32),
                                          ALU.subtract).then_inc(s_ffn_lo, 1)
                    order.leave(n)
                t += 2 * n
                done += n

                def down(i, tail=False):
                    for j in range(2):
                        tt, sl = 2 * i + (t + j), (t + j) % 2
                        f = 2 * i + j
                        for h in range(2):
                            dve.wait_ge(s_acc, 2 * tt + (h + 1))
                            fs = slice(f, f + 1) if isinstance(f, int) else bass.ds(f, 1)
                            r = resid[:, fs, h * HALF:(h + 1) * HALF].rearrange("p a n -> p (a n)")
                            dve.tensor_tensor(r, ps(2 * sl + h), r, ALU.add).then_inc(s_free, 1)
                        if not tail:
                            split(tt + 2, sl)

                with dve.Fori(0, 4 if done < FF_TILES else 3) as i:
                    down(i)
                if done == FF_TILES:
                    down(3, True)
                t += 8
            dve.wait_ge(s_gfin_loaded, 16)
            for b in range(NB):
                n = b % 2
                dve.wait_ge(s_out_squared, 2 * b + 2)
                order.link(dve.reciprocal(stats[:, 4 + n:5 + n], stats[:, 2 + n:3 + n]))
                dve.scalar_tensor_tensor(out=ot[n][:, :], in0=ot[n][:, :], scalar=stats[:, 4 + n:5 + n],
                                         in1=gfin[:, :], op0=ALU.mult, op1=ALU.mult).then_inc(s_out_normed, 1)


N_PAR = len(PARAM_ROWS) + 3 + 4 + 1


_INS = ['x', 'norm_g', 'w_in', 'conv_w', 'q_norm_g', 'k_norm_g', 'sinks', 'w_conv_out', 'w_attn_out', 'gate_b', 'w_out',
        'mem_2', 'norm_mix_w_2', 'w_in_2', 'pool_w_2', 'pool_scale_2', 'gk_w2_2', 'gk_b_2', 'gla_norm_w_2', 'w_out_2',
        'norm_xattn_w_2', 'norm_mem_w_2', 'xattn_wq_2', 'xattn_wkv_2', 'xattn_wo_2', 'norm_ffn_w_2', 'ffn_w_up_2',
        'ffn_conv_w_2', 'ffn_conv_b_2', 'ffn_w_down_2', 'norm_final_w_2']
_OUTS = [((1, 1024, 1024), 'float32')]


def kernel(**inputs):
    import numpy as _np
    import concourse.bacc as _bacc
    from concourse import mybir as _mybir
    from concourse.bass_utils import run_bass_kernel_spmd as _run

    nc = _bacc.Bacc("TRN2", target_bir_lowering=False, num_devices=1)
    arrays, args = {}, []
    for name in _INS:
        a = _np.ascontiguousarray(inputs[name])
        arrays[f"in_{name}_dram"] = a
        args.append(nc.dram_tensor(f"in_{name}_dram", a.shape, _mybir.dt.from_np(a.dtype), kind="ExternalInput").ap())
    for i, (shape, dtype) in enumerate(_OUTS):
        dt = _mybir.dt.from_np(_np.dtype(dtype))
        args.append(nc.dram_tensor(f"out_{i}_dram", shape, dt, kind="ExternalOutput").ap())
    hybrid_then_mixer_kernel(nc, *args)
    r = _run(nc, [arrays], core_ids=[0])
    return r.results[0]["out_0_dram"]
```

```python
from contextlib import ExitStack

import concourse.bass as bass
from concourse import mybir

F32 = mybir.dt.float32
F32R = mybir.dt.float32r
U32 = mybir.dt.uint32
ALU = mybir.AluOpType
ACT = mybir.ActivationFunctionType
AX_X = mybir.AxisListType.X

P = 128
D = 1024
S = 1024
KT = D // P
HALF = 512
NB = S // P
EPS = 1e-6
NEG = -1e30

V_C, B_C, C_C, Z_C, Q_C, K_C, V_A, Z_A, G_A, G_B = 0, 8, 16, 24, 32, 40, 42, 44, 52, 60
HEADS, KV, DH = 16, 4, 64
MEM = 256
POOL_WINDOWS = (2, 4, 8, 16)
CHUNK = 64
XHEADS, XD = 4, 256
FF = 2816
FF_TILES = FF // P
FF_GROUPS = (8, 8, 6)

T_KV = 0
T_Q = T_KV + 4
T_CONV = T_Q + 8
T_Z = T_CONV + 32
T_YB = T_Z + 8
T_YA = T_YB + 16
T_WO = T_YA + 16
T_P = T_WO + 8
T_GL = T_P + 4
T_QK = T_GL + 1
T_V = T_QK + 4
T_R = T_V + 4
T_WO2 = T_R + 4
T_XQ = T_WO2 + 8
X_TILES = [("q", n) for n in range(4)]
for _n in range(4):
    X_TILES += [("q", 4 + _n), ("k", 2 * _n), ("k", 2 * _n + 1), ("v", 2 * _n), ("v", 2 * _n + 1)]
T_X4 = T_XQ + 4
T_XO = T_XQ + len(X_TILES)
T_FF = T_XO + 8
T_END = T_FF + sum(2 * n + 8 for n in FF_GROUPS)

PARAM_ROWS = [("norm_g", 8), ("conv_w", 24), ("gate_b", 16), ("norm_mix_w_2", 8), ("pool_scale_2", 4),
              ("gk_b_2", 2), ("gla_norm_w_2", 1), ("norm_xattn_w_2", 8), ("norm_mem_w_2", 8),
              ("norm_ffn_w_2", 8)]
PCOL, _at = {}, 0
for _name, _n in PARAM_ROWS:
    PCOL[_name] = _at
    _at += _n
ROWS0 = _at
FFW = ROWS0
FFW2 = FFW + 2 * 2 * FF_TILES
PCOLS = FFW2 + 2 * 2 * FF_TILES


class Tally:

    def __init__(self, eng, sem):
        self.eng, self.sem, self.base, self.n, self.i, self.per = eng, sem, 0, 0, None, 0

    def value(self):
        v = self.base + self.n
        return v if self.i is None else self.i * self.per + v

    def add(self, ins):
        self.n += 1
        ins.then_inc(self.sem, 1)

    def link(self, ins):
        self.add(ins)
        self.eng.wait_ge(self.sem, self.value())

    def enter(self, i, per, start=0):
        self.base += self.n - start * per
        self.n, self.i, self.per = 0, i, per

    def leave(self, end):
        assert self.n == self.per, (self.n, self.per)
        self.base += self.per * end
        self.n, self.i = 0, None


def hybrid_then_mixer_kernel(nc, x, norm_g, w_in, conv_w, q_norm_g, k_norm_g, sinks, w_conv_out, w_attn_out,
                             gate_b, w_out, mem_2, norm_mix_w_2, w_in_2, pool_w_2, pool_scale_2, gk_w2_2,
                             gk_b_2, gla_norm_w_2, w_out_2, norm_xattn_w_2, norm_mem_w_2, xattn_wq_2,
                             xattn_wkv_2, xattn_wo_2, norm_ffn_w_2, ffn_w_up_2, ffn_conv_w_2, ffn_conv_b_2,
                             ffn_w_down_2, norm_final_w_2, out):
    ctx = ExitStack()
    with ctx:
        def sem(name):
            return ctx.enter_context(nc.semaphore(name))

        BIG = KT * S * 4
        arena_bytes = nc.sbuf_bytes_remaining // 64 * 64
        arena = ctx.enter_context(nc.sbuf_tensor("arena", [P, arena_bytes // 4], F32))
        base0 = (nc.sbuf_usable_end - nc.sbuf_bytes_remaining - arena_bytes) // 32 * 32 + 32
        end0 = nc.sbuf_usable_end - nc.sbuf_bytes_remaining
        A, B, C, DD, E = (base0 + n * BIG for n in range(5))
        WRING = base0 + 5 * BIG

        def at(name, shape, dtype, offset):
            size = 4
            for n in shape[1:]:
                size *= n
            assert offset + size <= end0, (name, offset + size - end0)
            return nc.alloc_sbuf_tensor_at(name, shape, dtype, offset=offset)

        wbytes = KT * P * 4
        wraw = [at(f"wraw{n}", [P, KT, P], F32, WRING + n * wbytes) for n in range(2)]
        whi = [at(f"whi{n}", [P, KT, P], F32R, WRING + (2 + n) * wbytes) for n in range(2)]
        wlo = [at(f"wlo{n}", [P, KT, P], F32R, WRING + (4 + n) * wbytes) for n in range(2)]
        top = [WRING + 6 * wbytes]

        def keep(name, shape, dtype):
            t = at(name, shape, dtype, top[0])
            size = 4
            for n in shape[1:]:
                size *= n
            top[0] += (size + 31) // 32 * 32
            return t

        R = keep("R", [P, S], F32)
        ident = keep("ident", [P, P], F32)
        ones = keep("ones", [P, P], F32)
        head_ones = keep("head_ones", [P, P], F32)
        mask_rest = keep("mask_rest", [P, 2 * P], F32)
        late = top[0]
        mask_first = keep("mask_first", [P, 2 * P], F32)
        half_sel = keep("half_sel", [P, 30], F32)
        pcol = keep("pcol", [P, PCOLS], F32)
        hgb = keep("hgb", [P, 16], F32)
        sink = keep("sink", [P, HEADS], F32)
        gcols = keep("gcols", [P, 2], F32)
        gkq = keep("gkq", [P, 1], F32)
        eps = keep("eps", [P, 1], F32)
        idle_act = keep("idle_act", [P, 8], F32)
        idle_dve = keep("idle_dve", [P, 8], F32)
        holds = [0]
        rq = keep("rq", [P, NB, 2, 4, 2], F32)
        small = keep("small", [P, 7, 2, 4], F32)
        mx, nm, sd, es, sums, den, rqb = ([small[:, m, n, :] for n in range(2)] for m in range(7))
        cmask = at("chunk_mask", [P, P], F32, late)
        dec = at("dec", [P, 2, S // CHUNK], F32, late + 512)
        stats = at("stats", [P, 8], F32, late + 640)
        rcnt = at("rcnt", [P, 16], F32, late + 672)
        TMP = top[0]

        sq = [at(f"sq{n}", [P, S], F32, TMP + n * 4 * S) for n in range(2)]
        ssum = at("ssum", [P, S], F32, TMP + 8 * S)
        rows = at("rows", [P, 3, P], F32, TMP + 12 * S)
        vraw = at("vraw", [P, 2, S], F32, TMP)
        zraw = at("zraw", [P, S], F32, TMP)
        zth = at("zth", [P, S], F32, TMP + 4 * S)
        zo = at("zo", [P, S], F32, TMP + 8 * S)
        tv = at("tv", [P, S], F32, TMP)
        cv = at("cv", [P, S + 2], F32, TMP + 4 * S)
        zt = at("zt", [P, S], F32, E + 24576)
        th = at("th", [P, S], F32, E + 28672)
        h1 = at("h1", [P, HALF], F32, TMP + 8 * S + 32)

        xhi = at("xhi", [P, KT, S], F32R, A)
        xlo = at("xlo", [P, KT, S], F32R, B)
        xraw = at("xraw", [P, NB, D], F32, C)
        xt32 = at("xt32", [P, KT, S], F32, DD)
        q32 = at("q32", [P, 2, 4, S], F32, C)
        sqq = at("sqq", [P, 2, 4, S], F32, E)
        kT32 = at("kT32", [P, 2, P + S], F32, DD)
        v32 = at("v32", [P, NB + 1, 2 * P], F32, DD + 9216)
        rk = at("rk", [P, 2, S], F32, DD + 9216)
        kraw = at("kraw", [P, 2, S], F32, DD + 18432)
        khi = at("khi", [P, 2, 2 * P], F32R, DD + 18432)
        klo = at("klo", [P, 2, 2 * P], F32R, DD + 20480)
        vhi = at("vhi", [P, 2, 2, P], F32R, DD + 22528)
        vlo = at("vlo", [P, 2, 2, P], F32R, DD + 24576)
        sq16 = at("sq16", [16, S], F32, TMP + 8 * S)
        qhi = at("qhi", [P, 2, 4 * P], F32R, E)
        qlo = at("qlo", [P, 2, 4 * P], F32R, E + 4096)
        Sx = [at(f"Sx{n}", [P, 4, 2 * P], F32, E + 8192 + 4096 * n) for n in range(2)]
        pthi = at("pthi", [P, 2, 4 * P], F32R, E + 16384)
        ptlo = at("ptlo", [P, 2, 4 * P], F32R, E + 20480)
        ohi = at("ohi", [P, KT, S], F32R, DD)
        olo = at("olo", [P, KT, S], F32R, E)
        yc32 = at("yc32", [P, KT, S], F32, E)
        merged = at("merged", [P, KT, S], F32, C)
        mhi = at("mhi", [P, KT, S], F32R, A)
        mlo = at("mlo", [P, KT, S], F32R, B)
        resid = at("resid", [P, KT, S], F32, DD)
        x2hi = at("x2hi", [P, KT, S], F32R, E)
        x2lo = at("x2lo", [P, KT, S], F32R, C)
        qk32 = at("qk32", [P, 4, S], F32, A)
        gv32 = at("gv32", [P, 4, S], F32, A + BIG // 2)
        r32 = at("r32", [P, 4, S], F32, B)
        pool32 = at("pool32", [P, 4, S], F32, B + BIG // 2)
        pa = at("pool_a", [P, S], F32, TMP)
        pb = at("pool_b", [P, S], F32, TMP + 4 * S)
        pw = at("pool_w", [P, 4, P], F32, TMP + 8 * S)
        gk = at("gk", [P, 2, S], F32, TMP)
        gsum = at("gate_sum", [P, S], F32, TMP + 8 * S)
        ghalf = at("gate_half", [P, HALF], F32, TMP + 12 * S)
        glow = at("gate_low", [16, S], F32, B)
        gkw = at("gk_w2", [16, 2 * P], F32, B + 4 * S)
        c2hi = at("c2hi", [P, KT, S], F32R, C)
        c2lo = at("c2lo", [P, KT, S], F32R, E)
        gvt = [at(f"gvt{n}", [P, 4 * P], F32, E + 2048 * n) for n in range(2)]
        gst = [at(f"gst{n}", [P, 2, 2, P], F32, E + 4096 + 2048 * n) for n in range(2)]
        gss = [at(f"gss{n}", [P, 2, 2, P], F32, E + 8192 + 2048 * n) for n in range(2)]
        gket = [at(f"gket{n}", [P, 2 * P], F32, E + 12288 + 1024 * n) for n in range(2)]
        gosq = at("gosq", [P, 2, 2 * P], F32, TMP + 8 * S)
        go = [at(f"go{n}", [P, 2, 2 * P], F32, TMP + 8 * S + 2048 + 2048 * n) for n in range(2)]
        x3hi = at("x3hi", [P, KT, S], F32R, A)
        x3lo = at("x3lo", [P, KT, S], F32R, B)
        xq32 = at("xq32", [P, KT, S], F32, E)
        mthi = at("mem_hi", [P, KT, MEM], F32R, C)
        mtlo = at("mem_lo", [P, KT, MEM], F32R, C + 8192)
        mraw = at("mem_raw", [P, 2, D], F32, C + 16384)
        mkhi = at("mem_k_hi", [P, KT, MEM], F32R, C + 16384)
        mklo = at("mem_k_lo", [P, KT, MEM], F32R, C + 24576)
        mv32 = at("mem_v", [P, 2, D], F32, TMP)
        mvt = at("mem_v_turned", [P, KT, MEM], F32, TMP)
        mjunk = at("mem_squares", [P, D], F32, TMP + 8192)
        xsx = [at(f"xsx{n}", [P, 2, MEM], F32, TMP + 8192 + 2048 * n) for n in range(2)]
        hqhi = [at(f"hqhi{n}", [P, 2, S], F32R, A + 16384 * n) for n in range(2)]
        hqlo = [at(f"hqlo{n}", [P, 2, S], F32R, A + 16384 * n + 8192) for n in range(2)]
        hvhi = [at(f"hvhi{n}", [P, 2, XD], F32R, C + 4096 * n) for n in range(2)]
        hvlo = [at(f"hvlo{n}", [P, 2, XD], F32R, C + 4096 * n + 2048) for n in range(2)]
        xpthi = [at(f"xpthi{n}", [P, 2, MEM], F32R, C + 8192 + 4096 * n) for n in range(2)]
        xptlo = [at(f"xptlo{n}", [P, 2, MEM], F32R, C + 8192 + 4096 * n + 2048) for n in range(2)]
        xohi = at("xohi", [P, KT, S], F32R, E)
        xolo = at("xolo", [P, KT, S], F32R, B)
        x4hi = at("x4hi", [P, KT, S], F32R, A)
        x4lo = at("x4lo", [P, KT, S], F32R, C)
        ubuf = at("ffn_u", [P, S + 2], F32, TMP)
        yg = at("ffn_gate", [P, S], F32, TMP + 4 * S + 32)
        yv = at("ffn_value", [P, S], F32, TMP + 8 * S + 32)
        fhi = at("fhi", [P, KT, S], F32R, E)
        flo = at("flo", [P, KT, S], F32R, B)
        y = at("y", [P, NB, D], F32, C)
        gfin = at("gfin", [P, D], F32, A)
        ojunk = at("out_squares", [P, NB, P], F32, A + 4 * D)
        osq = at("out_square_sums", [P, NB, KT], F32, A + 8 * D)
        osum, oroot, oinv = (at(name, [P, NB], F32, A + 8 * D + 1024 + 32 * n)
                             for n, name in enumerate(("out_sum", "out_root", "out_inverse")))

        def qm(h):
            return h % 2 * 2 + h // 2

        def by_half(a):
            return a.rearrange("p (m q) n -> p q m n", q=2)

        bank = [ctx.enter_context(nc.psum_tensor(f"bank{n}", [P, 2, HALF], F32)) for n in range(4)]

        def ps(n):
            return bank[n // 2][:, n % 2, :]

        s_par = sem("params_loaded")
        s_par2 = sem("later_params_loaded")
        s_x = [sem(f"x_loaded{n}") for n in range(4)]
        s_const = sem("consts_built")
        s_w = [sem(f"weights_loaded{n}") for n in range(2)]
        s_whi = sem("weights_hi")
        s_wlo = sem("weights_lo")
        s_acc = sem("acc_ready")
        s_free = sem("acc_free")
        s_pt = sem("params_transposed")
        s_pcol = sem("pcol_ready")
        s_xt = sem("x_transposed")
        s_xc = sem("x_copied")
        s_spill = sem("x_spilled")
        s_back = sem("x_back")
        s_xhi = sem("x_hi")
        s_xlo = sem("x_lo")
        s_sq = sem("squares_ready")
        s_sum = sem("squares_summed")
        s_ms = sem("mean_square")
        s_rs = sem("root")
        s_r = sem("r_ready")
        s_dve = sem("dve_order")
        s_ksq = sem("k_squares")
        s_kms = sem("k_mean_square")
        s_krs = sem("k_root")
        s_kn = sem("k_normed")
        s_pad = sem("kv_padded")
        s_qsq = sem("q_squares")
        s_qms = sem("q_mean_square")
        s_q16 = sem("q_sums_copied")
        s_q16t = sem("q_sums_turned")
        s_qrs = sem("q_root")
        s_vt = sem("v_transposed")
        s_v = sem("v_ready")
        s_phi = sem("unit_hi")
        s_plo = sem("unit_lo")
        s_vhi = sem("unit_v_hi")
        s_vlo = sem("unit_v_lo")
        s_s = sem("scores_ready")
        s_sf = sem("scores_read")
        s_neg = sem("neg_max")
        s_exp = sem("exp_done")
        s_p = sem("probs_ready")
        s_t = sem("probs_transposed")
        s_pthi = sem("pt_hi")
        s_ptlo = sem("pt_lo")
        s_o = sem("o_ready")
        s_od = sem("o_copied")
        s_zt = sem("z_tanh")
        s_zof = sem("z_gated")
        s_zhi = sem("z_hi")
        s_zlo = sem("z_lo")
        s_gt = sem("gate_tanh")
        s_ct = sem("conv_tanh")
        s_cof = sem("conv_gated")
        s_conv_stored = sem("conv_stored")
        s_conv_back = [sem(f"conv_back{n}") for n in range(4)]
        s_chi = sem("conv_hi")
        s_clo = sem("conv_lo")
        s_mg = sem("merged_ready")
        s_mhi = sem("merged_hi")
        s_mlo = sem("merged_lo")
        s_ft = sem("out_transposed")
        s_fc = sem("out_copied")
        s_store = sem("out_stored")
        s_p_windows = sem("p_windows")
        s_pool_mixed = sem("pool_mixed")
        s_pool_done = sem("pool_done")
        s_late = sem("late_consts_built")
        s_pw_loaded = sem("pool_w_loaded")
        s_gate_z = sem("gate_z")
        s_gl_min = sem("gate_min")
        s_gl_sum = sem("gate_sums")
        s_gk_used = sem("gk_exp_used")
        s_ffn_gate = sem("ffn_gate_conv")
        s_gate_exp = sem("gate_exp")
        s_gate_ln = sem("gate_ln")
        s_gk_exp = sem("gk_exp")
        s_r_tanh = sem("r_tanh")
        s_r_silu = sem("r_silu")
        s_gk_loaded = sem("gk_loaded")
        s_gla_turned = sem("gla_turned")
        s_gla_copied = sem("gla_copied")
        s_gla_scores = sem("gla_scores")
        s_gla_masked = sem("gla_masked")
        s_gla_kv = sem("gla_kv")
        s_gla_state = sem("gla_state")
        s_gla_o = sem("gla_o")
        s_gla_o_copied = sem("gla_o_copied")
        s_gla_o_sum = sem("gla_o_sum")
        s_gla_o_root = sem("gla_o_root")
        s_gla_gated = sem("gla_gated")
        s_gla_hi = sem("gla_hi")
        s_gla_lo = sem("gla_lo")
        s_concat_hi = sem("concat_hi")
        s_concat_lo = sem("concat_lo")
        s_mem_loaded = sem("mem_loaded")
        s_mem_squared = sem("mem_squared")
        s_mem_inverse = sem("mem_inverse")
        s_mem_scaled = sem("mem_scaled")
        s_mem_turned = sem("mem_turned")
        s_mem_hi_ready = sem("mem_hi_ready")
        s_mem_lo_ready = sem("mem_lo_ready")
        s_mem_k_hi_ready = sem("mem_k_hi_ready")
        s_head_hi = sem("head_hi")
        s_head_lo = sem("head_lo")
        s_mem_v_turned = sem("mem_v_turned")
        s_mem_v = sem("mem_v_ready")
        s_head_v_hi = sem("head_v_hi")
        s_head_v_lo = sem("head_v_lo")
        s_x_scores = sem("x_scores")
        s_x_max = sem("x_max")
        s_x_exp = sem("x_exp")
        s_x_probs = sem("x_probs")
        s_x_turned = sem("x_turned")
        s_x_pt_hi = sem("x_pt_hi")
        s_x_pt_lo = sem("x_pt_lo")
        s_x_o = sem("x_o")
        s_x_o_hi = sem("x_o_hi")
        s_x_o_lo = sem("x_o_lo")
        s_ffn_tanh = sem("ffn_tanh")
        s_ffn_prod = sem("ffn_prod")
        s_ffn_hi = sem("ffn_hi")
        s_ffn_lo = sem("ffn_lo")
        s_gfin_loaded = sem("gfin_loaded")
        s_out_squared = sem("out_squared")
        s_out_normed = [sem(f"out_normed{n}") for n in range(2)]
        s_out_inverse = sem("out_inverse")
        s_out_summed = sem("out_summed")
        s_out_root = sem("out_root")

        CONV_BANKS = ((0, 1), (2, 1))
        CONSTS, LATE_CONSTS = 15, 19

        def tiles(w):
            return w.rearrange("(k p) (t n) -> p k t n", p=P, n=P)

        w1 = tiles(w_in[0])
        spill = nc.dram_tensor("x_spill", [P, KT * S], F32).ap()
        spill_v = spill.rearrange("p (k s) -> p k s", k=KT)
        conv_spill = nc.dram_tensor("conv_spill", [P, KT * S], F32).ap().rearrange("p (k s) -> p k s", k=KT)

        block = ctx.enter_context(nc.Block())

        def cut(start, n):
            return slice(start, start + n) if isinstance(start, int) else bass.ds(start, n)

        def first_block(b):
            return isinstance(b, int)

        def hold(eng, sem, value):
            eng.wait_ge(sem, value)
            holds[0] = (holds[0] + 1) % 8
            if eng.engine == nc.scalar.engine:
                eng.activation(idle_act[:, holds[0]:holds[0] + 1], eps[:, :], ACT.Copy)
            else:
                eng.tensor_copy(idle_dve[:, holds[0]:holds[0] + 1], eps[:, :])

        @block.sync
        def _(sp):
            def load(t, slot, src):
                if not isinstance(t, int) or t >= 2:
                    sp.wait_ge(s_wlo, t - 1)
                k = src.shape[1]
                sp.dma_start(wraw[slot][:, 0:k, :], src).then_inc(s_w[slot], 16)

            def loads(t0, n, *srcs):
                m = len(srcs)
                with sp.Fori(0, n // m) as i:
                    for j, (w, c, step) in enumerate(srcs):
                        load(m * i + (t0 + j), (t0 + j) % 2, w[:, :, bass.ds(i * step + c, 1), :]
                             .rearrange("p k t n -> p k (t n)"))

            n_par = [0]

            def par(dst, src):
                sp.dma_start(dst, src).then_inc(s_par, 16)
                n_par[0] += 1

            named = dict(norm_g=norm_g, conv_w=conv_w, gate_b=gate_b, norm_mix_w_2=norm_mix_w_2,
                         pool_scale_2=pool_scale_2, gk_b_2=gk_b_2, gla_norm_w_2=gla_norm_w_2,
                         norm_xattn_w_2=norm_xattn_w_2, norm_mem_w_2=norm_mem_w_2, norm_ffn_w_2=norm_ffn_w_2)
            x_v = x[0].rearrange("(b p) d -> p b d", p=P)

            def load_x(n):
                c = slice(n * D // 4, (n + 1) * D // 4)
                sp.dma_start(xraw[:, :, c], x_v[:, :, c]).then_inc(s_x[n], 16)

            load_x(0)
            for name, n in PARAM_ROWS:
                src = named[name]
                src = src.rearrange("a b (t n) -> (a b t) n", n=P) if name == "conv_w" \
                    else src.rearrange("a (t n) -> (a t) n", n=P)
                par(rows[PCOL[name]:PCOL[name] + n, 0, :], src)
            assert n_par[0] == N_PAR
            for n in range(1, 4):
                load_x(n)

            for t, c in ((0, K_C), (1, K_C + 1), (2, V_A), (3, V_A + 1)):
                load(t, t % 2, w1[:, :, c, :])
                if t == 1:
                    for f in range(KT):
                        sp.wait_ge(s_xc, 2 * f + 2)
                        sp.dma_start(spill_v[:, f, :], xt32[:, f, :]).then_inc(s_spill, 16)
            loads(T_Q, 8, (w1, Q_C, 2), (w1, Q_C + 1, 2))
            loads(T_CONV, 32, (w1, V_C, 1), (w1, C_C, 1), (w1, B_C, 1), (w1, Z_C, 1))
            loads(T_Z, 8, (w1, Z_A, 2), (w1, Z_A + 1, 2))
            loads(T_YB, 16, (w1, G_B, 1), (tiles(w_attn_out[0]), 0, 1))
            loads(T_YA, 16, (w1, G_A, 1), (tiles(w_conv_out[0]), 0, 1))
            wo = tiles(w_out[0])
            loads(T_WO, 8, (wo, 0, 2), (wo, 1, 2))
            win2 = w_in_2[0]
            w2p = tiles(win2[:, 0:4 * P])
            w2q = tiles(win2[:, 4 * P:8 * P])
            w2v = tiles(win2[:, 8 * P:12 * P])
            w2g = tiles(win2[:, 12 * P:13 * P])
            w2r = tiles(win2[:, 12 * P + 16:16 * P + 16])
            loads(T_P, 4, (w2p, 0, 2), (w2p, 1, 2))
            load(T_GL, T_GL % 2, w2g[:, :, 0, :])
            loads(T_QK, 4, (w2q, 0, 2), (w2q, 1, 2))
            loads(T_V, 4, (w2v, 0, 2), (w2v, 1, 2))
            loads(T_R, 4, (w2r, 0, 2), (w2r, 1, 2))
            w = tiles(w_out_2[0])
            loads(T_WO2, 8, (w, 0, 2), (w, 1, 2))
            wq, wkv = tiles(xattn_wq_2[0]), tiles(xattn_wkv_2[0])
            loads(T_XQ, 4, (wq, 0, 2), (wq, 1, 2))
            loads(T_X4, 20, *[{"q": (wq, n, 2), "k": (wkv, n, 4), "v": (wkv, KT + n, 4)}[kind]
                              for kind, n in X_TILES[4:14]])
            w = tiles(xattn_wo_2[0])
            loads(T_XO, 8, (w, 0, 2), (w, 1, 2))
            wup = tiles(ffn_w_up_2[0])
            t, c = T_FF, 0
            for n in FF_GROUPS:
                loads(t, 2 * n, (wup, c, 1), (wup, FF_TILES + c, 1))
                t += 2 * n
                w = tiles(ffn_w_down_2[0, c * P:(c + n) * P, :])
                loads(t, 8, (w, 0, 2), (w, 1, 2))
                t, c = t + 8, c + n
            out_v = out[0].rearrange("(b p) d -> p b d", p=P)
            for b in range(NB):
                sp.wait_ge(s_out_normed[b % 2], b // 2 + 1)
                sp.dma_start(out_v[:, b, :], y[:, b, :]).then_inc(s_store, 16)
            sp.wait_ge(s_store, 16 * NB)

        @block.gpsimd
        def _(pool):
            built = Tally(pool, s_const)
            built.link(pool.memset(ident[:, :], 0.0))
            built.link(pool.affine_select(out=ident[:, :], in_=ident[:, :], compare_op=ALU.not_equal, fill=1.0,
                                          base=0, pattern=[[-1, P]], channel_multiplier=1))
            built.link(pool.memset(eps[:, :], EPS))
            built.link(pool.memset(ones[:, :], 1.0))
            built.link(pool.memset(head_ones[:, :], 0.0))
            built.link(pool.memset(half_sel[:, :], 0.0))
            for h in range(2):
                built.link(pool.memset(head_ones[64 * h:64 * h + 64, 64 * h:64 * h + 64], 1.0))
                built.link(pool.memset(half_sel[64 * h:64 * h + 64, 14 + h:15 + h], 1.0))
            built.link(pool.memset(mask_rest[:, :], 0.0))
            built.link(pool.affine_select(out=mask_rest[:, :], in_=mask_rest[:, :], compare_op=ALU.is_gt, fill=NEG,
                                          base=0, pattern=[[1, 2 * P]], channel_multiplier=-1))
            built.link(pool.affine_select(out=mask_rest[:, :], in_=mask_rest[:, :], compare_op=ALU.is_ge, fill=NEG,
                                          base=P, pattern=[[-1, 2 * P]], channel_multiplier=1))
            built.link(pool.memset(mask_first[:, 0:P], NEG))
            built.link(pool.tensor_copy(mask_first[:, P:2 * P], mask_rest[:, P:2 * P]))
            assert built.n == CONSTS
            fw = ffn_conv_w_2.rearrange("a b (t n) -> (a b t) n", n=P)
            late = [(rows[0:4 * FF_TILES, 1, :], fw[0:4 * FF_TILES, :]),
                    (rows[0:2 * FF_TILES, 2, :], fw[4 * FF_TILES:6 * FF_TILES, :]),
                    (rows[2 * FF_TILES:4 * FF_TILES, 2, :], ffn_conv_b_2.rearrange("a (t n) -> (a t) n", n=P)),
                    (sink[:, :], sinks.broadcast_to([P, HEADS]))]
            for h in range(2):
                late += [(gcols[64 * h:64 * h + 64, 0:1], q_norm_g.rearrange("a d -> d a")),
                         (gcols[64 * h:64 * h + 64, 1:2], k_norm_g.rearrange("a d -> d a"))]
            assert len(late) == N_PAR2
            for dst, src in late:
                pool.dma_start(dst, src).then_inc(s_par2, 16)

            def sum_squares(n, f, buf):
                pool.wait_ge(s_sq, f + (8 * n + 1))
                if isinstance(f, int) and f == 0:
                    if n:
                        pool.wait_ge(s_ms, 2 * n)
                    pool.tensor_copy(ssum[:, :], sq[buf][:, :]).then_inc(s_sum, 1)
                else:
                    pool.wait_ge(s_sum, f + 8 * n)
                    pool.tensor_tensor(ssum[:, :], ssum[:, :], sq[buf][:, :], ALU.add).then_inc(s_sum, 1)

            for f in range(KT):
                sum_squares(0, f, f % 2)
            pool.wait_ge(s_kn, 4)
            pool.memset(kT32[:, :, 0:P], 0.0).then_inc(s_pad, 1)
            pool.memset(v32[:, 0, :], 0.0).then_inc(s_pad, 1)
            pool.wait_ge(s_sf, KV)
            late_built = Tally(pool, s_late)
            late_built.link(pool.memset(cmask[:, :], 1.0))
            late_built.link(pool.affine_select(out=cmask[:, :], in_=cmask[:, :], compare_op=ALU.is_ge, fill=0.0,
                                               base=0, pattern=[[1, P]], channel_multiplier=-1))
            late_built.link(pool.memset(cmask[0:CHUNK, CHUNK:P], 0.0))
            for n in range(16):
                late_built.link(pool.memset(rcnt[:, n:n + 1], 1.0 / (n + 1)))
            assert late_built.n == LATE_CONSTS
            with pool.Fori(0, KT) as i:
                pool.wait_ge(s_cof, i + 1)
                pool.dma_start(conv_spill[:, bass.ds(i, 1), :].rearrange("p a n -> p (a n)"), tv[:, :])\
                    .then_inc(s_conv_stored, 16)
            pool.wait_ge(s_conv_stored, 16 * KT)
            pool.wait_ge(s_acc, 2 * T_YA)
            for n in range(4):
                pool.dma_start(yc32[:, 2 * n:2 * n + 2, :], conv_spill[:, 2 * n:2 * n + 2, :])\
                    .then_inc(s_conv_back[n], 16)
            pool.wait_ge(s_acc, 2 * T_WO)
            for n in range(4):
                if n:
                    pool.wait_ge(s_back, 16 * n)
                pool.dma_start(resid[:, 2 * n:2 * n + 2, :], spill_v[:, 2 * n:2 * n + 2, :]).then_inc(s_back, 16)
            for f in range(KT):
                sum_squares(1, f, f % 2)
            pool.wait_ge(s_ms, 4)
            pool.dma_start(pw[:, :, :], pool_w_2[0].rearrange("g c d -> c g d")).then_inc(s_pw_loaded, 16)
            pool.wait_ge(s_acc, 2 * T_P)
            pool.dma_start(gkw[:, :], gk_w2_2[0]).then_inc(s_gk_loaded, 16)
            for f in range(KT):
                sum_squares(2, f, f % 2)
            pool.wait_ge(s_acc, 2 * T_XQ)
            pool.dma_start(mraw[:, :, :], mem_2[0].rearrange("(b p) d -> p b d", p=P)).then_inc(s_mem_loaded, 16)
            for f in range(KT):
                sum_squares(3, f, f % 2)
            pool.wait_ge(s_acc, 2 * (T_END - KT))
            pool.dma_start(gfin[:, :], norm_final_w_2.rearrange("(a d) -> a d", a=1).broadcast_to([P, D]))\
                .then_inc(s_gfin_loaded, 16)

        @block.tensor
        def _(pe):
            def each(sem, base):
                return lambda k, h: None if h else (sem, base + k + 1)

            def dense(t, slot, hi, lo, k_tiles=KT, ready=None, banks=None):
                pe.wait_ge(s_wlo, t + 1)
                for h in range(2):
                    if banks is not None and h == 1:
                        pe.wait_ge(s_free, 2 * t)
                    elif not isinstance(t, int) or t >= 2:
                        pe.wait_ge(s_free, 2 * t + (h - 3))
                    acc = ps(2 * slot + h if banks is None else banks[slot][h])
                    for k in range(k_tiles):
                        if ready is not None and ready(k, h) is not None:
                            pe.wait_ge(*ready(k, h))
                        xh, xl = hi[:, k, h * HALF:(h + 1) * HALF], lo[:, k, h * HALF:(h + 1) * HALF]
                        pe.matmul(acc, whi[slot][:, k, :], xh, start=(k == 0), stop=False)
                        pe.matmul(acc, whi[slot][:, k, :], xl, start=False, stop=False)
                        last = pe.matmul(acc, wlo[slot][:, k, :], xh, start=False, stop=(k == k_tiles - 1))
                    last.then_inc(s_acc, 1)

            def mean_square(n):
                pe.wait_ge(s_sum, 8 * (n + 1))
                for h in range(2):
                    pe.matmul(ps(4 + h), ones[:, :], ssum[:, h * HALF:(h + 1) * HALF], start=True, stop=True)\
                        .then_inc(s_ms, 1)

            pe.wait_ge(s_const, CONSTS)
            pe.wait_ge(s_par, 16 * N_PAR)
            pe.transpose(ps(7)[:, 0:ROWS0], rows[0:ROWS0, 0, :], ident[0:ROWS0, 0:ROWS0]).then_inc(s_pt, 1)
            for f in range(KT):
                for h in range(2):
                    n = 2 * f + h
                    pe.wait_ge(s_x[f // 2], 16)
                    if n == 3:
                        pe.wait_ge(s_pcol, 1)
                    if n >= 4:
                        pe.wait_ge(s_xc, n - 3)
                    for j in range(4):
                        last = pe.transpose(ps(4 + n % 4)[:, j * P:(j + 1) * P],
                                            xraw[:, 4 * h + j, f * P:(f + 1) * P], ident[:, :])
                    last.then_inc(s_xt, 1)
            pe.wait_ge(s_xc, 16)
            dense(0, 0, xhi, xlo, ready=each(s_xlo, 0))
            mean_square(0)
            pe.wait_ge(s_par2, 16 * N_PAR2)
            for n in range(2):
                m = 4 * FF_TILES
                last = pe.transpose(ps(7)[:, n * m:(n + 1) * m], rows[0:m, 1 + n, :], ident[0:m, 0:m])
            last.then_inc(s_pt, 1)
            for t in range(1, 4):
                dense(t, t % 2, xhi, xlo)
            pe.wait_ge(s_ksq, 2)
            pe.wait_ge(s_r, 2)
            pe.wait_ge(s_pcol, 2)
            for n in range(4):
                pe.matmul(ps(4 + n), head_ones[:, :], rk[:, n // 2, (n % 2) * HALF:(n % 2 + 1) * HALF],
                          start=True, stop=True).then_inc(s_kms, 1)
            with pe.Fori(0, 4) as i:
                for j in range(2):
                    dense(2 * i + (T_Q + j), (T_Q + j) % 2, xhi, xlo)
            pe.wait_ge(s_qsq, 8)
            pe.wait_ge(s_free, 2 * T_CONV)
            for h in range(2):
                for j in range(8):
                    last = pe.matmul(ps(h)[0:16, :], half_sel[:, 14 - 2 * j:30 - 2 * j],
                                     sqq[:, j // 4, j % 4, h * HALF:(h + 1) * HALF], start=(j == 0), stop=(j == 7))
                last.then_inc(s_qms, 1)
            pe.wait_ge(s_krs, 4)
            for c in range(4):
                for n in range(4):
                    b, f = 2 * c + n // 2, n % 2
                    last = pe.transpose(ps(4 + c)[:, n * P:(n + 1) * P], vraw[:, f, b * P:(b + 1) * P], ident[:, :])
                last.then_inc(s_vt, 1)
            pe.wait_ge(s_q16, 2)
            for b in range(NB):
                last = pe.transpose(ps(3)[:, b * 16:(b + 1) * 16], sq16[:, b * P:(b + 1) * P], ident[0:16, 0:16])
            last.then_inc(s_q16t, 1)
            pe.wait_ge(s_v, 4)

            def scores(b, g):
                gg, q = g // 2, 64 * (g % 2)
                pe.wait_ge(s_plo, 2 * b + (gg + 1))
                if not first_block(b) or 4 * b + g > 0:
                    pe.wait_ge(s_sf, 4 * b + g)
                for hh in range(4):
                    o = ps(4 + hh // 2)[:, (hh % 2) * 2 * P:(hh % 2 + 1) * 2 * P]
                    qh, ql = (w[q:q + 64, gg, hh * P:(hh + 1) * P] for w in (qhi, qlo))
                    kh, kl = (w[q:q + 64, gg, :] for w in (khi, klo))
                    pe.matmul(o, qh, kh, start=True, stop=False)
                    pe.matmul(o, qh, kl, start=False, stop=False)
                    last = pe.matmul(o, ql, kh, start=False, stop=True)
                last.then_inc(s_s, 1)

            def turn(u, par, first=False):
                pe.wait_ge(s_p, u + 1)
                if not first:
                    pe.wait_ge(s_ptlo, u)
                for kb in range(2):
                    for hh in range(4):
                        last = pe.transpose(ps(6 + kb)[:, hh * P:(hh + 1) * P],
                                            Sx[par][:, hh, kb * P:(kb + 1) * P], ident[:, :])
                last.then_inc(s_t, 1)

            def weigh(u, b, g, first=False):
                pe.wait_ge(s_vlo, 2 * b + (g // 2 + 1))
                pe.wait_ge(s_ptlo, u + 1)
                if not first:
                    pe.wait_ge(s_od, u)
                for kb in range(2):
                    vh, vl = vhi[:, g // 2, kb, :], vlo[:, g // 2, kb, :]
                    pe.matmul(ps(3), vh, pthi[:, kb, :], start=(kb == 0), stop=False)
                    pe.matmul(ps(3), vh, ptlo[:, kb, :], start=False, stop=False)
                    last = pe.matmul(ps(3), vl, pthi[:, kb, :], start=False, stop=(kb == 1))
                last.then_inc(s_o, 1)

            def attend(b):
                for g in range(KV):
                    u = 4 * b + g
                    if not first_block(b) or g >= 2:
                        turn(u - 2, g % 2, first=isinstance(u, int) and u == 2)
                    if not first_block(b) or g >= 3:
                        weigh(u - 3, b if g == 3 else b - 1, (g - 3) % 4, first=isinstance(u, int) and u == 3)
                    dense(u + T_CONV, g % 2, xhi, xlo, banks=CONV_BANKS)
                    scores(b, g)

            attend(0)
            with pe.Fori(1, NB) as b:
                attend(b)
            last_u = 4 * NB
            turn(last_u - 2, 0)
            weigh(last_u - 3, NB - 1, 1)
            dense(T_Z, T_Z % 2, xhi, xlo, banks=CONV_BANKS)
            turn(last_u - 1, 1)
            weigh(last_u - 2, NB - 1, 2)
            weigh(last_u - 1, NB - 1, 3)
            pe.wait_ge(s_od, last_u)

            dense(T_Z + 1, (T_Z + 1) % 2, xhi, xlo)
            with pe.Fori(1, 4) as i:
                for j in range(2):
                    dense(2 * i + (T_Z + j), (T_Z + j) % 2, xhi, xlo)
            with pe.Fori(0, 8) as i:
                dense(2 * i + T_YB, T_YB % 2, xhi, xlo)
                pe.wait_ge(s_zlo, 9)
                dense(2 * i + (T_YB + 1), (T_YB + 1) % 2, ohi, olo)
            with pe.Fori(0, 8) as i:
                dense(2 * i + T_YA, T_YA % 2, xhi, xlo)
                dense(2 * i + (T_YA + 1), (T_YA + 1) % 2, ohi, olo, ready=each(s_clo, 0))
            with pe.Fori(0, 4) as i:
                for j in range(2):
                    dense(2 * i + (T_WO + j), (T_WO + j) % 2, mhi, mlo, ready=each(s_mlo, 0))
            dense(T_P, T_P % 2, x2hi, x2lo, ready=each(s_xlo, 8))
            mean_square(1)
            for t in range(T_P + 1, T_QK):
                dense(t, t % 2, x2hi, x2lo)
            pe.wait_ge(s_pw_loaded, 16)
            for g in range(4):
                for h in range(2):
                    n = 2 * g + h
                    pe.wait_ge(s_p_windows, g + 1)
                    if n == 0:
                        pe.wait_ge(s_r, 4)
                    if n >= 4:
                        pe.wait_ge(s_pool_done, n - 3)
                    pe.matmul(ps(4 + n % 4), pw[:, g, :], pool32[:, g, h * HALF:(h + 1) * HALF],
                              start=True, stop=True).then_inc(s_pool_mixed, 1)
            dense(T_QK, T_QK % 2, x2hi, x2lo)
            pe.wait_ge(s_gk_loaded, 16)
            pe.wait_ge(s_free, 2 * (T_GL + 1))
            pe.wait_ge(s_pool_done, 8)
            for m in range(2):
                for h in range(2):
                    last = pe.matmul(ps(4 + 2 * m + h), gkw[:, m * P:(m + 1) * P],
                                     glow[:, h * HALF:(h + 1) * HALF], start=True, stop=True)
            last.then_inc(s_gate_z, 1)
            dense(T_QK + 1, (T_QK + 1) % 2, x2hi, x2lo)
            with pe.Fori(0, (T_WO2 - T_QK - 2) // 2) as i:
                for j in range(2):
                    dense(2 * i + (T_QK + 2 + j), (T_QK + j) % 2, x2hi, x2lo)

            def gla_turn(b):
                blk = slice(b * P, (b + 1) * P)
                pe.wait_ge(s_gla_masked, b + 1 if b == 0 else b)
                if b:
                    pe.wait_ge(s_gla_copied, b)
                for h in range(4):
                    pe.transpose(ps(4)[:, h * P:(h + 1) * P], gv32[:, h, blk], ident[:, :])
                for m in range(2):
                    last = pe.transpose(ps(6)[:, (2 + m) * P:(3 + m) * P], gk[:, m, blk], ident[:, :])
                last.then_inc(s_gla_turned, 1)

            def gla_scores(b):
                blk = slice(b * P, (b + 1) * P)
                if b:
                    pe.wait_ge(s_gla_copied, b + 1)
                for h in range(4):
                    q, m = 64 * (h % 2), h // 2
                    last = pe.matmul(bank[3][:, h % 2, m * P:(m + 1) * P], qk32[q:q + 64, 2 + m, blk], qk32[q:q + 64, m, blk],
                                     start=True, stop=True)
                last.then_inc(s_gla_scores, 1)

            def gla_kv(b):
                pe.wait_ge(s_gla_copied, b + 1)
                if b:
                    pe.wait_ge(s_gla_state, b)
                for c in range(2):
                    for h in range(4):
                        q, m = 64 * (h % 2), h // 2
                        rows_c = slice(c * CHUNK, (c + 1) * CHUNK)
                        last = pe.matmul(bank[1][q:q + 64, c, m * P:(m + 1) * P],
                                         gket[b % 2][rows_c, h * 64:(h + 1) * 64],
                                         gvt[b % 2][rows_c, h * P:(h + 1) * P], start=True, stop=True)
                last.then_inc(s_gla_kv, 1)

            def gla_out(b):
                pe.wait_ge(s_gla_masked, b + 1)
                pe.wait_ge(s_gla_state, b + 1)
                if b:
                    pe.wait_ge(s_gla_o_copied, b)
                for h in range(4):
                    q, m = 64 * (h % 2), h // 2
                    pe.matmul(bank[0][:, h % 2, m * P:(m + 1) * P], gvt[b % 2][:, h * P:(h + 1) * P],
                              gst[b % 2][:, h % 2, m, :], start=True, stop=False, skip_group_check=True)
                    for c in range(2):
                        lo = m * P + c * CHUNK
                        tok = b * P + c * CHUNK
                        last = pe.matmul(bank[0][:, h % 2, lo:lo + CHUNK], gss[b % 2][q:q + 64, c, m, :],
                                         qk32[q:q + 64, m, tok:tok + CHUNK], start=False, stop=(c == 1),
                                         skip_group_check=True)
                last.then_inc(s_gla_o, 1)

            def gla_sum(b):
                pe.wait_ge(s_gla_o_copied, b + 1)
                if b:
                    pe.wait_ge(s_gla_gated, b)
                pe.matmul(ps(5), ones[:, :], gosq[:, :, :].rearrange("p q n -> p (q n)"), start=True, stop=True)\
                    .then_inc(s_gla_o_sum, 1)

            pe.wait_ge(s_free, 2 * T_WO2)
            pe.wait_ge(s_gk_used, 8)
            pe.wait_ge(s_r_silu, 8)
            gla_scores(0)
            gla_turn(0)
            gla_kv(0)
            for b in range(NB):
                if b + 1 < NB:
                    gla_turn(b + 1)
                gla_out(b)
                if b + 1 < NB:
                    gla_scores(b + 1)
                    gla_kv(b + 1)
                gla_sum(b)
            pe.wait_ge(s_gla_o_copied, NB)
            with pe.Fori(0, 4) as i:
                for j in range(2):
                    dense(2 * i + (T_WO2 + j), (T_WO2 + j) % 2, c2hi, c2lo,
                          ready=lambda k, h: None if h else (s_concat_lo, k + 1) if k < 4 else (s_gla_lo, NB))

            def mem_tile(t, slot):
                pe.wait_ge(s_wlo, t + 1)
                pe.wait_ge(s_free, 2 * t - 2)
                acc = ps(2 * slot)[:, 0:MEM]
                for k in range(KT):
                    pe.matmul(acc, whi[slot][:, k, :], mthi[:, k, :], start=(k == 0), stop=False)
                    pe.matmul(acc, whi[slot][:, k, :], mtlo[:, k, :], start=False, stop=False)
                    last = pe.matmul(acc, wlo[slot][:, k, :], mthi[:, k, :], start=False, stop=(k == KT - 1))
                last.then_inc(s_acc, 2)

            dense(T_XQ, T_XQ % 2, x3hi, x3lo, ready=each(s_xlo, 16))
            mean_square(2)
            dense(T_XQ + 1, (T_XQ + 1) % 2, x3hi, x3lo)
            dense(T_XQ + 2, T_XQ % 2, x3hi, x3lo)
            pe.wait_ge(s_mem_scaled, 2)
            pe.wait_ge(s_r, 6)
            for c in range(4):
                for n in range(4):
                    f, a = 2 * c + n // 2, n % 2
                    last = pe.transpose(ps(4 + c)[:, n * P:(n + 1) * P], mraw[:, a, f * P:(f + 1) * P], ident[:, :])
                last.then_inc(s_mem_turned, 1)
            dense(T_XQ + 3, (T_XQ + 3) % 2, x3hi, x3lo)
            with pe.Fori(0, 2) as i:
                for j, (kind, _) in enumerate(X_TILES[4:14]):
                    t, slot = 10 * i + (T_X4 + j), (T_X4 + j) % 2
                    if kind == "q":
                        dense(t, slot, x3hi, x3lo)
                    else:
                        if j == 1:
                            pe.wait_ge(s_mem_lo_ready, 4)
                        mem_tile(t, slot)
            pe.wait_ge(s_free, 2 * T_XO)
            for c in range(4):
                for n in range(4):
                    a, f = n // 2, 2 * c + n % 2
                    last = pe.transpose(ps(c)[:, n * P:(n + 1) * P], mvt[:, f, a * P:(a + 1) * P], ident[:, :])
            last.then_inc(s_mem_v_turned, 1)

            def x_scores(h, par, j):
                u = 4 * h + j
                pe.wait_ge(s_head_lo, h + 1)
                if u >= 2:
                    pe.wait_ge(s_x_exp, u - 1)
                for a in range(2):
                    blk = slice((2 * j + a) * P, (2 * j + a + 1) * P)
                    o = ps(4 + j % 2)[:, a * MEM:(a + 1) * MEM]
                    for k in range(2):
                        kh, kl = mkhi[:, 2 * h + k, :], mklo[:, 2 * h + k, :]
                        pe.matmul(o, hqhi[par][:, k, blk], kh, start=(k == 0), stop=False)
                        pe.matmul(o, hqhi[par][:, k, blk], kl, start=False, stop=False)
                        last = pe.matmul(o, hqlo[par][:, k, blk], kh, start=False, stop=(k == 1))
                last.then_inc(s_x_scores, 1)

            def x_turn(u, j):
                pe.wait_ge(s_x_probs, u + 1)
                if u >= 2:
                    pe.wait_ge(s_x_pt_lo, u - 1)
                for kb in range(2):
                    for a in range(2):
                        last = pe.transpose(ps(6 + j % 2)[:, (2 * kb + a) * P:(2 * kb + a + 1) * P],
                                            xsx[j % 2][:, a, kb * P:(kb + 1) * P], ident[:, :])
                last.then_inc(s_x_turned, 1)

            def x_weigh(u, par, j):
                pe.wait_ge(s_x_pt_lo, u + 1)
                pe.wait_ge(s_head_v_lo, u // 4 + 1)
                if u >= 2:
                    pe.wait_ge(s_x_o_lo, u - 1)
                for e in range(2):
                    o = ps(j % 2)[:, e * MEM:(e + 1) * MEM]
                    for kb in range(2):
                        vh, vl = (w[par][:, kb, e * P:(e + 1) * P] for w in (hvhi, hvlo))
                        pe.matmul(o, vh, xpthi[j % 2][:, kb, :], start=(kb == 0), stop=False)
                        pe.matmul(o, vh, xptlo[j % 2][:, kb, :], start=False, stop=False)
                        last = pe.matmul(o, vl, xpthi[j % 2][:, kb, :], start=False, stop=(kb == 1))
                last.then_inc(s_x_o, 1)

            def x_head(h, par):
                for j in range(4):
                    u = 4 * h + j
                    x_scores(h, par, j)
                    if u >= 2:
                        x_turn(u - 2, j)
                    if u >= 4:
                        x_weigh(u - 4, 1 - par, j)

            x_head(0, 0)
            x_head(1, 1)
            x_head(2, 0)
            x_head(3, 1)
            last_u = 4 * XHEADS
            for n in range(4):
                if n < 2:
                    x_turn(last_u - 2 + n, n)
                x_weigh(last_u - 4 + n, 1, n)
            pe.wait_ge(s_x_o_lo, last_u)
            with pe.Fori(0, 4) as i:
                for j in range(2):
                    dense(2 * i + (T_XO + j), (T_XO + j) % 2, xohi, xolo)

            t, done = T_FF, 0
            for n in FF_GROUPS:
                if t == T_FF:
                    dense(t, t % 2, x4hi, x4lo, ready=each(s_xlo, 24))
                    mean_square(3)
                    dense(t + 1, (t + 1) % 2, x4hi, x4lo)
                first = 1 if t == T_FF else 0
                with pe.Fori(first, n) as i:
                    for j in range(2):
                        dense(2 * i + (t + j), (t + j) % 2, x4hi, x4lo)
                t += 2 * n
                done += n
                if done == FF_TILES:
                    break
                with pe.Fori(0, 4) as i:
                    for j in range(2):
                        dense(2 * i + (t + j), (t + j) % 2, fhi, flo, k_tiles=n,
                              ready=lambda k, h, n=n, done=done: (s_ffn_lo, 2 * (done - n + k) + h + 1))
                t += 8
            def turn_result(f):
                pe.wait_ge(s_free, 2 * (t + f) + 2)
                for c in range(2):
                    n = 2 * f + c
                    if n >= 4:
                        pe.wait_ge(s_fc, n - 3)
                    for j in range(4):
                        b = 4 * c + j
                        last = pe.transpose(ps(4 + n % 4)[:, j * P:(j + 1) * P], resid[:, f, b * P:(b + 1) * P],
                                            ident[:, :])
                    last.then_inc(s_ft, 1)

            for f in range(KT):
                dense(t + f, (t + f) % 2, fhi, flo, k_tiles=FF_GROUPS[-1],
                      ready=lambda k, h: (s_ffn_lo, 2 * (done - FF_GROUPS[-1] + k) + h + 1))
                if f:
                    turn_result(f - 1)
            turn_result(KT - 1)

        @block.scalar
        def _(act):
            def split(t, slot):
                act.wait_ge(s_w[slot], 16 * (t // 2 + 1))
                if t >= 2:
                    act.wait_ge(s_acc, 2 * (t - 1))
                act.activation(whi[slot][:, :, :], wraw[slot][:, :, :], ACT.Copy).then_inc(s_whi, 1)

            def split_at(i, m, t0):
                slot = t0 % 2
                act.wait_ge(s_w[slot], i * (8 * m) + 16 * (t0 // 2 + 1))
                act.wait_ge(s_acc, i * (2 * m) + 2 * (t0 - 1))
                act.activation(whi[slot][:, :, :], wraw[slot][:, :, :], ACT.Copy).then_inc(s_whi, 1)

            def prepare(f, buf, src, hi, g):
                act.activation(hi[:, f, :], src[:, f, :], ACT.Copy, scale=pcol[:, g:g + 1]).then_inc(s_xhi, 1)
                if f >= 2:
                    act.wait_ge(s_sum, f - 1)
                act.activation(sq[buf][:, :], src[:, f, :], ACT.Square).then_inc(s_sq, 1)

            def root(n):
                for h in range(2):
                    act.wait_ge(s_ms, 2 * n + h + 1)
                    act.activation(ps(4 + h), ps(4 + h), ACT.Sqrt, bias=eps[:, 0:1], scale=1.0 / D)\
                        .then_inc(s_rs, 1)

            act.wait_ge(s_pt, 1)
            act.activation(pcol[:, 0:ROWS0], ps(7)[:, 0:ROWS0], ACT.Copy).then_inc(s_pcol, 1)
            act.wait_ge(s_pcol, 1)
            for f in range(KT):
                act.wait_ge(s_xc, 2 * f + 2)
                prepare(f, f % 2, xt32, xhi, PCOL["norm_g"] + f)
                if f == 4:
                    split(0, 0)
            split(1, 1)
            root(0)
            act.wait_ge(s_pt, 2)
            act.activation(pcol[:, ROWS0:PCOLS], ps(7)[:, 0:PCOLS - ROWS0], ACT.Copy).then_inc(s_pcol, 1)
            for t in range(4):
                if t:
                    split(t + 1, (t + 1) % 2)
                if t < 2:
                    act.wait_ge(s_free, 2 * t + 2)
                    act.activation(rk[:, t, :], kraw[:, t, :], ACT.Square).then_inc(s_ksq, 1)
            for n in range(4):
                act.wait_ge(s_kms, n + 1)
                act.activation(rk[:, n // 2, (n % 2) * HALF:(n % 2 + 1) * HALF], ps(4 + n), ACT.Sqrt,
                               bias=eps[:, 0:1], scale=1.0 / DH).then_inc(s_krs, 1)
            with act.Fori(0, 2) as i:
                for jj in range(4):
                    split_at(i, 4, T_Q + jj + 1)
                    q, j = 64 * (jj // 2), jj % 2
                    hold(act, s_free, i * 8 + 2 * (T_Q + jj + 1))
                    act.activation(sqq[q:q + 64, bass.ds(i, 1), 2 * j:2 * j + 2, :],
                                   q32[q:q + 64, bass.ds(i, 1), 2 * j:2 * j + 2, :], ACT.Square).then_inc(s_qsq, 1)
            for h in range(2):
                act.wait_ge(s_qms, h + 1)
                act.activation(sq16[:, h * HALF:(h + 1) * HALF], ps(h)[0:16, :], ACT.Copy).then_inc(s_q16, 1)
            act.wait_ge(s_pad, 2)
            for c in range(4):
                act.wait_ge(s_vt, c + 1)
                act.activation(v32[:, 1 + 2 * c:3 + 2 * c, :], ps(4 + c).rearrange("p (b n) -> p b n", b=2), ACT.Copy)\
                    .then_inc(s_v, 1)
            act.wait_ge(s_v, 4)
            act.wait_ge(s_q16t, 1)
            act.activation(rq[:, :, :, :, :].rearrange("p b g h s -> p (b g h s)"), ps(3)[:, 0:P], ACT.Sqrt,
                           bias=eps[:, 0:1], scale=1.0 / DH).then_inc(s_qrs, 1)

            def unit_hi(b, gg):
                if not first_block(b):
                    hold(act, s_s, 4 * b + (2 * gg - 2))
                cur = cut(b * P, P)
                keys = cut(b * P, 2 * P)
                act.activation(qhi[:, gg, :].rearrange("p (h n) -> p h n", h=4), q32[:, gg, :, cur], ACT.Copy)
                act.activation(khi[:, gg, :], kT32[:, gg, keys], ACT.Copy).then_inc(s_phi, 1)

            def values_hi(b, gg):
                blocks = cut(b, 2)
                if not first_block(b):
                    hold(act, s_o, 4 * b + (2 * gg - 2))
                act.activation(vhi[:, gg, :, :], v32[:, blocks, gg * P:(gg + 1) * P], ACT.Copy).then_inc(s_vhi, 1)

            def exps(u, par):
                act.wait_ge(s_neg, u + 1)
                for hh in range(4):
                    act.activation(Sx[par][:, hh, :], Sx[par][:, hh, :], ACT.Exp, bias=nm[par][:, hh:hh + 1],
                                   accum_out=sums[par][:, hh:hh + 1])
                act.activation(es[par][:, :], sd[par][:, :], ACT.Exp).then_inc(s_exp, 1)

            def turned_hi(u):
                act.wait_ge(s_t, u + 1)
                if not isinstance(u, int) or u > 0:
                    act.wait_ge(s_o, u)
                act.activation(pthi[:, :, :], bank[3][:, :, :], ACT.Copy).then_inc(s_pthi, 1)

            def keep_o(u, b, g):
                q = 64 * (g % 2)
                cur = cut(b * P, P)
                act.activation(q32[q:q + 64, g // 2, :, cur],
                               ps(3)[q:q + 64, :].rearrange("p (h n) -> p h n", h=4), ACT.Copy).then_inc(s_od, 1)

            def attend(b):
                for g in range(KV):
                    u = 4 * b + g
                    if first_block(b):
                        split(T_CONV + g + 1, (T_CONV + g + 1) % 2)
                    else:
                        split_at(b, 4, T_CONV + g + 1)
                    if g % 2 == 0:
                        unit_hi(b, g // 2)
                    else:
                        values_hi(b, g // 2)
                    if not first_block(b) or g >= 2:
                        turned_hi(u - 2)
                    if not first_block(b) or g >= 3:
                        keep_o(u - 3, b if g == 3 else b - 1, (g - 3) % 4)
                    exps(u, g % 2)
                    if g == 3:
                        act.wait_ge(s_free, 8 * b + (2 * T_CONV + 8))
                        act.activation(th[:, :], zt[:, :], ACT.Tanh, scale=0.5).then_inc(s_ct, 1)

            attend(0)
            with act.Fori(1, NB) as b:
                attend(b)
            last_u = 4 * NB
            turned_hi(last_u - 2)
            keep_o(last_u - 3, NB - 1, 1)
            split(T_Z + 1, (T_Z + 1) % 2)
            turned_hi(last_u - 1)
            keep_o(last_u - 2, NB - 1, 2)
            act.wait_ge(s_o, last_u)
            keep_o(last_u - 1, NB - 1, 3)
            act.wait_ge(s_od, last_u)

            act.wait_ge(s_conv_stored, 16 * KT)
            with act.Fori(0, 2) as i:
                for jj in range(4):
                    q, j = 64 * (jj // 2), jj % 2
                    split_at(i, 4, T_Z + jj + 2)
                    hold(act, s_zlo, i * 4 + (jj + 1))
                    for s in range(2):
                        last = act.activation(zo[64 * s:64 * s + 64, :],
                                              q32[q:q + 64, bass.ds(i, 1), 2 * j + s, :]
                                              .rearrange("p a n -> p (a n)"), ACT.Copy)
                    act.wait_ge(s_free, i * 8 + (2 * T_Z + 2 * jj + 2))
                    act.activation(zth[:, :], zraw[:, :], ACT.Tanh, scale=0.5).then_inc(s_zt, 1)
                    hold(act, s_zof, i * 4 + (jj + 1))
                    act.activation(ohi[:, bass.ds(i * 4 + jj, 1), :].rearrange("p a n -> p (a n)"), zo[:, :],
                                   ACT.Copy).then_inc(s_zhi, 1)

            def gates(i, t0, g0, n0):
                for h in range(2):
                    hold(act, s_free, i * 4 + (2 * t0 + h + 1))
                    act.activation(tv[:, h * HALF:(h + 1) * HALF], tv[:, h * HALF:(h + 1) * HALF], ACT.Tanh,
                                   scale=0.5, bias=hgb[:, bass.ds(i + g0, 1)]).then_inc(s_gt, 1)

            with act.Fori(0, 8) as i:
                split_at(i, 2, T_YB + 2)
                gates(i, T_YB, 8, 0)
                split_at(i, 2, T_YB + 3)
            for f in range(KT):
                act.wait_ge(s_conv_back[f // 2], 16)
                act.activation(ohi[:, f, :], yc32[:, f, :], ACT.Copy).then_inc(s_chi, 1)
            split(T_YA + 2, T_YA % 2)
            gates(0, T_YA, 0, 16)
            split(T_YA + 3, (T_YA + 3) % 2)
            with act.Fori(1, 8) as i:
                split_at(i, 2, T_YA + 2)
                gates(i, T_YA, 0, 16)
                split_at(i, 2, T_YA + 3)
            for f in range(KT):
                act.wait_ge(s_mg, 2 * f + 2)
                act.activation(mhi[:, f, :], merged[:, f, :], ACT.Copy).then_inc(s_mhi, 1)

            def residual(n, t0, hi, g):
                with act.Fori(0, 4) as i:
                    for j in range(2):
                        split_at(i, 2, t0 + j + 2)
                        act.wait_ge(s_free, i * 4 + (2 * t0 + 2 * j + 2))
                        f = 2 * i + j
                        act.activation(hi[:, bass.ds(f, 1), :], resid[:, bass.ds(f, 1), :], ACT.Copy,
                                       scale=pcol[:, bass.ds(f + g, 1)]).then_inc(s_xhi, 1)
                        hold(act, s_sum, f + (8 * n - 1))
                        act.activation(sq[j][:, :].rearrange("p (a n) -> p a n", a=1), resid[:, bass.ds(f, 1), :],
                                       ACT.Square).then_inc(s_sq, 1)

            residual(1, T_WO, x2hi, PCOL["norm_mix_w_2"])
            root(1)
            for n in range(T_P, T_QK + 1):
                split(n + 2, n % 2)

            def log_gates(m):
                for h in range(2):
                    n = 2 * m + h
                    act.wait_ge(s_gl_min, n + 1)
                    act.activation(ghalf[:, :], ghalf[:, :], ACT.Exp).then_inc(s_gate_exp, 1)
                    act.wait_ge(s_gate_exp, n + 1)
                    act.activation(ghalf[:, :], ghalf[:, :], ACT.Ln, bias=ones[:, 0:1]).then_inc(s_gate_ln, 1)

            def gate_exps(m):
                act.wait_ge(s_gl_sum, m + 1)
                last = gsum[:, :].rearrange("p (c n) -> p c n", n=CHUNK)[:, :, CHUNK - 1:CHUNK]\
                    .rearrange("p c n -> p (c n)")
                act.activation(dec[:, m, :], last, ACT.Exp, scale=1.0 / 16)
                for h in range(2):
                    half = slice(h * HALF, (h + 1) * HALF)
                    n = 4 * m + 2 * h
                    if n:
                        act.wait_ge(s_gk_used, n)
                    act.activation(ghalf[:, :], gsum[:, half], ACT.Exp, scale=1.0 / 16).then_inc(s_gk_exp, 1)
                    act.wait_ge(s_gk_used, n + 1)
                    act.activation(ghalf[:, :], gsum[:, half], ACT.Exp, scale=-1.0 / 16)
                    act.activation(gk[:, m, half], gk[:, m, half], ACT.Exp, scale=1.0 / 16).then_inc(s_gk_exp, 1)

            for n in range(T_QK + 1, T_WO2):
                split(n + 2, n % 2)
                if n == T_QK + 2:
                    log_gates(0)
                if n == T_V:
                    gate_exps(0)
                if n == T_V + 1:
                    log_gates(1)
                if n == T_V + 3:
                    gate_exps(1)
                if n >= T_R:
                    for h in range(2):
                        act.wait_ge(s_free, 2 * n + h + 1)
                        if n > T_R:
                            act.wait_ge(s_r_silu, 2 * (n - T_R) + h - 1)
                        act.activation(ps(4 + h), r32[:, qm(n - T_R), h * HALF:(h + 1) * HALF], ACT.Tanh, scale=0.5)\
                            .then_inc(s_r_tanh, 1)

            def gla_copy(b):
                act.wait_ge(s_gla_turned, b + 1)
                if b >= 2:
                    act.wait_ge(s_gla_o, b - 1)
                act.activation(gvt[b % 2][:, :], ps(4), ACT.Copy)
                act.activation(gket[b % 2][:, :], ps(6)[:, 2 * P:4 * P], ACT.Copy).then_inc(s_gla_copied, 1)

            def gla_keep(b):
                act.wait_ge(s_gla_o, b + 1)
                if b:
                    act.wait_ge(s_gla_o_sum, b)
                act.activation(gosq[:, :, :], bank[0][:, :, 0:2 * P], ACT.Square)
                if b >= 2:
                    act.wait_ge(s_gla_lo, b - 1)
                act.activation(go[b % 2][:, :, :], bank[0][:, :, 0:2 * P], ACT.Copy).then_inc(s_gla_o_copied, 1)

            def gla_root(b):
                act.wait_ge(s_gla_o_sum, b + 1)
                act.activation(ps(5), ps(5), ACT.Sqrt, bias=eps[:, 0:1],
                               scale=1.0 / P).then_inc(s_gla_o_root, 1)

            def gla_hi(b):
                act.wait_ge(s_gla_gated, b + 1)
                act.activation(by_half(c2hi[:, 4:8, b * P:(b + 1) * P]),
                               go[b % 2][:, :, :].rearrange("p q (m n) -> p q m n", m=2), ACT.Copy).then_inc(s_gla_hi, 1)

            gla_copy(0)
            for b in range(NB):
                if b + 1 < NB:
                    gla_copy(b + 1)
                gla_keep(b)
                gla_root(b)
                if b:
                    gla_hi(b - 1)
                if 1 <= b < 5:
                    act.activation(c2hi[:, b - 1, :], pool32[:, b - 1, :], ACT.Copy).then_inc(s_concat_hi, 1)
            gla_hi(NB - 1)
            residual(2, T_WO2, x3hi, PCOL["norm_xattn_w_2"])

            root(2)
            split(T_XQ + 2, T_XQ % 2)
            act.wait_ge(s_mem_loaded, 16)
            act.wait_ge(s_ms, 6)
            for a in range(2):
                act.activation(mjunk[:, :], mraw[:, a, :], ACT.Square, accum_out=stats[:, a:a + 1])\
                    .then_inc(s_mem_squared, 1)
                act.wait_ge(s_mem_squared, a + 1)
            act.activation(stats[:, 2:4], stats[:, 0:2], ACT.Sqrt, bias=eps[:, 0:1], scale=1.0 / D)\
                .then_inc(s_mem_squared, 1)
            act.wait_ge(s_mem_inverse, 1)
            for a in range(2):
                act.activation(mraw[:, a, :], mraw[:, a, :], ACT.Copy, scale=stats[:, 4 + a:5 + a])\
                    .then_inc(s_mem_scaled, 1)
            split(T_XQ + 3, (T_XQ + 3) % 2)
            split(T_XQ + 4, T_XQ % 2)
            for c in range(4):
                act.wait_ge(s_mem_turned, c + 1)
                for f in range(2 * c, 2 * c + 2):
                    last = act.activation(mthi[:, f, :], ps(4 + c)[:, (f % 2) * MEM:(f % 2 + 1) * MEM], ACT.Copy,
                                          scale=pcol[:, PCOL["norm_mem_w_2"] + f:PCOL["norm_mem_w_2"] + f + 1])
                last.then_inc(s_mem_hi_ready, 1)
            for j, (kind, n) in enumerate(X_TILES):
                t = T_XQ + j
                if kind == "k":
                    act.wait_ge(s_acc, 2 * t + 2)
                    act.activation(mkhi[:, n, :], ps(2 * (t % 2))[:, 0:MEM], ACT.Copy).then_inc(s_mem_k_hi_ready, 1)
                if j >= 3:
                    split(t + 2, t % 2)

            def head_hi(h, par):
                if h >= 2:
                    act.wait_ge(s_x_scores, 4 * h - 4)
                act.activation(hqhi[par][:, :, :], xq32[:, 2 * h:2 * h + 2, :], ACT.Copy).then_inc(s_head_hi, 1)

            def head_v_hi(h, par):
                act.wait_ge(s_mem_v, 4)
                if h >= 2:
                    act.wait_ge(s_x_o, 4 * h - 4)
                act.activation(hvhi[par][:, :, :], mv32[:, :, h * XD:(h + 1) * XD], ACT.Copy)\
                    .then_inc(s_head_v_hi, 1)

            def x_exps(u, j):
                act.wait_ge(s_x_max, u + 1)
                if u >= 2:
                    act.wait_ge(s_x_turned, u - 1)
                for a in range(2):
                    last = act.activation(xsx[j % 2][:, a, :], ps(4 + j % 2)[:, a * MEM:(a + 1) * MEM], ACT.Exp,
                                          bias=nm[j % 2][:, a:a + 1], scale=float(XD) ** -0.5,
                                          accum_out=sums[j % 2][:, a:a + 1])
                last.then_inc(s_x_exp, 1)

            def x_turned_hi(u, j):
                act.wait_ge(s_x_turned, u + 1)
                if u >= 2:
                    act.wait_ge(s_x_o, u - 1)
                act.activation(xpthi[j % 2][:, :, :], ps(6 + j % 2).rearrange("p (a n) -> p a n", a=2), ACT.Copy)\
                    .then_inc(s_x_pt_hi, 1)

            def x_out_hi(u, h, j):
                act.wait_ge(s_x_o, u + 1)
                act.activation(xohi[:, 2 * h:2 * h + 2, 2 * j * P:2 * (j + 1) * P],
                               ps(j % 2).rearrange("p (a n) -> p a n", a=2), ACT.Copy).then_inc(s_x_o_hi, 1)

            act.wait_ge(s_free, 2 * T_XO)
            head_hi(0, 0)
            for u in range(4 * XHEADS + 4):
                h, j = u // 4, u % 4
                if u < 4 * XHEADS:
                    x_exps(u, j)
                if 2 <= u < 4 * XHEADS + 2:
                    x_turned_hi(u - 2, j)
                if u >= 4:
                    x_out_hi(u - 4, (u - 4) // 4, j)
                if u == 0:
                    head_v_hi(0, 0)
                if u == 1:
                    head_hi(1, 1)
                if j == 0 and 1 <= h < 3:
                    head_hi(h + 1, (h + 1) % 2)
                if j == 3 and h < 3:
                    head_v_hi(h + 1, (h + 1) % 2)
            residual(3, T_XO, x4hi, PCOL["norm_ffn_w_2"])

            def square_result(f):
                for c in range(2):
                    n = 2 * f + c
                    act.wait_ge(s_ft, n + 1)
                    if f:
                        act.wait_ge(s_out_squared, n - 1)
                    for j in range(4):
                        last = act.activation(ojunk[:, 4 * c + j, :], ps(4 + n % 4)[:, j * P:(j + 1) * P], ACT.Square,
                                              accum_out=osq[:, 4 * c + j, f:f + 1])
                    last.then_inc(s_out_squared, 1)

            root(3)
            t, done = T_FF, 0
            for n in FF_GROUPS:
                with act.Fori(0, n) as i:
                    split_at(i, 2, t + 2)
                    for h in range(2):
                        act.wait_ge(s_ffn_gate, i + (done + 1))
                        act.activation(ps(4 + h), yg[:, h * HALF:(h + 1) * HALF], ACT.Tanh, scale=0.5)\
                            .then_inc(s_ffn_tanh, 1)
                    for h in range(2):
                        if h == 1:
                            split_at(i, 2, t + 3)
                        hold(act, s_ffn_prod, i * 2 + (2 * done + h + 1))
                        act.activation(fhi[:, bass.ds(i, 1), h * HALF:(h + 1) * HALF]
                                       .rearrange("p a n -> p (a n)"), yv[:, h * HALF:(h + 1) * HALF],
                                       ACT.Copy).then_inc(s_ffn_hi, 1)
                t += 2 * n
                done += n
                if done == FF_TILES:
                    break
                with act.Fori(0, 4) as i:
                    for j in range(2):
                        split_at(i, 2, t + j + 2)
                t += 8
            for f in range(KT):
                if f + 2 < KT:
                    split(t + f + 2, (t + f) % 2)
                if f:
                    square_result(f - 1)
            square_result(KT - 1)
            act.wait_ge(s_out_summed, 1)
            act.activation(oroot[:, :], osum[:, :], ACT.Sqrt, bias=eps[:, 0:1], scale=1.0 / D).then_inc(s_out_root, 1)
            act.wait_ge(s_out_inverse, 1)
            for b in range(1, NB, 2):
                act.activation(y[:, b, :], y[:, b, :], ACT.Copy, scale=oinv[:, b:b + 1]).then_inc(s_out_normed[1], 1)

        @block.vector
        def _(dve):
            order = Tally(dve, s_dve)

            def split(t, slot):
                dve.wait_ge(s_whi, t + 1)
                dve.tensor_tensor(wlo[slot][:, :, :], wraw[slot][:, :, :], whi[slot][:, :, :].bitcast(F32),
                                  ALU.subtract).then_inc(s_wlo, 1)

            def evac(t, h, slot, dst, parts=(0, P), bank_at=None):
                dve.wait_ge(s_acc, 2 * t + (h + 1))
                lo, hi = parts
                acc = ps(2 * slot + h if bank_at is None else bank_at)
                ins = dve.tensor_tensor(dst, acc[lo:hi, :], R[lo:hi, h * HALF:(h + 1) * HALF], ALU.mult)
                return ins

            def lower(n, f, src, hi, lo, g):
                dve.wait_ge(s_xhi, f + (8 * n + 1))
                fs, gs = cut(f, 1), cut(g, 1)
                dve.scalar_tensor_tensor(out=lo[:, fs, :], in0=src[:, fs, :], scalar=pcol[:, gs],
                                         in1=hi[:, fs, :].bitcast(F32), op0=ALU.mult, op1=ALU.subtract)\
                    .then_inc(s_xlo, 1)

            def inverse(n):
                for h in range(2):
                    dve.wait_ge(s_rs, 2 * n + h + 1)
                    dve.reciprocal(R[:, h * HALF:(h + 1) * HALF], ps(4 + h)).then_inc(s_r, 1)
                dve.wait_ge(s_r, 2 * n + 2)

            dve.wait_ge(s_pcol, 1)
            order.link(dve.tensor_scalar(hgb[:, :], pcol[:, PCOL["gate_b"]:PCOL["gate_b"] + 16], 0.5, None, ALU.mult))
            for f in range(KT + 1):
                for h in range(2):
                    if f < KT:
                        n = 2 * f + h
                        dve.wait_ge(s_xt, n + 1)
                        dve.tensor_copy(xt32[:, f, h * HALF:(h + 1) * HALF], ps(4 + n % 4)).then_inc(s_xc, 1)
                if f:
                    lower(0, f - 1, xt32, xhi, xlo, PCOL["norm_g"] + f - 1)
                if f == 5:
                    split(0, 0)
            split(1, 1)
            inverse(0)
            dve.wait_ge(s_par2, 16 * N_PAR2)
            order.link(dve.tensor_tensor(gkq[:, :], gcols[:, 0:1], gcols[:, 1:2], ALU.mult))
            dve.wait_ge(s_spill, 16 * KT)
            dve.wait_ge(s_sq, 8)
            for t in range(4):
                if t:
                    split(t + 1, (t + 1) % 2)
                for h in range(2):
                    dst = (kraw if t < 2 else vraw)[:, t % 2, h * HALF:(h + 1) * HALF]
                    evac(t, h, t % 2, dst).then_inc(s_free, 1)
            dve.wait_ge(s_krs, 4)
            with dve.Fori(0, 2) as i:
                order.enter(i, 2)
                for jj in range(4):
                    t, slot = i * 4 + (T_Q + jj), (T_Q + jj) % 2
                    split(t + 1, 1 - slot)
                    if jj % 2 == 0:
                        h = slice(jj // 2 * HALF, (jj // 2 + 1) * HALF)
                        hp = slice(P + jj // 2 * HALF, P + (jj // 2 + 1) * HALF)
                        order.link(dve.reciprocal(rk[:, bass.ds(i, 1), h], rk[:, bass.ds(i, 1), h]))
                        dve.scalar_tensor_tensor(out=kT32[:, bass.ds(i, 1), hp], in0=kraw[:, bass.ds(i, 1), h],
                                                 scalar=gkq[:, 0:1], in1=rk[:, bass.ds(i, 1), h], op0=ALU.mult,
                                                 op1=ALU.mult).then_inc(s_kn, 1)
                    q, j = 64 * (jj // 2), jj % 2
                    for h in range(2):
                        for s in range(2):
                            dst = q32[q:q + 64, bass.ds(i, 1), 2 * j + s, h * HALF:(h + 1) * HALF]\
                                .rearrange("p a n -> p (a n)")
                            ins = evac(t, h, slot, dst, (64 * s, 64 * s + 64))
                        ins.then_inc(s_free, 1)
                order.leave(2)
            dve.wait_ge(s_qrs, 1)
            rq_flat = rq[:, :, :, :, :].rearrange("p b g h s -> p (b g h s)")
            order.link(dve.reciprocal(rq_flat, rq_flat))
            order.link(dve.tensor_scalar(rq_flat, rq_flat, float(DH) ** -0.5, None, ALU.mult))

            def unit_lo(b, gg):
                cur = cut(b * P, P)
                keys = cut(b * P, 2 * P)
                dve.wait_ge(s_phi, 2 * b + (gg + 1))
                dve.tensor_tensor(qlo[:, gg, :].rearrange("p (h n) -> p h n", h=4), q32[:, gg, :, cur],
                                  qhi[:, gg, :].bitcast(F32).rearrange("p (h n) -> p h n", h=4), ALU.subtract)
                dve.tensor_tensor(klo[:, gg, :], kT32[:, gg, keys], khi[:, gg, :].bitcast(F32), ALU.subtract)\
                    .then_inc(s_plo, 1)

            def values_lo(b, gg):
                blocks = cut(b, 2)
                dve.wait_ge(s_vhi, 2 * b + (gg + 1))
                dve.tensor_tensor(vlo[:, gg, :, :], v32[:, blocks, gg * P:(gg + 1) * P],
                                  vhi[:, gg, :, :].bitcast(F32), ALU.subtract).then_inc(s_vlo, 1)

            def maxima(b, g, par):
                u = 4 * b + g
                if not first_block(b) or g >= 2:
                    dve.wait_ge(s_t, u - 1)
                hold(dve, s_s, u + 1)
                mask = mask_first if first_block(b) else mask_rest
                for hh in range(4):
                    h = 4 * g + hh
                    last = dve.tensor_tensor_reduce(
                        Sx[par][:, hh, :], ps(4 + hh // 2)[:, (hh % 2) * 2 * P:(hh % 2 + 1) * 2 * P], mask[:, :],
                        rqb[par][:, hh:hh + 1], sink[:, h:h + 1], ALU.add, ALU.max, mx[par][:, hh:hh + 1])
                last.then_inc(s_sf, 1)
                dve.wait_ge(s_sf, u + 1)
                dve.tensor_scalar(nm[par][:, :], mx[par][:, :], -1.0, None, ALU.mult)
                dve.tensor_tensor(sd[par][:, :], sink[:, 4 * g:4 * g + 4], mx[par][:, :], ALU.subtract)\
                    .then_inc(s_neg, 1)

            def load_rq(b, g, par):
                order.add(dve.tensor_copy(rqb[par][:, :], rq[:, cut(b, 1), g // 2, :, g % 2]
                                          .rearrange("p a h -> p (a h)")))
                dve.wait_ge(order.sem, order.value())

            def normalise(u, par):
                dve.wait_ge(s_exp, u + 1)
                order.link(dve.tensor_tensor(den[par][:, :], sums[par][:, :], es[par][:, :], ALU.add))
                order.link(dve.reciprocal(den[par][:, :], den[par][:, :]))
                for hh in range(4):
                    last = dve.tensor_scalar(Sx[par][:, hh, :], Sx[par][:, hh, :], den[par][:, hh:hh + 1], None,
                                             ALU.mult)
                last.then_inc(s_p, 1)

            def turned_lo(u):
                dve.wait_ge(s_pthi, u + 1)
                dve.tensor_tensor(ptlo[:, :, :], bank[3][:, :, :], pthi[:, :, :].bitcast(F32), ALU.subtract)\
                    .then_inc(s_ptlo, 1)

            CW = PCOL["conv_w"]
            hs = [slice(h * HALF, (h + 1) * HALF) for h in range(2)]

            def conv_part(b, g):
                t = 4 * b + (T_CONV + g)
                if g == 0 and not first_block(b):
                    dve.wait_ge(s_conv_stored, b * 16)
                dst = (tv, zt, zt, zt)[g]
                for h in range(2):
                    evac(t, h, 0, dst[:, hs[h]], bank_at=CONV_BANKS[g % 2][h]).then_inc(s_free, 1)
                dve.wait_ge(s_free, 8 * b + (2 * (T_CONV + g) + 2))
                if g == 1:
                    order.link(dve.tensor_tensor(cv[:, 2:2 + S], zt[:, :], tv[:, :], ALU.mult))
                    tap = [pcol[:, cut(b + (CW + 8 * n), 1)] for n in range(3)]
                    order.link(dve.tensor_scalar(tv[:, :], cv[:, 0:S], tap[0], None, ALU.mult))
                    for n in (1, 2):
                        order.link(dve.scalar_tensor_tensor(out=tv[:, :], in0=cv[:, n:n + S], scalar=tap[n],
                                                            in1=tv[:, :], op0=ALU.mult, op1=ALU.add))
                if g == 2:
                    order.link(dve.tensor_tensor(tv[:, :], zt[:, :], tv[:, :], ALU.mult))
                if g == 3:
                    dve.wait_ge(s_ct, b + 1)
                    order.link(dve.scalar_tensor_tensor(out=zt[:, :], in0=th[:, :], scalar=1.0, in1=zt[:, :],
                                                        op0=ALU.add, op1=ALU.mult))
                    dve.scalar_tensor_tensor(out=tv[:, :], in0=zt[:, :], scalar=0.5, in1=tv[:, :],
                                             op0=ALU.mult, op1=ALU.mult).then_inc(s_cof, 1)
                    dve.wait_ge(s_cof, b + 1)

            def attend(b):
                for g in range(KV):
                    u = 4 * b + g
                    split(u + (T_CONV + 1), (g + 1) % 2)
                    if g % 2 == 0:
                        unit_lo(b, g // 2)
                    else:
                        values_lo(b, g // 2)
                    if not first_block(b) or g >= 1:
                        normalise(u - 1, (g - 1) % 2)
                    if not first_block(b) or g >= 2:
                        turned_lo(u - 2)
                    load_rq(b, g, g % 2)
                    maxima(b, g, g % 2)
                    conv_part(b, g)

            dve.wait_ge(s_vt, 4)
            dve.memset(cv[:, 0:2], 0.0).then_inc(s_zlo, 1)
            dve.wait_ge(s_zlo, 1)
            attend(0)
            with dve.Fori(1, NB) as b:
                order.enter(b, 18, 1)
                attend(b)
                order.leave(NB)
            last_u = 4 * NB
            normalise(last_u - 1, 1)
            turned_lo(last_u - 2)
            split(T_Z + 1, (T_Z + 1) % 2)
            turned_lo(last_u - 1)

            dve.wait_ge(s_conv_stored, 16 * KT)
            with dve.Fori(0, 2) as i:
                order.enter(i, 4)
                for jj in range(4):
                    t, slot = i * 4 + (T_Z + jj), (T_Z + jj) % 2
                    for h in range(2):
                        evac(t, h, slot, zraw[:, h * HALF:(h + 1) * HALF]).then_inc(s_free, 1)
                    split(t + 2, slot)
                    dve.wait_ge(s_zt, i * 4 + (jj + 1))
                    dve.wait_ge(s_free, i * 8 + (2 * T_Z + 2 * jj + 2))
                    order.link(dve.scalar_tensor_tensor(out=zth[:, :], in0=zth[:, :], scalar=1.0, in1=zraw[:, :],
                                                        op0=ALU.add, op1=ALU.mult))
                    dve.scalar_tensor_tensor(out=zo[:, :], in0=zth[:, :], scalar=0.5, in1=zo[:, :],
                                             op0=ALU.mult, op1=ALU.mult).then_inc(s_zof, 1)
                    dve.wait_ge(s_zhi, i * 4 + (jj + 1))
                    fs = bass.ds(i * 4 + jj, 1)
                    dve.tensor_tensor(olo[:, fs, :].rearrange("p a n -> p (a n)"), zo[:, :],
                                      ohi[:, fs, :].rearrange("p a n -> p (a n)").bitcast(F32),
                                      ALU.subtract).then_inc(s_zlo, 1)
                order.leave(2)

            def branch(t0, n0, last):
                def tile(i):
                    for h in range(2):
                        evac(2 * i + t0, h, t0 % 2, tv[:, h * HALF:(h + 1) * HALF]).then_inc(s_free, 1)
                    if last and isinstance(i, int):
                        for f in range(KT):
                            dve.wait_ge(s_chi, f + 1)
                            dve.tensor_tensor(olo[:, f, :], yc32[:, f, :], ohi[:, f, :].bitcast(F32),
                                              ALU.subtract).then_inc(s_clo, 1)
                    split(2 * i + (t0 + 2), t0 % 2)
                    for h in range(2):
                        dve.wait_ge(s_gt, i * 2 + (n0 + h + 1))
                        dve.wait_ge(s_acc, i * 4 + (2 * t0 + 2 + h + 1))
                        dve.scalar_tensor_tensor(out=h1[:, :], in0=tv[:, h * HALF:(h + 1) * HALF], scalar=1.0,
                                                 in1=ps(2 * ((t0 + 1) % 2) + h), op0=ALU.add, op1=ALU.mult)\
                            .then_inc(s_free, 1)
                        dve.wait_ge(s_free, i * 4 + (2 * t0 + 2 + h + 1))
                        m = merged[:, bass.ds(i, 1), h * HALF:(h + 1) * HALF].rearrange("p a n -> p (a n)")
                        if last:
                            dve.scalar_tensor_tensor(out=m, in0=h1[:, :], scalar=0.5, in1=m, op0=ALU.mult,
                                                     op1=ALU.add).then_inc(s_mg, 1)
                            dve.wait_ge(s_mg, i * 2 + (h + 1))
                        else:
                            order.link(dve.tensor_scalar(m, h1[:, :], 0.5, None, ALU.mult))
                    split(2 * i + (t0 + 3), (t0 + 1) % 2)

                if last:
                    tile(0)
                with dve.Fori(1 if last else 0, 8) as i:
                    order.enter(i, 0 if last else 2)
                    tile(i)
                    order.leave(8)

            branch(T_YB, 0, False)
            branch(T_YA, 16, True)
            for f in range(KT):
                dve.wait_ge(s_mhi, f + 1)
                dve.tensor_tensor(mlo[:, f, :], merged[:, f, :], mhi[:, f, :].bitcast(F32), ALU.subtract)\
                    .then_inc(s_mlo, 1)

            def residual(n, t0, hi, lo, g):
                with dve.Fori(0, 4) as i:
                    for j in range(2):
                        t, slot = 2 * i + (t0 + j), (t0 + j) % 2
                        f = 2 * i + j
                        if n == 1 and j == 0:
                            dve.wait_ge(s_back, 16 * i + 16)
                        for h in range(2):
                            dve.wait_ge(s_acc, 2 * t + (h + 1))
                            r = resid[:, bass.ds(f, 1), h * HALF:(h + 1) * HALF].rearrange("p a n -> p (a n)")
                            dve.tensor_tensor(r, ps(2 * slot + h), r, ALU.add).then_inc(s_free, 1)
                        split(t + 2, slot)
                        lower(n, f, resid, hi, lo, f + g)

            residual(1, T_WO, x2hi, x2lo, PCOL["norm_mix_w_2"])
            dve.wait_ge(s_late, LATE_CONSTS)
            order.link(dve.memset(stats[:, :], 0.0))
            inverse(1)
            for g, w in enumerate(POOL_WINDOWS):
                t, slot = T_P + g, (T_P + g) % 2
                for h in range(2):
                    evac(t, h, slot, pool32[:, g, h * HALF:(h + 1) * HALF]).then_inc(s_free, 1)
                split(t + 2, slot)
                dve.wait_ge(s_free, 2 * t + 2)
                src, step, bufs = pool32[:, g, :], 1, (pa, pb)
                while step < w:
                    dst = bufs[0][:, :]
                    dve.tensor_tensor(dst[:, step:S], src[:, step:S], src[:, 0:S - step], ALU.add)
                    order.link(dve.tensor_copy(dst[:, 0:step], src[:, 0:step]))
                    src, step, bufs = dst, 2 * step, bufs[::-1]
                other = bufs[0]
                order.link(dve.tensor_tensor(other[:, 0:w], src[:, 0:w], rcnt[:, 0:w], ALU.mult))
                dve.scalar_tensor_tensor(out=pool32[:, g, w:S], in0=src[:, w:S], scalar=1.0 / w,
                                         in1=pool32[:, g, w:S], op0=ALU.mult, op1=ALU.subtract)
                dve.tensor_tensor(pool32[:, g, 0:w], other[:, 0:w], pool32[:, g, 0:w], ALU.subtract)\
                    .then_inc(s_p_windows, 1)
                dve.wait_ge(s_p_windows, g + 1)
            for h in range(2):
                evac(T_GL, h, T_GL % 2, glow[:, h * HALF:(h + 1) * HALF], (0, 16)).then_inc(s_free, 1)
            split(T_GL + 2, T_GL % 2)
            for n in range(8):
                g, h = n // 2, n % 2
                c = PCOL["pool_scale_2"] + g
                dve.wait_ge(s_pool_mixed, n + 1)
                dve.tensor_scalar(pool32[:, g, h * HALF:(h + 1) * HALF], ps(4 + n % 4), pcol[:, c:c + 1], None,
                                  ALU.mult).then_inc(s_pool_done, 1)

            def put(n, dst):
                for h in range(2):
                    evac(n, h, n % 2, dst[:, h * HALF:(h + 1) * HALF]).then_inc(s_free, 1)

            put(T_QK, qk32[:, 0, :])
            split(T_QK + 2, T_QK % 2)

            def log_gates(m):
                b = PCOL["gk_b_2"] + m
                for h in range(2):
                    n = 2 * m + h
                    half = slice(h * HALF, (h + 1) * HALF)
                    order.link(dve.tensor_scalar(gk[:, m, half], ps(4 + n), pcol[:, b:b + 1], None, ALU.add))
                    order.link(dve.tensor_scalar(gsum[:, half], gk[:, m, half], 0.0, None, ALU.min))
                    dve.scalar_tensor_tensor(out=ghalf[:, :], in0=gsum[:, half], scalar=2.0, in1=gk[:, m, half],
                                             op0=ALU.mult, op1=ALU.subtract).then_inc(s_gl_min, 1)
                    dve.wait_ge(s_gate_ln, n + 1)
                    order.link(dve.tensor_tensor(gk[:, m, half], gsum[:, half], ghalf[:, :], ALU.subtract))

            def gate_sums(m):
                for c in range(S // CHUNK):
                    chunk = slice(c * CHUNK, (c + 1) * CHUNK)
                    last = dve.tensor_tensor_scan(gsum[:, chunk], ones[:, 0:CHUNK], gk[:, m, chunk], 0.0,
                                                  ALU.mult, ALU.add)
                order.link(last)
                g3 = gsum[:, :].rearrange("p (c n) -> p c n", n=CHUNK)
                dve.tensor_tensor(gk[:, m, :].rearrange("p (c n) -> p c n", n=CHUNK),
                                  g3[:, :, CHUNK - 1:CHUNK].broadcast_to([P, S // CHUNK, CHUNK]), g3, ALU.subtract)\
                    .then_inc(s_gl_sum, 1)

            def gate_products(m):
                for h in range(2):
                    half = slice(h * HALF, (h + 1) * HALF)
                    n = 4 * m + 2 * h
                    dve.wait_ge(s_gk_exp, n + 1)
                    dve.scalar_tensor_tensor(out=qk32[:, m, half], in0=qk32[:, m, half], scalar=0.125,
                                             in1=ghalf[:, :], op0=ALU.mult, op1=ALU.mult).then_inc(s_gk_used, 1)
                    dve.wait_ge(s_gk_exp, n + 2)
                    order.link(dve.tensor_tensor(gk[:, m, half], gk[:, m, half], qk32[:, 2 + m, half], ALU.mult))
                    dve.tensor_tensor(qk32[:, 2 + m, half], qk32[:, 2 + m, half], ghalf[:, :], ALU.mult)\
                        .then_inc(s_gk_used, 1)
                dve.wait_ge(s_gk_used, 4 * m + 4)

            for n in range(T_QK + 1, T_WO2):
                dst = qk32[:, n - T_QK, :] if n < T_V else gv32[:, n - T_V, :] if n < T_R else r32[:, qm(n - T_R), :]
                put(n, dst)
                split(n + 2, n % 2)
                if n == T_QK + 2:
                    dve.wait_ge(s_gate_z, 1)
                    log_gates(0)
                if n == T_QK + 3:
                    gate_sums(0)
                if n == T_V:
                    gate_products(0)
                if n == T_V + 1:
                    log_gates(1)
                if n == T_V + 2:
                    gate_sums(1)
                if n == T_V + 3:
                    gate_products(1)
                if n >= T_R:
                    for h in range(2):
                        k = 2 * (n - T_R) + h
                        dve.wait_ge(s_r_tanh, k + 1)
                        r = r32[:, qm(n - T_R), h * HALF:(h + 1) * HALF]
                        dve.scalar_tensor_tensor(out=r, in0=ps(4 + h), scalar=1.0, in1=r, op0=ALU.add,
                                                 op1=ALU.mult).then_inc(s_r_silu, 1)
            dve.wait_ge(s_r_silu, 8)
            for n in range(2):
                order.link(dve.memset(gst[n][:, :, :, :], 0.0))
            order.link(dve.memset(gss[0][:, :, :, :], 0.0))

            def gla_mask(b):
                dve.wait_ge(s_gla_scores, b + 1)
                if b >= 2:
                    dve.wait_ge(s_gla_o, b - 1)
                dve.copy_predicated(gst[b % 2][:, :, :, :], cmask[:, :].bitcast(U32)
                                    .rearrange("p (a b n) -> p a b n", a=1, b=1).broadcast_to([P, 2, 2, P]),
                                    bank[3][:, :, 0:2 * P].rearrange("p q (m n) -> p q m n", m=2))\
                    .then_inc(s_gla_masked, 1)

            def gla_state(b):
                dve.wait_ge(s_gla_kv, b + 1)
                if b:
                    dve.wait_ge(s_gla_o, b)
                for c in range(2):
                    new = gss[b % 2][:, 1, :, :] if c == 0 else gss[(b + 1) % 2][:, 0, :, :]
                    for m in range(2):
                        last = dve.scalar_tensor_tensor(
                            out=new[:, m, :], in0=gss[b % 2][:, c, m, :], scalar=dec[:, m, 2 * b + c:2 * b + c + 1],
                            in1=bank[1][:, c, m * P:(m + 1) * P], op0=ALU.mult, op1=ALU.add)
                    if c == 0:
                        order.link(last)
                    else:
                        last.then_inc(s_gla_state, 1)
                        dve.wait_ge(s_gla_state, b + 1)

            def gla_gate(b):
                dve.wait_ge(s_gla_o_root, b + 1)
                c = PCOL["gla_norm_w_2"]
                grec = R[:, 0:HALF].rearrange("p (q n) -> p q n", q=2)
                order.link(dve.reciprocal(grec, ps(5).rearrange("p (q n) -> p q n", q=2)))
                order.link(dve.scalar_tensor_tensor(out=go[b % 2][:, :, :], in0=go[b % 2][:, :, :],
                                                    scalar=pcol[:, c:c + 1], in1=grec, op0=ALU.mult,
                                                    op1=ALU.mult))
                o = go[b % 2][:, :, :].rearrange("p q (m n) -> p (q m) n", m=2)
                dve.scalar_tensor_tensor(out=o, in0=o, scalar=0.5, in1=r32[:, :, b * P:(b + 1) * P], op0=ALU.mult,
                                         op1=ALU.mult).then_inc(s_gla_gated, 1)

            def gla_lo(b):
                dve.wait_ge(s_gla_hi, b + 1)
                blk = slice(b * P, (b + 1) * P)
                dve.tensor_tensor(by_half(c2lo[:, 4:8, blk]), go[b % 2][:, :, :].rearrange("p q (m n) -> p q m n", m=2),
                                  by_half(c2hi[:, 4:8, blk]).bitcast(F32), ALU.subtract).then_inc(s_gla_lo, 1)

            def pooled_lo(g):
                dve.wait_ge(s_concat_hi, g + 1)
                dve.tensor_tensor(c2lo[:, g, :], pool32[:, g, :], c2hi[:, g, :].bitcast(F32),
                                  ALU.subtract).then_inc(s_concat_lo, 1)

            gla_mask(0)
            gla_state(0)
            for b in range(NB):
                if b + 1 < NB:
                    gla_mask(b + 1)
                    gla_state(b + 1)
                if b == NB - 1:
                    dve.wait_ge(s_gla_o, NB)
                    pooled_lo(0)
                    pooled_lo(1)
                if b:
                    gla_lo(b - 1)
                gla_gate(b)
            pooled_lo(2)
            gla_lo(NB - 1)
            pooled_lo(3)
            residual(2, T_WO2, x3hi, x3lo, PCOL["norm_xattn_w_2"])

            inverse(2)
            put(T_XQ, xq32[:, 0, :])
            split(T_XQ + 2, T_XQ % 2)
            dve.wait_ge(s_mem_squared, 3)
            dve.reciprocal(stats[:, 4:6], stats[:, 2:4]).then_inc(s_mem_inverse, 1)
            put(T_XQ + 1, xq32[:, 1, :])
            split(T_XQ + 3, (T_XQ + 3) % 2)
            put(T_XQ + 2, xq32[:, 2, :])
            split(T_XQ + 4, T_XQ % 2)
            for c in range(4):
                dve.wait_ge(s_mem_hi_ready, c + 1)
                for f in range(2 * c, 2 * c + 2):
                    g = PCOL["norm_mem_w_2"] + f
                    last = dve.scalar_tensor_tensor(out=mtlo[:, f, :], in0=ps(4 + c)[:, (f % 2) * MEM:(f % 2 + 1) * MEM],
                                                    scalar=pcol[:, g:g + 1], in1=mthi[:, f, :].bitcast(F32),
                                                    op0=ALU.mult, op1=ALU.subtract)
                last.then_inc(s_mem_lo_ready, 1)
            k_tiles = 0
            for j, (kind, n) in enumerate(X_TILES):
                t = T_XQ + j
                if j < 3:
                    continue
                if kind == "q":
                    put(t, xq32[:, n, :])
                elif kind == "k":
                    k_tiles += 1
                    dve.wait_ge(s_mem_k_hi_ready, k_tiles)
                    dve.tensor_tensor(mklo[:, n, :], ps(2 * (t % 2))[:, 0:MEM], mkhi[:, n, :].bitcast(F32),
                                      ALU.subtract).then_inc(s_free, 2)
                else:
                    dve.wait_ge(s_acc, 2 * t + 2)
                    dve.tensor_copy(mvt[:, n, :], ps(2 * (t % 2))[:, 0:MEM]).then_inc(s_free, 2)
                split(t + 2, t % 2)

            def head_lo(h, par):
                dve.wait_ge(s_head_hi, h + 1)
                dve.tensor_tensor(hqlo[par][:, :, :], xq32[:, 2 * h:2 * h + 2, :], hqhi[par][:, :, :].bitcast(F32),
                                  ALU.subtract).then_inc(s_head_lo, 1)

            def head_v_lo(h, par):
                dve.wait_ge(s_head_v_hi, h + 1)
                dve.tensor_tensor(hvlo[par][:, :, :], mv32[:, :, h * XD:(h + 1) * XD],
                                  hvhi[par][:, :, :].bitcast(F32), ALU.subtract).then_inc(s_head_v_lo, 1)

            def x_maxima(u, j):
                dve.wait_ge(s_x_scores, u + 1)
                if u >= 2:
                    dve.wait_ge(s_x_exp, u - 1)
                order.link(dve.tensor_reduce(mx[j % 2][:, 0:2], ps(4 + j % 2).rearrange("p (a n) -> p a n", a=2),
                                             AX_X, ALU.max))
                dve.tensor_scalar(nm[j % 2][:, 0:2], mx[j % 2][:, 0:2], -float(XD) ** -0.5, None, ALU.mult)\
                    .then_inc(s_x_max, 1)

            def x_normalise(u, j):
                dve.wait_ge(s_x_exp, u + 1)
                order.link(dve.reciprocal(den[j % 2][:, 0:2], sums[j % 2][:, 0:2]))
                for a in range(2):
                    last = dve.tensor_scalar(xsx[j % 2][:, a, :], xsx[j % 2][:, a, :], den[j % 2][:, a:a + 1], None,
                                             ALU.mult)
                last.then_inc(s_x_probs, 1)

            def x_turned_lo(u, j):
                dve.wait_ge(s_x_pt_hi, u + 1)
                dve.tensor_tensor(xptlo[j % 2][:, :, :], ps(6 + j % 2).rearrange("p (a n) -> p a n", a=2),
                                  xpthi[j % 2][:, :, :].bitcast(F32), ALU.subtract).then_inc(s_x_pt_lo, 1)

            def x_out_lo(u, h, j):
                dve.wait_ge(s_x_o_hi, u + 1)
                tok = slice(2 * j * P, 2 * (j + 1) * P)
                dve.tensor_tensor(xolo[:, 2 * h:2 * h + 2, tok], ps(j % 2).rearrange("p (a n) -> p a n", a=2),
                                  xohi[:, 2 * h:2 * h + 2, tok].bitcast(F32), ALU.subtract).then_inc(s_x_o_lo, 1)

            head_lo(0, 0)
            for u in range(4 * XHEADS + 5):
                h, j = u // 4, u % 4
                if u < 4 * XHEADS:
                    x_maxima(u, j)
                if u == 0:
                    dve.wait_ge(s_mem_v_turned, 1)
                    for c in range(4):
                        dve.tensor_copy(mv32[:, :, 2 * c * P:2 * (c + 1) * P], ps(c).rearrange("p (a n) -> p a n", a=2))\
                            .then_inc(s_mem_v, 1)
                if 1 <= u < 4 * XHEADS + 1:
                    x_normalise(u - 1, (u - 1) % 4)
                if 3 <= u < 4 * XHEADS + 3:
                    x_turned_lo(u - 3, (u - 3) % 4)
                if u >= 5:
                    x_out_lo(u - 5, (u - 5) // 4, (u - 5) % 4)
                if u == 1:
                    head_v_lo(0, 0)
                if u == 2:
                    head_lo(1, 1)
                if j == 1 and 1 <= h < 3:
                    head_lo(h + 1, (h + 1) % 2)
                if j == 0 and 1 <= h < 4:
                    head_v_lo(h, h % 2)
            residual(3, T_XO, x4hi, x4lo, PCOL["norm_ffn_w_2"])

            t, done = T_FF, 0
            inverse(3)
            order.link(dve.memset(ubuf[:, 0:2], 0.0))

            def conv(i, dst, c, at0, n):
                col = [pcol[:, bass.ds(i + (FFW + 2 * FF_TILES * m + c), 1)] for m in range(4)]
                d = dst[:, at0:at0 + n]
                order.link(dve.tensor_scalar(d, ubuf[:, at0:at0 + n], col[0], col[3], ALU.mult, ALU.add))
                order.link(dve.scalar_tensor_tensor(out=d, in0=ubuf[:, at0 + 1:at0 + 1 + n], scalar=col[1], in1=d,
                                                    op0=ALU.mult, op1=ALU.add))
                return dve.scalar_tensor_tensor(out=d, in0=ubuf[:, at0 + 2:at0 + 2 + n], scalar=col[2], in1=d,
                                                op0=ALU.mult, op1=ALU.add)

            for n in FF_GROUPS:
                with dve.Fori(0, n) as i:
                    order.enter(i, 10)
                    tt, sl = 2 * i + t, t % 2
                    for h in range(2):
                        evac(tt, h, sl, ubuf[:, 2 + h * HALF:2 + (h + 1) * HALF]).then_inc(s_free, 1)
                    split(tt + 2, sl)
                    dve.wait_ge(s_free, i * 4 + (2 * t + 2))
                    conv(i, yg, done, 0, S).then_inc(s_ffn_gate, 1)
                    dve.wait_ge(s_ffn_gate, i + (done + 1))
                    for h in range(2):
                        half = slice(h * HALF, (h + 1) * HALF)
                        evac(tt + 1, h, 1 - sl, ubuf[:, 2 + h * HALF:2 + (h + 1) * HALF]).then_inc(s_free, 1)
                        if h == 1:
                            split(tt + 3, 1 - sl)
                        dve.wait_ge(s_free, i * 4 + (2 * t + 3 + h))
                        order.link(conv(i, yv, FF_TILES + done, h * HALF, HALF))
                        dve.wait_ge(s_ffn_tanh, i * 2 + (2 * done + h + 1))
                        order.link(dve.scalar_tensor_tensor(out=yg[:, half], in0=ps(4 + h), scalar=1.0,
                                                            in1=yg[:, half], op0=ALU.add, op1=ALU.mult))
                        dve.scalar_tensor_tensor(out=yv[:, half], in0=yg[:, half], scalar=0.5, in1=yv[:, half],
                                                 op0=ALU.mult, op1=ALU.mult).then_inc(s_ffn_prod, 1)
                        dve.wait_ge(s_ffn_hi, i * 2 + (2 * done + h + 1))
                        dve.tensor_tensor(flo[:, bass.ds(i, 1), half].rearrange("p a n -> p (a n)"), yv[:, half],
                                          fhi[:, bass.ds(i, 1), half].rearrange("p a n -> p (a n)").bitcast(F32),
                                          ALU.subtract).then_inc(s_ffn_lo, 1)
                    order.leave(n)
                t += 2 * n
                done += n

                if done == FF_TILES:
                    break
                with dve.Fori(0, 4) as i:
                    for j in range(2):
                        tt, sl = 2 * i + (t + j), (t + j) % 2
                        for h in range(2):
                            dve.wait_ge(s_acc, 2 * tt + (h + 1))
                            r = resid[:, bass.ds(2 * i + j, 1), h * HALF:(h + 1) * HALF].rearrange("p a n -> p (a n)")
                            dve.tensor_tensor(r, ps(2 * sl + h), r, ALU.add).then_inc(s_free, 1)
                        split(tt + 2, sl)
                t += 8

            def scale_result(f):
                for c in range(2):
                    n = 2 * f + c
                    dve.wait_ge(s_out_squared, n + 1)
                    dve.tensor_tensor(y[:, 4 * c:4 * c + 4, f * P:(f + 1) * P],
                                      ps(4 + n % 4).rearrange("p (b n) -> p b n", b=4),
                                      gfin[:, f * P:(f + 1) * P].rearrange("p (a n) -> p a n", a=1)
                                      .broadcast_to([P, 4, P]), ALU.mult).then_inc(s_fc, 1)

            dve.wait_ge(s_gfin_loaded, 16)
            for f in range(KT):
                tt, sl = t + f, (t + f) % 2
                for h in range(2):
                    dve.wait_ge(s_acc, 2 * tt + h + 1)
                    r = resid[:, f, h * HALF:(h + 1) * HALF]
                    dve.tensor_tensor(r, ps(2 * sl + h), r, ALU.add).then_inc(s_free, 1)
                if f + 2 < KT:
                    split(tt + 2, sl)
                if f:
                    scale_result(f - 1)
            scale_result(KT - 1)
            dve.tensor_reduce(osum[:, :], osq[:, :, :], AX_X, ALU.add).then_inc(s_out_summed, 1)
            dve.wait_ge(s_out_root, 1)
            dve.reciprocal(oinv[:, :], oroot[:, :]).then_inc(s_out_inverse, 1)
            dve.wait_ge(s_out_inverse, 1)
            dve.wait_ge(s_fc, 2 * KT)
            for b in range(0, NB, 2):
                dve.tensor_scalar(y[:, b, :], y[:, b, :], oinv[:, b:b + 1], None, ALU.mult).then_inc(s_out_normed[0], 1)


N_PAR, N_PAR2 = len(PARAM_ROWS), 3 + 1 + 4


_INS = ['x', 'norm_g', 'w_in', 'conv_w', 'q_norm_g', 'k_norm_g', 'sinks', 'w_conv_out', 'w_attn_out', 'gate_b', 'w_out',
        'mem_2', 'norm_mix_w_2', 'w_in_2', 'pool_w_2', 'pool_scale_2', 'gk_w2_2', 'gk_b_2', 'gla_norm_w_2', 'w_out_2',
        'norm_xattn_w_2', 'norm_mem_w_2', 'xattn_wq_2', 'xattn_wkv_2', 'xattn_wo_2', 'norm_ffn_w_2', 'ffn_w_up_2',
        'ffn_conv_w_2', 'ffn_conv_b_2', 'ffn_w_down_2', 'norm_final_w_2']
_OUTS = [((1, 1024, 1024), 'float32')]


def kernel(**inputs):
    import numpy as _np
    import concourse.bacc as _bacc
    from concourse import mybir as _mybir
    from concourse.bass_utils import run_bass_kernel_spmd as _run

    nc = _bacc.Bacc("TRN2", target_bir_lowering=False, num_devices=1)
    arrays, args = {}, []
    for name in _INS:
        a = _np.ascontiguousarray(inputs[name])
        arrays[f"in_{name}_dram"] = a
        args.append(nc.dram_tensor(f"in_{name}_dram", a.shape, _mybir.dt.from_np(a.dtype), kind="ExternalInput").ap())
    for i, (shape, dtype) in enumerate(_OUTS):
        dt = _mybir.dt.from_np(_np.dtype(dtype))
        args.append(nc.dram_tensor(f"out_{i}_dram", shape, dt, kind="ExternalOutput").ap())
    hybrid_then_mixer_kernel(nc, *args)
    r = _run(nc, [arrays], core_ids=[0])
    return r.results[0]["out_0_dram"]
```
